# Optimizing a Trainium2 kernel written in Bass

```python
import jax
import jax.numpy as jnp
from jax import lax
import numpy as np
import jax, jax.numpy as jnp

D_MODEL = 1024
BATCH = 1
SEQ = 1024
DEPTH = 1

CHUNK = 64
D_MLSTM = D_MODEL // 2
D_POOL = D_MODEL - D_MLSTM
N_HEADS = 4
HEAD_DIM = D_MLSTM // N_HEADS
CONV_WIDTH = 4
POOL_WINDOWS = (2, 4, 8, 16)
N_POOL_GROUPS = len(POOL_WINDOWS)
POOL_GROUP_DIM = D_POOL // N_POOL_GROUPS
N_EXPERT_GROUPS = 4
EXPERTS_PER_GROUP = 8
N_EXPERTS = N_EXPERT_GROUPS * EXPERTS_PER_GROUP
TOP_K = 2
D_EXPERT = D_MODEL // 2
MOE_BLOCK = 128
EPS = 1e-6

COL_U = 0
COL_V = COL_U + D_MLSTM
COL_O = COL_V + D_MLSTM
COL_I = COL_O + D_MLSTM
COL_F = COL_I + N_HEADS
COL_P = COL_F + N_HEADS
IN_COLS = COL_P + D_POOL


def rms_norm(x, g):
    xf = x.astype(jnp.float32)
    y = xf * lax.rsqrt(jnp.mean(xf * xf, axis=-1, keepdims=True) + EPS)
    return (y * g.astype(jnp.float32)).astype(x.dtype)

def causal_conv(x, w, b):
    k_w, ch = w.shape
    y = lax.conv_general_dilated(x, w[:, None, :], window_strides=(1,), padding=[(k_w - 1, 0)],
                                 dimension_numbers=('NWC', 'WIO', 'NWC'), feature_group_count=ch)
    return y + b

def mlstm_chunkwise(q, k, v, i_pre, f_pre):
    bsz, nh, seq, dh = q.shape
    nc = seq // CHUNK
    q = q.astype(jnp.float32) * (dh ** -0.5)
    k = k.astype(jnp.float32)
    v = v.astype(jnp.float32)
    log_i = i_pre.astype(jnp.float32)
    log_f = jax.nn.log_sigmoid(f_pre.astype(jnp.float32))

    def to_chunks(a):
        return jnp.moveaxis(a.reshape(bsz, nh, nc, CHUNK, *a.shape[3:]), 2, 0)

    qc, kc, vc, ic = to_chunks(q), to_chunks(k), to_chunks(v), to_chunks(log_i)
    bc = jnp.cumsum(to_chunks(log_f), axis=-1)
    causal = jnp.tril(jnp.ones((CHUNK, CHUNK), dtype=bool))

    def step(carry, inp):
        c_st, n_st, m_st = carry
        q_, k_, v_, ig, b_ = inp
        d_log = b_[..., :, None] - b_[..., None, :] + ig[..., None, :]
        d_log = jnp.where(causal, d_log, -jnp.inf)
        inter = b_ + m_st[..., None]
        m_t = jnp.maximum(inter, jnp.max(d_log, axis=-1))
        w_intra = jnp.exp(d_log - m_t[..., None])
        a_inter = jnp.exp(inter - m_t)
        s = jnp.einsum('bhtd,bhsd->bhts', q_, k_) * w_intra
        num = (a_inter[..., None] * jnp.einsum('bhed,bhtd->bhte', c_st, q_)
               + jnp.einsum('bhts,bhse->bhte', s, v_))
        den = a_inter * jnp.einsum('bhd,bhtd->bht', n_st, q_) + jnp.sum(s, axis=-1)
        h = num / jnp.maximum(jnp.abs(den), jnp.exp(-m_t))[..., None]
        b_last = b_[..., -1]
        w_log = b_last[..., None] - b_ + ig
        m_new = jnp.maximum(b_last + m_st, jnp.max(w_log, axis=-1))
        a_prev = jnp.exp(b_last + m_st - m_new)
        w_s = jnp.exp(w_log - m_new[..., None])
        c_new = a_prev[..., None, None] * c_st + jnp.einsum('bhs,bhse,bhsd->bhed', w_s, v_, k_)
        n_new = a_prev[..., None] * n_st + jnp.einsum('bhs,bhsd->bhd', w_s, k_)
        return (c_new, n_new, m_new), h

    init = (jnp.zeros((bsz, nh, dh, dh), jnp.float32), jnp.zeros((bsz, nh, dh), jnp.float32),
            jnp.zeros((bsz, nh), jnp.float32))
    _, hs = lax.scan(step, init, (qc, kc, vc, ic, bc))
    return jnp.moveaxis(hs, 0, 2).reshape(bsz, nh, seq, dh)

def mlstm_group(u, v, o_pre, i_pre, f_pre, conv_w, conv_b, w_q, w_k, b_i, b_f, norm_g, skip):
    bsz, seq, _ = u.shape
    uc = jax.nn.silu(causal_conv(u, conv_w, conv_b))
    uh = uc.reshape(bsz, seq, N_HEADS, HEAD_DIM)
    q = jnp.einsum('bshd,hde->bhse', uh, w_q)
    k = jnp.einsum('bshd,hde->bhse', uh, w_k)
    vh = v.reshape(bsz, seq, N_HEADS, HEAD_DIM).transpose(0, 2, 1, 3)
    ig = (i_pre + b_i).transpose(0, 2, 1)
    fg = (f_pre + b_f).transpose(0, 2, 1)
    h = mlstm_chunkwise(q, k, vh, ig, fg)
    h = h * lax.rsqrt(jnp.mean(h * h, axis=-1, keepdims=True) + EPS)
    h = h * norm_g.astype(jnp.float32).reshape(N_HEADS, 1, HEAD_DIM)
    h = h.transpose(0, 2, 1, 3).reshape(bsz, seq, D_MLSTM)
    out = jax.nn.sigmoid(o_pre.astype(jnp.float32)) * (h + skip.astype(jnp.float32) * uc.astype(jnp.float32))
    return out.astype(u.dtype)

def pool_group(p, w_pool, b_pool, pool_scale):
    bsz, seq, _ = p.shape
    pf = p.astype(jnp.float32).reshape(bsz, seq, N_POOL_GROUPS, POOL_GROUP_DIM)
    cs = jnp.pad(jnp.cumsum(pf, axis=1), ((0, 0), (1, 0), (0, 0), (0, 0)))
    t = jnp.arange(seq, dtype=jnp.int32)
    win = jnp.array(POOL_WINDOWS, dtype=jnp.int32)
    start = jnp.maximum(t[:, None] + 1 - win[None, :], 0)
    lo = cs[:, start, jnp.arange(N_POOL_GROUPS)[None, :]]
    count = jnp.minimum(t[:, None] + 1, win[None, :]).astype(jnp.float32)
    pooled = (cs[:, 1:] - lo) / count[None, :, :, None] - pf
    y = jnp.einsum('bsgc,gcd->bsgd', pooled, w_pool.astype(jnp.float32)).reshape(bsz, seq, D_POOL)
    y = (y + b_pool.astype(jnp.float32)) * pool_scale.astype(jnp.float32)
    return y.astype(p.dtype)

def hierarchical_moe(h, w_rg, b_rg, w_re, b_re, w_gate, w_up, w_down):
    bsz, seq, dm = h.shape
    n_tok = bsz * seq
    hf = h.reshape(n_tok, dm)
    g_logits = (hf @ w_rg + b_rg).astype(jnp.float32)
    g_prob = jax.nn.softmax(g_logits, axis=-1)
    g_idx = jnp.argmax(g_logits, axis=-1).astype(jnp.int32)
    g_gate = jnp.take_along_axis(g_prob, g_idx[:, None], axis=1)[:, 0]
    e_logits = (hf @ w_re + b_re).astype(jnp.float32).reshape(n_tok, N_EXPERT_GROUPS, EXPERTS_PER_GROUP)
    e_logits = jnp.take_along_axis(e_logits, g_idx[:, None, None], axis=1)[:, 0]
    top_val, top_loc = lax.top_k(e_logits, TOP_K)
    gates = jax.nn.softmax(top_val, axis=-1) * g_gate[:, None]
    expert = g_idx[:, None] * EXPERTS_PER_GROUP + top_loc.astype(jnp.int32)
    n_asg = n_tok * TOP_K
    flat_e = expert.reshape(n_asg)
    flat_tok = jnp.repeat(jnp.arange(n_tok, dtype=jnp.int32), TOP_K)
    flat_gate = gates.reshape(n_asg)
    order = jnp.argsort(flat_e)
    sorted_e = flat_e[order]
    counts = jnp.bincount(flat_e, length=N_EXPERTS).astype(jnp.int32)
    starts = jnp.cumsum(counts) - counts
    padded = (counts + MOE_BLOCK - 1) // MOE_BLOCK * MOE_BLOCK
    pad_ends = jnp.cumsum(padded)
    pad_starts = pad_ends - padded
    rank = jnp.arange(n_asg, dtype=jnp.int32) - starts[sorted_e]
    dest = pad_starts[sorted_e] + rank
    n_blocks = (n_asg + MOE_BLOCK - 1) // MOE_BLOCK + N_EXPERTS
    n_slots = n_blocks * MOE_BLOCK
    slot_tok = jnp.full((n_slots,), n_tok, jnp.int32).at[dest].set(flat_tok[order])
    slot_gate = jnp.zeros((n_slots,), jnp.float32).at[dest].set(flat_gate[order])
    block_pos = jnp.arange(n_blocks, dtype=jnp.int32) * MOE_BLOCK
    block_expert = jnp.minimum(jnp.searchsorted(pad_ends, block_pos, side='right'), N_EXPERTS - 1)

    def run_block(args):
        tok, e = args
        xb = hf[jnp.minimum(tok, n_tok - 1)]
        a = xb @ w_gate[e]
        b = xb @ w_up[e]
        return (jax.nn.silu(a) * b) @ w_down[e]

    out = lax.map(run_block, (slot_tok.reshape(n_blocks, MOE_BLOCK), block_expert))
    out = (out.reshape(n_slots, dm).astype(jnp.float32) * slot_gate[:, None]).astype(h.dtype)
    y = jnp.zeros((n_tok, dm), h.dtype).at[slot_tok].add(out, mode='drop')
    return y.reshape(bsz, seq, dm)

def first_inputs(seed: int = 0) -> dict:
    key = jax.random.key(seed)
    ks = jax.random.split(key, 28)
    L = DEPTH

    def nrm(k, shape, scale):
        return jax.random.normal(k, shape, jnp.float32) * scale

    return {
        'x': nrm(ks[0], (BATCH, SEQ, D_MODEL), 1.0),
        'c': nrm(ks[1], (BATCH, D_MODEL), 1.0),
        'ada_w': nrm(ks[2], (L, D_MODEL, 6 * D_MODEL), D_MODEL ** -0.5),
        'ada_b': nrm(ks[3], (L, 6 * D_MODEL), 0.02),
        'norm1_g': 1.0 + nrm(ks[4], (L, D_MODEL), 0.02),
        'w_in': nrm(ks[5], (L, D_MODEL, IN_COLS), D_MODEL ** -0.5),
        'conv_w': nrm(ks[6], (L, CONV_WIDTH, D_MLSTM), CONV_WIDTH ** -0.5),
        'conv_b': nrm(ks[7], (L, D_MLSTM), 0.02),
        'w_q': nrm(ks[8], (L, N_HEADS, HEAD_DIM, HEAD_DIM), HEAD_DIM ** -0.5),
        'w_k': nrm(ks[9], (L, N_HEADS, HEAD_DIM, HEAD_DIM), HEAD_DIM ** -0.5),
        'b_igate': nrm(ks[10], (L, N_HEADS), 0.1),
        'b_fgate': jnp.linspace(3.0, 6.0, N_HEADS, dtype=jnp.float32)[None, :] + nrm(ks[11], (L, N_HEADS), 0.1),
        'mlstm_norm_g': 1.0 + nrm(ks[12], (L, D_MLSTM), 0.02),
        'mlstm_skip': 1.0 + nrm(ks[13], (L, D_MLSTM), 0.1),
        'w_pool': nrm(ks[14], (L, N_POOL_GROUPS, POOL_GROUP_DIM, POOL_GROUP_DIM), POOL_GROUP_DIM ** -0.5),
        'b_pool': nrm(ks[15], (L, D_POOL), 0.02),
        'pool_scale': 1.0 + nrm(ks[16], (L, D_POOL), 0.1),
        'w_out': nrm(ks[17], (L, D_MODEL, D_MODEL), D_MODEL ** -0.5),
        'norm2_g': 1.0 + nrm(ks[18], (L, D_MODEL), 0.02),
        'w_router_group': nrm(ks[19], (L, D_MODEL, N_EXPERT_GROUPS), D_MODEL ** -0.5),
        'b_router_group': nrm(ks[20], (L, N_EXPERT_GROUPS), 0.01),
        'w_router_expert': nrm(ks[21], (L, D_MODEL, N_EXPERTS), D_MODEL ** -0.5),
        'b_router_expert': nrm(ks[22], (L, N_EXPERTS), 0.01),
        'w_expert_gate': nrm(ks[23], (L, N_EXPERTS, D_MODEL, D_EXPERT), D_MODEL ** -0.5),
        'w_expert_up': nrm(ks[24], (L, N_EXPERTS, D_MODEL, D_EXPERT), D_MODEL ** -0.5),
        'w_expert_down': nrm(ks[25], (L, N_EXPERTS, D_EXPERT, D_MODEL), D_EXPERT ** -0.5),
        'final_g': 1.0 + nrm(ks[26], (D_MODEL,), 0.02),
    }

def first_block(x, c, ada_w, ada_b, norm1_g, w_in, conv_w, conv_b, w_q, w_k, b_igate, b_fgate,
              mlstm_norm_g, mlstm_skip, w_pool, b_pool, pool_scale, w_out, norm2_g,
              w_router_group, b_router_group, w_router_expert, b_router_expert,
              w_expert_gate, w_expert_up, w_expert_down, final_g):
    bsz, seq, dm = x.shape
    for l in range(DEPTH):
        mod = (jax.nn.silu(c) @ ada_w[l] + ada_b[l]).reshape(bsz, 6, dm)
        shift_a, scale_a, gate_a = mod[:, 0, None, :], mod[:, 1, None, :], mod[:, 2, None, :]
        shift_f, scale_f, gate_f = mod[:, 3, None, :], mod[:, 4, None, :], mod[:, 5, None, :]
        h = rms_norm(x, norm1_g[l]) * (1.0 + scale_a) + shift_a
        proj = h @ w_in[l]
        y_m = mlstm_group(proj[..., COL_U:COL_V], proj[..., COL_V:COL_O], proj[..., COL_O:COL_I],
                          proj[..., COL_I:COL_F], proj[..., COL_F:COL_P], conv_w[l], conv_b[l],
                          w_q[l], w_k[l], b_igate[l], b_fgate[l], mlstm_norm_g[l], mlstm_skip[l])
        y_p = pool_group(proj[..., COL_P:IN_COLS], w_pool[l], b_pool[l], pool_scale[l])
        mix = jnp.concatenate([y_m, y_p], axis=-1) @ w_out[l]
        x = x + gate_a * mix
        h = rms_norm(x, norm2_g[l]) * (1.0 + scale_f) + shift_f
        x = x + gate_f * hierarchical_moe(h, w_router_group[l], b_router_group[l], w_router_expert[l],
                                          b_router_expert[l], w_expert_gate[l], w_expert_up[l],
                                          w_expert_down[l])
    return rms_norm(x, final_g)


N_MIXERS = 3
N_HEADS_2 = 16
HEAD_DIM_2 = D_MODEL // N_HEADS_2
Q_BLOCK = 128
SG_CHUNK = 128
SG_WIDTH = D_MODEL
SG_GROUPS = 8
SG_GROUP_DIM = SG_WIDTH // SG_GROUPS
CONV_WIDTH_2 = 31
D_FF = 4 * D_MODEL
N_A = (DEPTH + 2) // N_MIXERS
N_B = (DEPTH + 1) // N_MIXERS
N_C = DEPTH // N_MIXERS


def rms_norm_2(x, g):
    xf = x.astype(jnp.float32)
    y = xf * lax.rsqrt(jnp.mean(xf * xf, axis=-1, keepdims=True) + EPS)
    return (y * g.astype(jnp.float32)).astype(x.dtype)

def layer_norm(x, g, b):
    xf = x.astype(jnp.float32)
    mu = jnp.mean(xf, axis=-1, keepdims=True)
    xc = xf - mu
    y = xc * lax.rsqrt(jnp.mean(xc * xc, axis=-1, keepdims=True) + EPS)
    return (y * g.astype(jnp.float32) + b.astype(jnp.float32)).astype(x.dtype)

def fox_mixer(h, w_in, b_f, q_g, k_g, w_out):
    B, S, D = h.shape
    proj = h @ w_in
    q, k, v, f_pre = jnp.split(proj, [D, 2 * D, 3 * D], axis=-1)
    q = rms_norm_2(q.reshape(B, S, N_HEADS_2, HEAD_DIM_2), q_g)
    k = rms_norm_2(k.reshape(B, S, N_HEADS_2, HEAD_DIM_2), k_g)
    v = v.reshape(B, S, N_HEADS_2, HEAD_DIM_2)
    log_f = jax.nn.log_sigmoid(f_pre.astype(jnp.float32) + b_f.astype(jnp.float32))
    F = jnp.cumsum(log_f, axis=1).transpose(0, 2, 1)
    nb = S // Q_BLOCK
    qb = q.reshape(B, nb, Q_BLOCK, N_HEADS_2, HEAD_DIM_2).swapaxes(0, 1)
    Fq = F.reshape(B, N_HEADS_2, nb, Q_BLOCK).transpose(2, 0, 1, 3)
    k_pos = jnp.arange(S)
    scale = HEAD_DIM_2 ** -0.5

    def block(args):
        q_i, F_i, b_i = args
        logits = (jnp.einsum('bqhd,bkhd->bhqk', q_i, k).astype(jnp.float32) * scale
                  + (F_i[..., :, None] - F[..., None, :]))
        q_pos = b_i * Q_BLOCK + jnp.arange(Q_BLOCK)
        logits = jnp.where(k_pos[None, :] <= q_pos[:, None], logits, -jnp.inf)
        p = jax.nn.softmax(logits, axis=-1).astype(v.dtype)
        return jnp.einsum('bhqk,bkhd->bqhd', p, v)

    o = lax.map(block, (qb, Fq, jnp.arange(nb)))
    o = o.swapaxes(0, 1).reshape(B, S, D)
    return o @ w_out

def gmlp_mixer(h, w_in, ln_g, ln_b, w_s, b_s, w_out):
    B, S, _ = h.shape
    uv = jax.nn.gelu(h @ w_in)
    u, v = jnp.split(uv, 2, axis=-1)
    v = layer_norm(v, ln_g, ln_b)
    v = v.reshape(B, S // SG_CHUNK, SG_CHUNK, SG_GROUPS, SG_GROUP_DIM)
    cid = jnp.arange(SG_CHUNK) // CHUNK
    mask = cid[None, :] <= cid[:, None]
    ws = jnp.where(mask[None], w_s, jnp.zeros_like(w_s))
    v = jnp.einsum('gts,bnsgc->bntgc', ws, v) + b_s.T[:, :, None]
    v = v.reshape(B, S, SG_WIDTH)
    return (u * v) @ w_out

def conv_mixer(h, w_pw1, b_pw1, w_dw, b_dw, ln_g, ln_b, w_pw2, b_pw2):
    D = h.shape[-1]
    y = jax.nn.glu(h @ w_pw1 + b_pw1, axis=-1)
    y = lax.conv_general_dilated(y, w_dw[:, None, :], window_strides=(1,),
                                 padding=[(CONV_WIDTH_2 - 1, 0)],
                                 dimension_numbers=('NWC', 'WIO', 'NWC'),
                                 feature_group_count=D) + b_dw
    y = jax.nn.silu(layer_norm(y, ln_g, ln_b))
    return y @ w_pw2 + b_pw2

def second_inputs(seed: int = 0) -> dict:
    key = jax.random.key(seed)
    ks = iter(jax.random.split(key, 40))
    D = D_MODEL

    def nrm(shape, scale):
        return jax.random.normal(next(ks), shape, jnp.float32) * scale

    def gain(shape):
        return 1.0 + nrm(shape, 0.05)

    return {
        "x": nrm((BATCH, SEQ, D), 1.0),
        "c": nrm((BATCH, D), 1.0),
        "norm_mix": gain((DEPTH, D)),
        "norm_mlp": gain((DEPTH, D)),
        "w_ada": nrm((DEPTH, D, 6 * D), 0.5 * D ** -0.5),
        "b_ada": nrm((DEPTH, 6 * D), 0.02),
        "w_mlp_in": nrm((DEPTH, D, D_FF), D ** -0.5),
        "w_mlp_out": nrm((DEPTH, D_FF, D), D_FF ** -0.5),
        "fox_w_in": nrm((N_A, D, 3 * D + N_HEADS_2), D ** -0.5),
        "fox_b_f": jax.random.uniform(next(ks), (N_A, N_HEADS_2), jnp.float32, 1.0, 6.0),
        "fox_q_norm": gain((N_A, HEAD_DIM_2)),
        "fox_k_norm": gain((N_A, HEAD_DIM_2)),
        "fox_w_out": nrm((N_A, D, D), D ** -0.5),
        "sg_w_in": nrm((N_B, D, 2 * SG_WIDTH), D ** -0.5),
        "sg_ln_g": gain((N_B, SG_WIDTH)),
        "sg_ln_b": nrm((N_B, SG_WIDTH), 0.02),
        "sg_w_s": nrm((N_B, SG_GROUPS, SG_CHUNK, SG_CHUNK), 0.5 * SG_CHUNK ** -0.5),
        "sg_b_s": 1.0 + nrm((N_B, SG_GROUPS, SG_CHUNK), 0.02),
        "sg_w_out": nrm((N_B, SG_WIDTH, D), SG_WIDTH ** -0.5),
        "cv_w_pw1": nrm((N_C, D, 2 * D), D ** -0.5),
        "cv_b_pw1": nrm((N_C, 2 * D), 0.02),
        "cv_w_dw": nrm((N_C, CONV_WIDTH_2, D), CONV_WIDTH_2 ** -0.5),
        "cv_b_dw": nrm((N_C, D), 0.02),
        "cv_ln_g": gain((N_C, D)),
        "cv_ln_b": nrm((N_C, D), 0.02),
        "cv_w_pw2": nrm((N_C, D, D), D ** -0.5),
        "cv_b_pw2": nrm((N_C, D), 0.02),
    }

def second_block(x, c, norm_mix, norm_mlp, w_ada, b_ada, w_mlp_in, w_mlp_out,
              fox_w_in, fox_b_f, fox_q_norm, fox_k_norm, fox_w_out,
              sg_w_in, sg_ln_g, sg_ln_b, sg_w_s, sg_b_s, sg_w_out,
              cv_w_pw1, cv_b_pw1, cv_w_dw, cv_b_dw, cv_ln_g, cv_ln_b, cv_w_pw2, cv_b_pw2):
    c_act = jax.nn.silu(c)
    for i in range(DEPTH):
        kind = i % N_MIXERS
        j = i // N_MIXERS
        mod = c_act @ w_ada[i] + b_ada[i]
        sh_m, sc_m, g_m, sh_f, sc_f, g_f = [m[:, None, :] for m in jnp.split(mod, 6, axis=-1)]
        h = rms_norm_2(x, norm_mix[i]) * (1 + sc_m) + sh_m
        if kind == 0:
            y = fox_mixer(h, fox_w_in[j], fox_b_f[j], fox_q_norm[j], fox_k_norm[j], fox_w_out[j])
        elif kind == 1:
            y = gmlp_mixer(h, sg_w_in[j], sg_ln_g[j], sg_ln_b[j], sg_w_s[j], sg_b_s[j], sg_w_out[j])
        else:
            y = conv_mixer(h, cv_w_pw1[j], cv_b_pw1[j], cv_w_dw[j], cv_b_dw[j],
                           cv_ln_g[j], cv_ln_b[j], cv_w_pw2[j], cv_b_pw2[j])
        x = x + g_m * y
        h = rms_norm_2(x, norm_mlp[i]) * (1 + sc_f) + sh_f
        x = x + g_f * (jnp.square(jax.nn.relu(h @ w_mlp_in[i])) @ w_mlp_out[i])
    return x


def setup_inputs(seed=0):
    out = dict(first_inputs(seed))
    for name, value in second_inputs(seed + 1).items():
        if name != "x":
            out[name + "_2"] = value
    return out


def reference(
    x, c, ada_w, ada_b, norm1_g, w_in, conv_w, conv_b, w_q, w_k, b_igate, b_fgate, mlstm_norm_g,
    mlstm_skip, w_pool, b_pool, pool_scale, w_out, norm2_g, w_router_group, b_router_group,
    w_router_expert, b_router_expert, w_expert_gate, w_expert_up, w_expert_down, final_g, c_2,
    norm_mix_2, norm_mlp_2, w_ada_2, b_ada_2, w_mlp_in_2, w_mlp_out_2, fox_w_in_2, fox_b_f_2,
    fox_q_norm_2, fox_k_norm_2, fox_w_out_2, sg_w_in_2, sg_ln_g_2, sg_ln_b_2, sg_w_s_2,
    sg_b_s_2, sg_w_out_2, cv_w_pw1_2, cv_b_pw1_2, cv_w_dw_2, cv_b_dw_2, cv_ln_g_2, cv_ln_b_2,
    cv_w_pw2_2, cv_b_pw2_2,
):
    x = first_block(
        x, c, ada_w, ada_b, norm1_g, w_in, conv_w, conv_b, w_q, w_k, b_igate, b_fgate,
        mlstm_norm_g, mlstm_skip, w_pool, b_pool, pool_scale, w_out, norm2_g, w_router_group,
        b_router_group, w_router_expert, b_router_expert, w_expert_gate, w_expert_up,
        w_expert_down, final_g,
    )
    return second_block(
        x, c_2, norm_mix_2, norm_mlp_2, w_ada_2, b_ada_2, w_mlp_in_2, w_mlp_out_2, fox_w_in_2,
        fox_b_f_2, fox_q_norm_2, fox_k_norm_2, fox_w_out_2, sg_w_in_2, sg_ln_g_2, sg_ln_b_2,
        sg_w_s_2, sg_b_s_2, sg_w_out_2, cv_w_pw1_2, cv_b_pw1_2, cv_w_dw_2, cv_b_dw_2, cv_ln_g_2,
        cv_ln_b_2, cv_w_pw2_2, cv_b_pw2_2,
    )


_drawn_inputs = setup_inputs


def setup_inputs(seed=0):
    import zlib

    import numpy as np

    out = dict(_drawn_inputs(seed))
    spreads = {}
    factors = {'b_igate': 200.0,
     'mlstm_norm_g': 3.845,
     'b_pool': 3.77,
     'b_router_group': 4.393,
     'b_router_expert': 4.141,
     'final_g': 2.733,
     'norm_mix_2': 7.982,
     'fox_q_norm_2': 8.0,
     'fox_k_norm_2': 8.0,
     'norm_mlp_2': 8.0}
    for name, (base, spread) in spreads.items():
        noise = np.random.default_rng([zlib.crc32(name.encode()), seed]).standard_normal(out[name].shape)
        drawn = base * np.exp(spread * noise) if base else spread * noise
        out[name] = jnp.asarray(drawn.astype(out[name].dtype))
    for name, factor in factors.items():
        out[name] = (out[name] * factor).astype(out[name].dtype)
    return out
```

```python
from contextlib import ExitStack

import concourse.bass as bass
from concourse import mybir

F32 = mybir.dt.float32
F32R = mybir.dt.float32r
I32 = mybir.dt.int32
U32 = mybir.dt.uint32
BF16 = mybir.dt.bfloat16
ALU = mybir.AluOpType
ACT = mybir.ActivationFunctionType
X = mybir.AxisListType.X

P = 128
S = 1024
D = 1024
TT = S // P
KT = D // P
HALF = 512
EPS = 1e-6
ROOT_D = float(D) ** 0.5
NEG = -3.0e38

HM = 4
POOL_PAD = 16
CW = 4

NE = 32
EG = 4
EPG = NE // EG
DE = 512
JT = DE // P
MINB = S * 2 // P
MAXB = S * 2 // P + NE

HF = 16
DH = 64
PAIRS = HF // 2
FF = 4096
FB = FF // HALF


def build(nc, a, out):
    top = ExitStack()
    with top:
        def sbuf(ctx, name, shape, dt=F32):
            return ctx.enter_context(nc.sbuf_tensor(name, shape, dt))

        def phase(f, *more):
            sems = []

            def sem(name):
                sems.append(nc.alloc_semaphore(name))
                return sems[-1]

            f(nc, a, sbuf, sem, bank, ident, ones, mhalf, gates, colmod, *more)
            nc.clear_and_free_semaphores(sems)
            nc.all_engine_barrier()

        psum = top.enter_context(nc.psum_tensor("psum", [P, 8, HALF], F32))
        bank = [psum[:, i, :] for i in range(8)]

        ident = sbuf(top, "ident", [P, P])
        ones = sbuf(top, "ones", [P, P])
        gates = sbuf(top, "gates", [P, 4, D])
        colmod = sbuf(top, "colmod", [P, 2, 4, KT])
        mhalf = sbuf(top, "minus_half", [P, 1])

        normed_dram = nc.dram_tensor("normed_rows", [S, D], F32, kind="Internal").ap()
        slots_dram = nc.dram_tensor("slot_tokens", [P * MAXB, 1], I32, kind="Internal").ap()
        moe_dram = nc.dram_tensor("expert_rows", [MAXB * P, D], F32, kind="Internal").ap()
        negf_dram = nc.dram_tensor("minus_log_forget", [HF, S], F32, kind="Internal").ap()
        x2_dram = nc.dram_tensor("second_residual", [S, D], F32, kind="Internal").ap()

        phase(modulation)
        with ExitStack() as xs:
            x1 = sbuf(xs, "x1", [P, TT, D])
            phase(mixer, x1, moe_dram)
            phase(moe, x1, normed_dram, slots_dram, moe_dram, x2_dram)
        with ExitStack() as xs:
            x3 = sbuf(xs, "x3", [P, TT, D])
            hT = sbuf(xs, "fox_hT", [P, KT, S])
            phase(attention, psum, x2_dram, negf_dram, x3, hT)
            phase(mlp, x3, hT, out)


def modulation(nc, a, sbuf, sem, bank, ident, ones, mhalf, gates, colmod):
    with ExitStack() as ctx:
        ws = sbuf(ctx, "ada_rows", [P, 2, 6 * D])
        acc = sbuf(ctx, "ada_acc", [P, 2, 6 * D])
        brow = sbuf(ctx, "ada_bias_row", [1, 2, 6 * D])
        ccol = sbuf(ctx, "c_col", [P, 2, KT])
        csil = sbuf(ctx, "c_silu", [P, 2, KT])
        bcol = sbuf(ctx, "ada_bias_col", [P, 2, 6, KT])
        gcol = sbuf(ctx, "norm_gain_col", [P, 2, 2, KT])
        tcol = sbuf(ctx, "mod_col", [P, 2, 4, KT])
        par, row0, row1 = sem("m_params"), sem("m_rows0"), sem("m_rows1")
        rows = [row0, row1]
        csilu, macc, red, modc, modg, idm = (sem("m_silu"), sem("m_acc"), sem("m_reduced"), sem("m_cols"), sem("m_gates"), sem("m_ident"))
        w = [a["ada_w"], a["w_ada_2"]]
        b = [a["ada_b"], a["b_ada_2"]]
        gains = [[a["norm1_g"], a["norm2_g"]], [a["norm_mix_2"], a["norm_mlp_2"]]]
        with nc.Block() as block:
            @block.sync
            def _(sp):
                for l, c in enumerate((a["c"], a["c_2"])):
                    sp.dma_start(ccol[:, l, :], c[0].rearrange("(p k) -> p k", k=KT)).then_inc(par, 16)
                for j in range(2 * KT):
                    l, k = divmod(j, KT)
                    if j >= 2:
                        sp.wait_ge(macc, j - 1)
                    sp.dma_start(ws[:, j % 2, :], w[l][0].rearrange("(p k) n -> p k n", k=KT)[:, k, :]).then_inc(rows[j % 2], 16)

            @block.scalar
            def _(act):
                for l in range(2):
                    act.dma_start(bcol[:, l], b[l][0].rearrange("(q p k) -> p q k", p=P, k=KT)).then_inc(par, 16)
                    act.dma_start(brow[:, l, :], b[l]).then_inc(par, 16)
                    for g in range(2):
                        act.dma_start(gcol[:, l, g, :], gains[l][g][0].rearrange("(p k) -> p k", k=KT)).then_inc(par, 16)
                act.wait_ge(par, 16 * 10)
                act.activation(csil[:], ccol[:], ACT.Silu).then_inc(csilu, 1)

            @block.gpsimd
            def _(pool):
                pool.memset(ident[:], 0.0).then_inc(idm, 1)
                pool.memset(ones[:], 1.0).then_inc(idm, 1)
                pool.memset(mhalf[:], -0.5).then_inc(idm, 1)
                pool.wait_ge(idm, 3)
                pool.affine_select(out=ident[:], in_=ident[:], compare_op=ALU.not_equal, fill=1.0, base=0,
                                   pattern=[[-1, P]], channel_multiplier=1).then_inc(idm, 1)

            @block.vector
            def _(dve):
                dve.wait_ge(csilu, 1)
                for j in range(2 * KT):
                    l, k = divmod(j, KT)
                    dve.wait_ge(rows[j % 2], 16 * (j // 2 + 1))
                    if k == 0:
                        dve.tensor_scalar(acc[:, l, :], ws[:, j % 2, :], csil[:, l, k:k + 1], None, ALU.mult).then_inc(macc, 1)
                    else:
                        dve.wait_ge(macc, j)
                        dve.scalar_tensor_tensor(acc[:, l, :], ws[:, j % 2, :], csil[:, l, k:k + 1], acc[:, l, :],
                                                 ALU.mult, ALU.add).then_inc(macc, 1)
                for l in range(2):
                    dve.wait_ge(red, 5 * l + 1)
                    dve.tensor_tensor(tcol[:, l, 0:2, :], bank[4 + l][:, l * 32:l * 32 + 16].rearrange("p (q k) -> p q k", k=KT),
                                      bcol[:, l, 0:2, :], ALU.add).then_inc(modc, 1)
                    dve.tensor_tensor(tcol[:, l, 2:4, :], bank[4 + l][:, l * 32 + 16:l * 32 + 32].rearrange("p (q k) -> p q k", k=KT),
                                      bcol[:, l, 3:5, :], ALU.add).then_inc(modc, 1)
                    dve.wait_ge(modc, 6 * l + 2)
                    for g in range(2):
                        dve.tensor_copy(colmod[:, l, 2 * g, :], tcol[:, l, 2 * g, :]).then_inc(modc, 1)
                        dve.scalar_tensor_tensor(colmod[:, l, 2 * g + 1, :], tcol[:, l, 2 * g + 1, :], 1.0, gcol[:, l, g, :],
                                                 ALU.add, ALU.mult).then_inc(modc, 1)
                    for n in range(4):
                        dve.wait_ge(red, 5 * l + 2 + n)
                        dve.tensor_copy(gates[:, 2 * l + n // 2, (n % 2) * HALF:(n % 2 + 1) * HALF], bank[n][:]).then_inc(modg, 1)

            @block.tensor
            def _(pe):
                pe.wait_ge(idm, 4)
                pe.wait_ge(par, 16 * 10)
                for l in range(2):
                    pe.wait_ge(macc, KT * (l + 1))
                    for qi, q in enumerate((0, 1, 3, 4)):
                        for k in range(KT):
                            m = pe.matmul(bank[4 + l][:, l * 32 + qi * KT + k:l * 32 + qi * KT + k + 1],
                                          acc[:, l, q * D + k:(q + 1) * D:KT], ones[:, 0:1], start=True, stop=True)
                    m.then_inc(red, 1)
                    for n in range(4):
                        if l == 1:
                            pe.wait_ge(modg, n + 1)
                        at = (2 + 3 * (n // 2)) * D + (n % 2) * HALF
                        pe.matmul(bank[n][:], ones[:], acc[:, l, at:at + HALF], start=True, stop=False)
                        pe.matmul(bank[n][:], ones[0:1, :], brow[:, l, at:at + HALF], start=False, stop=True).then_inc(red, 1)


def mixer(nc, a, sbuf, sem, bank, ident, ones, mhalf, gates, colmod, x1, moe_dram):
    w_in = a["w_in"][0]
    w_in_pk = w_in.rearrange("(p k) n -> p k n", k=KT)
    DM = HM * P
    with ExitStack() as ctx:
        ucT = sbuf(ctx, "ucT", [P, HM, S])
        sgo = sbuf(ctx, "sigmoid_oT", [P, HM, S])
        vaug = sbuf(ctx, "v_aug", [P, TT, HM, P + 1])
        yT = sbuf(ctx, "yT", [P, 2 * HM, S])
        prow = sbuf(ctx, "param_rows", [36, P])
        pcol = sbuf(ctx, "param_cols", [P, 36])
        zrow = x1[0:HM, 6:8, :]
        bif = sbuf(ctx, "gate_bias", [HM, 2])
        par = sem("x_params")
        with ExitStack() as c2:
            hT = sbuf(c2, "hT", [P, KT, S])
            wb = sbuf(c2, "w_in_block", [P, 2, KT, HALF])
            wg = sbuf(c2, "w_in_gates", [P, KT, 36])
            wgl = sbuf(c2, "w_in_gates_loaded", [P, KT, 8])
            uT = yT[:, 0:HM, :]
            pp = yT[:, HM:2 * HM, :]
            stat = sbuf(c2, "stat", [P, TT, 2])
            xn = ucT[:, 0:2, :]
            sq = ucT[:, 2, :]
            xl, xs, nr, tr, hv = [sem("x_load0"), sem("x_load1")], sem("x_square"), sem("x_normed"), sem("x_turned"), sem("x_hT")
            xst, xse = sem("x_stat"), sem("x_eps")
            wl = [sem("x_w0"), sem("x_w1")]
            wgd, mm, ev, z, cv, padz = sem("x_wgates"), sem("x_proj"), sem("x_evac"), sem("x_zero"), sem("x_conv"), sem("x_padz")
            pc = sem("x_pcol")
            cols = [0, 2 * DM, 4 * 128 * 3 + 8, DM]
            with nc.Block() as block:
                @block.sync
                def _(sp):
                    for t in range(TT):
                        if t >= 2:
                            sp.wait_ge(nr, t - 1)
                        sp.dma_start(x1[:, t, :], a["x"][0, t * P:(t + 1) * P, :]).then_inc(xl[t % 2], 16)
                    for n in range(4):
                        if n >= 2:
                            sp.wait_ge(mm, 8 * (n - 1))
                        sp.dma_start(wb[:, n % 2], w_in_pk[:, :, cols[n]:cols[n] + HALF]).then_inc(wl[n % 2], 16)

                @block.gpsimd
                def _(pool):
                    for t in range(TT):
                        pool.wait_ge(xs, t + 1)
                        pool.tensor_scalar(stat[:, t, 0:1], stat[:, t, 0:1], D * EPS, None, ALU.add).then_inc(xse, 1)
                        pool.wait_ge(xse, t + 1)
                        pool.tensor_tensor(stat[:, t, 1:2], stat[:, t, 0:1], mhalf[:], ALU.pow).then_inc(xst, 1)
                    pool.memset(wg[:], 0.0).then_inc(z, 1)
                    pool.memset(vaug[:, :, :, P:P + 1], 1.0).then_inc(z, 1)
                    pool.wait_ge(wgd, 16)
                    pool.wait_ge(z, 2)
                    pool.tensor_copy(wg[:, :, 0:HM], wgl[:, :, 0:HM]).then_inc(z, 1)
                    pool.tensor_copy(wg[:, :, 32:32 + HM], wgl[:, :, HM:2 * HM]).then_inc(z, 1)

                @block.scalar
                def _(act):
                    act.dma_start(prow[0:16, :], a["conv_w"][0].rearrange("w (t p) -> (w t) p", p=P)).then_inc(par, 16)
                    for n, name in enumerate(("conv_b", "mlstm_norm_g", "mlstm_skip", "b_pool", "pool_scale")):
                        act.dma_start(prow[16 + 4 * n:20 + 4 * n, :], a[name][0].rearrange("(t p) -> t p", p=P)).then_inc(par, 16)
                    act.dma_start(bif[:, 0:1], a["b_igate"][0].rearrange("(h o) -> h o", o=1)).then_inc(par, 16)
                    act.dma_start(bif[:, 1:2], a["b_fgate"][0].rearrange("(h o) -> h o", o=1)).then_inc(par, 16)
                    act.dma_start(wgl[:], w_in_pk[:, :, 3 * DM:3 * DM + 8]).then_inc(wgd, 16)
                    for t in range(TT):
                        act.wait_ge(xl[t % 2], 16 * (t // 2 + 1))
                        if t >= 1:
                            act.wait_ge(xs, t)
                        act.activation(sq, x1[:, t, :], ACT.Square, accum_out=stat[:, t, 0:1]).then_inc(xs, 1)
                    for n in range(4):
                        for i in range(8):
                            act.wait_ge(mm, 8 * n + i + 1)
                            src = bank[2 + (8 * n + i) % 4][:]
                            m, hf = divmod(i, 2)
                            if n == 0:
                                ins = act.activation(uT[:, m, hf * HALF:(hf + 1) * HALF], src, ACT.Copy)
                            elif n == 1:
                                ins = act.activation(sgo[:, m, hf * HALF:(hf + 1) * HALF], src, ACT.Sigmoid)
                            elif n == 2:
                                ins = act.activation(pp[:, m, hf * HALF:(hf + 1) * HALF], src, ACT.Copy)
                            else:
                                ins = act.activation(vaug[:, i, :, 0:P], src.rearrange("p (h e) -> p h e", h=HM), ACT.Copy)
                            ins.then_inc(ev, 1)
                    act.wait_ge(par, 16 * 8)
                    for hf in range(2):
                        act.wait_ge(mm, 33 + hf)
                        for g in range(2):
                            act.activation(zrow[:, g, hf * HALF:(hf + 1) * HALF], bank[hf][32 * g:32 * g + HM, :], ACT.Identity,
                                           bias=bif[:, g:g + 1]).then_inc(ev, 1)
                    for m in range(HM):
                        act.wait_ge(cv, 4 * (m + 1))
                        act.activation(ucT[:, m, :], ucT[:, m, :], ACT.Silu, bias=pcol[:, 16 + m:17 + m]).then_inc(ev, 1)

                @block.vector
                def _(dve):
                    for t in range(TT):
                        dve.wait_ge(xst, t + 1)
                        if t >= 2:
                            dve.wait_ge(tr, 2 * (t - 1))
                        dve.tensor_scalar(xn[:, t % 2, :], x1[:, t, :], stat[:, t, 1:2], ROOT_D, ALU.mult, ALU.mult).then_inc(nr, 1)
                        for g in range(2):
                            dve.wait_ge(tr, 2 * t + g + 1)
                            for k in range(4 * g, 4 * g + 4):
                                ins = dve.tensor_scalar(hT[:, k, t * P:(t + 1) * P], bank[g][:, (k % 4) * P:(k % 4 + 1) * P],
                                                        colmod[:, 0, 1, k:k + 1], colmod[:, 0, 0, k:k + 1], ALU.mult, ALU.add)
                            ins.then_inc(hv, 1)
                    dve.wait_ge(pc, 1)
                    dve.tensor_copy(pcol[:], bank[6][:, 0:36]).then_inc(pc, 1)
                    dve.wait_ge(pc, 2)
                    dve.wait_ge(ev, 8)
                    for m in range(HM):
                        for j in range(CW):
                            src = uT[:, m, 0:S - j]
                            tap = pcol[:, 4 * (CW - 1 - j) + m:4 * (CW - 1 - j) + m + 1]
                            if j == 0:
                                dve.tensor_scalar(ucT[:, m, :], src, tap, None, ALU.mult).then_inc(cv, 1)
                            else:
                                dve.wait_ge(cv, 4 * m + j)
                                dve.scalar_tensor_tensor(ucT[:, m, j:], src, tap, ucT[:, m, j:], ALU.mult, ALU.add).then_inc(cv, 1)

                @block.tensor
                def _(pe):
                    for t in range(TT):
                        pe.wait_ge(nr, t + 1)
                        for g in range(2):
                            if t >= 1:
                                pe.wait_ge(hv, 2 * (t - 1) + g + 1)
                            for k in range(4 * g, 4 * g + 4):
                                ins = pe.transpose(bank[g][:, (k % 4) * P:(k % 4 + 1) * P], xn[:, t % 2, k:D:KT], ident[:])
                            ins.then_inc(tr, 1)
                    pe.wait_ge(hv, 2 * TT)
                    pe.wait_ge(par, 16 * 8)
                    pe.transpose(bank[6][:, 0:36], prow[:], ident[0:36, 0:36]).then_inc(pc, 1)
                    for n in range(4):
                        pe.wait_ge(wl[n % 2], 16 * (n // 2 + 1))
                        for i in range(8):
                            g = 8 * n + i
                            if g >= 4:
                                pe.wait_ge(ev, g - 3)
                            m, hf = divmod(i, 2)
                            for k in range(KT):
                                if n < 3:
                                    ins = pe.matmul(bank[2 + g % 4][:], wb[:, n % 2, k, m * P:(m + 1) * P], hT[:, k, hf * HALF:(hf + 1) * HALF],
                                                    start=(k == 0), stop=(k == KT - 1))
                                else:
                                    ins = pe.matmul(bank[2 + g % 4][:], hT[:, k, i * P:(i + 1) * P], wb[:, n % 2, k, :],
                                                    start=(k == 0), stop=(k == KT - 1))
                            ins.then_inc(mm, 1)
                    pe.wait_ge(z, 4)
                    for hf in range(2):
                        for k in range(KT):
                            ins = pe.matmul(bank[hf][0:36, :], wg[:, k, :], hT[:, k, hf * HALF:(hf + 1) * HALF], start=(k == 0), stop=(k == KT - 1))
                        ins.then_inc(mm, 1)

        NC_ = TT
        with ExitStack() as c2:
            qT = sbuf(c2, "qT", [P, HM, S])
            kT = sbuf(c2, "kT", [P, HM, S])
            ktok = sbuf(c2, "k_tok", [P, TT, HM, P])
            wq = sbuf(c2, "wq", [P, HM, P])
            wk = sbuf(c2, "wk", [P, HM, P])
            wp = sbuf(c2, "wpool", [P, HM, P])
            rr = x1[0:HM, 0:6, :]
            negM = rr[:, 1, :]
            packed = sbuf(c2, "packed_rows", [P, S])
            pk = sbuf(c2, "packed_cols", [P, TT, P])
            mprev = sbuf(c2, "m_prev", [HM, NC_])
            aprev = sbuf(c2, "a_prev", [HM, NC_])
            aprb = sbuf(c2, "a_prev_all", [P, HM, NC_])
            sel = sbuf(c2, "select_head", [HM, HM, P])
            NM = x1[:, 2:6, :]
            cmask = sbuf(c2, "causal", [P, P])
            state = sbuf(c2, "state", [P, HM, P + 1])
            lw = sem("c_w")
            rw = sem("c_rows")
            rdy = sem("c_ready")
            q1, q2 = sem("c_qk"), sem("c_qkev")
            g1, g2 = sem("c_setup"), sem("c_setup_done")
            pl = sem("c_pool")
            pm, pe_v = sem("c_poolmm"), sem("c_poolev")
            rowexp = sem("c_rowexp")
            with ExitStack() as c3:
                ps2 = sbuf(c3, "pool_sums", [P, 2, POOL_PAD + S])
                fix = sbuf(c3, "pool_fix", [P, HM, 16])
                with nc.Block() as block:
                    @block.sync
                    def _(sp):
                        sp.dma_start(wq[:], a["w_q"][0].rearrange("h d e -> d h e")).then_inc(lw, 16)
                        sp.dma_start(wk[:], a["w_k"][0].rearrange("h d e -> d h e")).then_inc(lw, 16)
                        sp.dma_start(wp[:], a["w_pool"][0].rearrange("g c d -> c g d")).then_inc(lw, 16)

                    @block.tensor
                    def _(pe):
                        pe.wait_ge(lw, 48)
                        n = 0
                        for h in range(HM):
                            for w_, in ((wq,), (wk,)):
                                for hf in range(2):
                                    if n >= 4:
                                        pe.wait_ge(q2, n - 3)
                                    pe.matmul(bank[n % 4][:], w_[:, h, :], ucT[:, h, hf * HALF:(hf + 1) * HALF], start=True, stop=True).then_inc(q1, 1)
                                    n += 1
                        for t in range(TT):
                            pe.wait_ge(q2, n - 3)
                            for h in range(HM):
                                ins = pe.matmul(bank[n % 4][:, h * P:(h + 1) * P], ucT[:, h, t * P:(t + 1) * P], wk[:, h, :], start=True, stop=True)
                            ins.then_inc(q1, 1)
                            n += 1
                        pe.wait_ge(g1, 8)
                        for t in range(TT):
                            if t in (4,):
                                pe.wait_ge(g2, 1)
                            ins = pe.transpose(bank[4][:, (t % 4) * P:(t % 4 + 1) * P], packed[:, t * P:(t + 1) * P], ident[:])
                            if t % 4 == 3:
                                ins.then_inc(rdy, 1)
                        pe.wait_ge(g1, 9)
                        for h in range(HM):
                            ins = pe.matmul(bank[5][:, h * NC_:(h + 1) * NC_], sel[:, h, :], aprev[:], start=True, stop=True)
                        ins.then_inc(rdy, 1)
                        n = 0
                        for h in range(HM):
                            for hf in range(2):
                                if n >= 2:
                                    pe.wait_ge(g2, 3 + n - 1)
                                pe.matmul(bank[6 + n % 2][:], sel[:, h, :], negM[:, hf * HALF:(hf + 1) * HALF], start=True, stop=True).then_inc(rdy, 1)
                                n += 1
                        pe.wait_ge(q2, 24)
                        for g in range(HM):
                            pe.wait_ge(pl, g + 1)
                            for hf in range(2):
                                if g >= 1:
                                    pe.wait_ge(pe_v, 2 * (g - 1) + hf + 1)
                                pe.matmul(bank[2 + hf][:], wp[:, g, :], yT[:, HM + g, hf * HALF:(hf + 1) * HALF], start=True, stop=True).then_inc(pm, 1)

                    @block.gpsimd
                    def _(pool):
                        pool.memset(packed[:], 0.0).then_inc(rw, 1)
                        pool.memset(rr[:, 5, :], 1.0).then_inc(rw, 1)
                        pool.memset(sel[:], 0.0).then_inc(rw, 1)
                        pool.memset(cmask[:], 0.0).then_inc(rw, 1)
                        pool.memset(mprev[:], 0.0).then_inc(rw, 1)
                        pool.memset(ps2[:, :, 0:POOL_PAD], 0.0).then_inc(rw, 1)
                        pool.iota(fix[:], [[0, HM], [1, 16]], base=1, channel_multiplier=0, allow_small_or_imprecise_dtypes=True).then_inc(rw, 1)
                        pool.wait_ge(rw, 7)
                        pool.memset(rr[:, 5, 0:S:P], 0.0).then_inc(rw, 1)
                        pool.affine_select(out=sel[:], in_=sel[:], compare_op=ALU.not_equal, fill=1.0, base=0,
                                           pattern=[[-1, HM], [0, P]], channel_multiplier=1).then_inc(rw, 1)
                        pool.affine_select(out=cmask[:], in_=cmask[:], compare_op=ALU.is_ge, fill=NEG, base=0,
                                           pattern=[[1, P]], channel_multiplier=-1).then_inc(rw, 1)

                    @block.scalar
                    def _(act):
                        n = 0
                        for h in range(HM):
                            for dst, sc in ((qT, P ** -0.5), (kT, 1.0)):
                                for hf in range(2):
                                    act.wait_ge(q1, n + 1)
                                    act.activation(dst[:, h, hf * HALF:(hf + 1) * HALF], bank[n % 4][:], ACT.Copy, scale=sc).then_inc(q2, 1)
                                    n += 1
                            if h == 0:
                                act.wait_ge(g1, 1)
                                act.activation(rr[:, 1, :], rr[:, 0, :], ACT.Exp, scale=-1.0).then_inc(rowexp, 1)
                                act.wait_ge(rowexp, 1)
                                act.activation(rr[:, 0, :], rr[:, 1, :], ACT.Ln, bias=1.0).then_inc(rowexp, 1)
                            if h == 2:
                                act.wait_ge(g1, 5)
                                act.activation(packed[32:32 + HM, :], rr[:, 0, :], ACT.Exp).then_inc(g1, 1)
                                act.activation(packed[64:64 + HM, :], rr[:, 2, :], ACT.Exp, scale=-1.0).then_inc(g1, 1)
                                act.activation(packed[96:96 + HM, :], rr[:, 4, :], ACT.Exp).then_inc(g1, 1)
                                act.activation(aprev[:], aprev[:], ACT.Exp).then_inc(g1, 1)
                        for t in range(TT):
                            act.wait_ge(q1, n + 1)
                            act.activation(ktok[:, t], bank[n % 4][:].rearrange("p (h e) -> p h e", h=HM), ACT.Copy).then_inc(q2, 1)
                            n += 1
                        for g in range(HM):
                            for hf in range(2):
                                act.wait_ge(pm, 2 * g + hf + 1)
                                act.activation(yT[:, HM + g, hf * HALF:(hf + 1) * HALF], bank[2 + hf][:], ACT.Identity,
                                               bias=pcol[:, 28 + g:29 + g]).then_inc(pe_v, 1)

                    @block.vector
                    def _(dve):
                        ch = [0]

                        def link(ins):
                            ins.then_inc(chain, 1)
                            ch[0] += 1
                            dve.wait_ge(chain, ch[0])

                        chain = sem("c_chain")
                        dve.wait_ge(rw, 10)
                        zi, zf = zrow[:, 0, :], zrow[:, 1, :]
                        dve.scalar_tensor_tensor(rr[:, 0, :], zf, -1.0, zf, ALU.mult, ALU.max).then_inc(g1, 1)
                        dve.wait_ge(rowexp, 2)
                        link(dve.scalar_tensor_tensor(rr[:, 1, :], zf, 0.0, rr[:, 0, :], ALU.min, ALU.subtract))
                        dve.tensor_tensor_scan(rr[:, 0, :], rr[:, 5, :], rr[:, 1, :], 0.0, ALU.mult, ALU.add)
                        link(dve.tensor_tensor_scan(rr[:, 2, :], rr[:, 1, :], zi, 0.0, ALU.add, ALU.max))
                        dve.tensor_tensor(packed[0:HM, :], zi, rr[:, 0, :], ALU.subtract)
                        dve.tensor_copy(mprev[:, 1:NC_], rr[:, 2, P - 1:S - P:P])
                        link(dve.tensor_tensor(rr[:, 3, :], rr[:, 2, :], rr[:, 0, :], ALU.subtract))
                        dve.tensor_scalar(negM, rr[:, 3, :], -1.0, None, ALU.mult).then_inc(g1, 1)
                        M3 = rr[:, 3, :].rearrange("h (c t) -> h c t", t=P)
                        last = rr[:, 3, P - 1:S:P]
                        dve.tensor_tensor(rr[:, 0, :].rearrange("h (c t) -> h c t", t=P), mprev[:].unsqueeze(2).to_broadcast([HM, NC_, P]),
                                          M3, ALU.subtract).then_inc(g1, 1)
                        dve.tensor_tensor(rr[:, 4, :].rearrange("h (c t) -> h c t", t=P), packed[0:HM, :].rearrange("h (c t) -> h c t", t=P),
                                          last.unsqueeze(2).to_broadcast([HM, NC_, P]), ALU.subtract).then_inc(g1, 1)
                        dve.tensor_tensor(aprev[:], mprev[:], last, ALU.subtract).then_inc(g1, 1)
                        link(dve.reciprocal(fix[:], fix[:]))
                        for g in range(HM):
                            win = 2 << g
                            link(dve.tensor_scalar(fix[:, g, :], fix[:, g, :], float(win), 1.0, ALU.mult, ALU.max))
                            link(dve.tensor_copy(ps2[:, 0, POOL_PAD:], yT[:, HM + g, :]))
                            src = 0
                            for j in range(g + 1):
                                link(dve.tensor_tensor(ps2[:, 1 - src, POOL_PAD:], ps2[:, src, POOL_PAD:],
                                                       ps2[:, src, POOL_PAD - (1 << j):POOL_PAD + S - (1 << j)], ALU.add))
                                src = 1 - src
                            link(dve.tensor_tensor(ps2[:, src, POOL_PAD:POOL_PAD + 16], ps2[:, src, POOL_PAD:POOL_PAD + 16], fix[:, g, :], ALU.mult))
                            dve.scalar_tensor_tensor(yT[:, HM + g, :], ps2[:, src, POOL_PAD:], 1.0 / win, yT[:, HM + g, :],
                                                     ALU.mult, ALU.subtract).then_inc(pl, 1)
                            dve.wait_ge(pl, g + 1)
                        for half in range(2):
                            dve.wait_ge(rdy, half + 1)
                            dve.tensor_copy(pk[:, 4 * half:4 * half + 4, :], bank[4][:].rearrange("p (t r) -> p t r", r=P)).then_inc(g2, 1)
                        dve.wait_ge(rdy, 3)
                        dve.tensor_copy(aprb[:], bank[5][:, 0:HM * NC_].rearrange("p (h c) -> p h c", c=NC_)).then_inc(g2, 1)
                        for n in range(8):
                            dve.wait_ge(rdy, 4 + n)
                            dve.tensor_copy(NM[:, n // 2, (n % 2) * HALF:(n % 2 + 1) * HALF], bank[6 + n % 2][:]).then_inc(g2, 1)
                        for g in range(HM):
                            dve.wait_ge(pe_v, 2 * g + 2)
                            dve.tensor_scalar(yT[:, HM + g, :], yT[:, HM + g, :], pcol[:, 32 + g:33 + g], None, ALU.mult).then_inc(pl, 1)
            with ExitStack() as c3:
                dl = sbuf(c3, "decay_log", [P, 2, P])
                de = sbuf(c3, "decay", [P, 2, P])
                st = sbuf(c3, "scores", [P, 2, P])
                vw = sbuf(c3, "v_weighted", [P, 2, P + 1])
                num = sbuf(c3, "num", [P, 2, P + 1])
                hn = sbuf(c3, "h_normed", [P, 2, P])
                hsq = sbuf(c3, "h_square", [P, 2, P])
                cst = sbuf(c3, "cell_stats", [P, 2, 6])
                inter = sbuf(c3, "inter", [P, 2, P + 1])
                ymix = sbuf(c3, "ymix", [P, 2, P])
                zrows = x1[:, 7, :]
                s_dl, s_de, s_qk, s_st, s_vw = sem("r_decaylog"), sem("r_decay"), sem("r_qk"), sem("r_scores"), sem("r_vw")
                s_ni, s_num, s_sq, s_hn, s_tr, s_up, s_y = sem("r_ni"), sem("r_num"), sem("r_sq"), sem("r_hn"), sem("r_tr"), sem("r_state"), sem("r_y")
                s_den, s_int, s_yc, s_ch = sem("r_den"), sem("r_inter"), sem("r_yc"), sem("r_chain")
                s_rs, s_se = sem("r_rstd"), sem("r_eps")
                steps = [(c, h) for c in range(NC_) for h in range(HM)]
                N = len(steps)
                s_zf, s_zd = sem("r_zeros"), sem("r_zeros_stored")
                with nc.Block() as block:
                    @block.sync
                    def _(sp):
                        sp.wait_ge(s_zf, 1)
                        sp.dma_start(moe_dram[MINB * P:, :].rearrange("(b p) n -> p b n", p=P),
                                     zrows[:].unsqueeze(1).to_broadcast([P, MAXB - MINB, D])).then_inc(s_zd, 16)
                        sp.wait_ge(s_zd, 16)

                    @block.tensor
                    def _(pe):
                        def scores(i):
                            c, h = steps[i]
                            if i >= 2:
                                pe.wait_ge(s_st, i - 1)
                            pe.matmul(bank[i % 2][:, 0:P], kT[:, h, c * P:(c + 1) * P], qT[:, h, c * P:(c + 1) * P], start=True, stop=True).then_inc(s_qk, 1)

                        def turn(i):
                            if i >= 2:
                                pe.wait_ge(s_y, i - 1)
                            pe.wait_ge(s_hn, i + 1)
                            pe.transpose(bank[6 + i % 2][:, 0:P], hn[:, i % 2, :], ident[:]).then_inc(s_tr, 1)

                        scores(0)
                        for i, (c, h) in enumerate(steps):
                            if i + 1 < N:
                                scores(i + 1)
                            pe.wait_ge(s_vw, i + 1)
                            if i >= 2:
                                pe.wait_ge(s_num, i - 1)
                                pe.wait_ge(s_up, i - 1)
                            if c >= 1:
                                pe.wait_ge(s_up, i - HM + 1)
                                pe.matmul(bank[2 + i % 2][:, 256:256 + P + 1], qT[:, h, c * P:(c + 1) * P], state[:, h, :], start=True, stop=True)
                            pe.matmul(bank[4 + i % 2][:, 0:P + 1], ktok[:, c, h, :], vw[:, i % 2, :], start=True, stop=True)
                            pe.wait_ge(s_st, i + 1)
                            pe.matmul(bank[2 + i % 2][:, 0:P + 1], st[:, i % 2, :], vaug[:, c, h, :], start=True, stop=True).then_inc(s_ni, 1)
                            if i >= 1:
                                turn(i - 1)
                        turn(N - 1)

                    @block.scalar
                    def _(act):
                        def decay(i):
                            act.wait_ge(s_dl, i + 1)
                            if i >= 2:
                                act.wait_ge(s_st, i - 1)
                            act.activation(de[:, i % 2, :], dl[:, i % 2, :], ACT.Exp).then_inc(s_de, 1)
                            c, h = steps[i]
                            if i >= 2:
                                act.wait_ge(s_ni, i - 1)
                            act.activation(vw[:, i % 2, :], vaug[:, c, h, :], ACT.Copy, scale=pk[:, c, 96 + h:97 + h]).then_inc(s_vw, 1)

                        decay(0)
                        for i in range(N):
                            if i + 1 < N:
                                decay(i + 1)
                            act.wait_ge(s_den, i + 1)
                            act.activation(hsq[:, i % 2, :], num[:, i % 2, 0:P], ACT.Square, scale=cst[:, i % 2, 1:2],
                                           accum_out=cst[:, i % 2, 2:3]).then_inc(s_sq, 1)

                    @block.gpsimd
                    def _(pool):
                        pool.memset(zrows[:], 0.0).then_inc(s_zf, 1)
                        for i in range(N):
                            pool.wait_ge(s_sq, i + 1)
                            if i >= 2:
                                pool.wait_ge(s_ch, 3 * (i - 2) + 3)
                            pool.tensor_scalar(cst[:, i % 2, 3:4], cst[:, i % 2, 2:3], P * EPS, None, ALU.add).then_inc(s_se, 1)
                            pool.wait_ge(s_se, i + 1)
                            pool.tensor_tensor(cst[:, i % 2, 4:5], cst[:, i % 2, 3:4], mhalf[:], ALU.pow).then_inc(s_rs, 1)

                    @block.vector
                    def _(dve):
                        def decay_log(i):
                            c, h = steps[i]
                            if i >= 2:
                                dve.wait_ge(s_de, i - 1)
                            dve.scalar_tensor_tensor(dl[:, i % 2, :], NM[:, h, c * P:(c + 1) * P], pk[:, c, h:h + 1], cmask[:],
                                                     ALU.add, ALU.add).then_inc(s_dl, 1)

                        def weigh(i):
                            dve.wait_ge(s_de, i + 1)
                            dve.wait_ge(s_qk, i + 1)
                            if i >= 2:
                                dve.wait_ge(s_ni, i - 1)
                            dve.tensor_tensor(st[:, i % 2, :], bank[i % 2][:, 0:P], de[:, i % 2, :], ALU.mult).then_inc(s_st, 1)

                        def finish(i):
                            c, h = steps[i]
                            at = slice(c * P, (c + 1) * P)
                            dve.tensor_scalar(ymix[:, i % 2, :], ucT[:, h, at], pcol[:, 24 + h:25 + h], None, ALU.mult).then_inc(s_yc, 1)
                            dve.wait_ge(s_tr, i + 1)
                            dve.wait_ge(s_yc, 2 * i + 1)
                            dve.scalar_tensor_tensor(ymix[:, i % 2, :], bank[6 + i % 2][:, 0:P], pcol[:, 20 + h:21 + h], ymix[:, i % 2, :],
                                                     ALU.mult, ALU.add).then_inc(s_yc, 1)
                            dve.wait_ge(s_yc, 2 * i + 2)
                            dve.tensor_tensor(yT[:, h, at], ymix[:, i % 2, :], sgo[:, h, at], ALU.mult).then_inc(s_y, 1)

                        decay_log(0)
                        decay_log(1)
                        weigh(0)
                        for i, (c, h) in enumerate(steps):
                            if i + 2 < N:
                                decay_log(i + 2)
                            if i + 1 < N:
                                weigh(i + 1)
                            b = i % 2
                            dve.wait_ge(s_ni, i + 1)
                            if i >= 2:
                                dve.wait_ge(s_sq, i - 1)
                            intra = bank[2 + b][:, 0:P + 1]
                            if c == 0:
                                dve.tensor_copy(num[:, b, :], intra).then_inc(s_num, 1)
                                dve.tensor_copy(state[:, h, :], bank[4 + b][:, 0:P + 1]).then_inc(s_up, 1)
                            else:
                                dve.tensor_scalar(inter[:, b, :], bank[2 + b][:, 256:256 + P + 1], pk[:, c, 32 + h:33 + h], None, ALU.mult).then_inc(s_int, 1)
                                dve.wait_ge(s_int, i - HM + 1)
                                dve.tensor_tensor(num[:, b, :], intra, inter[:, b, :], ALU.add).then_inc(s_num, 1)
                                dve.scalar_tensor_tensor(state[:, h, :], state[:, h, :], aprb[:, h, c:c + 1], bank[4 + b][:, 0:P + 1],
                                                         ALU.mult, ALU.add).then_inc(s_up, 1)
                            dve.wait_ge(s_num, i + 1)
                            dve.scalar_tensor_tensor(cst[:, b, 0:1], num[:, b, P:P + 1], -1.0, pk[:, c, 64 + h:65 + h], ALU.mult, ALU.max).then_inc(s_ch, 1)
                            dve.wait_ge(s_ch, 3 * i + 1)
                            dve.tensor_tensor(cst[:, b, 0:1], cst[:, b, 0:1], num[:, b, P:P + 1], ALU.max).then_inc(s_ch, 1)
                            dve.wait_ge(s_ch, 3 * i + 2)
                            dve.reciprocal(cst[:, b, 1:2], cst[:, b, 0:1]).then_inc(s_den, 1)
                            if i >= 1:
                                finish(i - 1)
                            dve.wait_ge(s_rs, i + 1)
                            dve.scalar_tensor_tensor(cst[:, b, 5:6], cst[:, b, 4:5], float(P) ** 0.5, cst[:, b, 1:2],
                                                     ALU.mult, ALU.mult).then_inc(s_ch, 1)
                            dve.wait_ge(s_ch, 3 * i + 3)
                            if i >= 2:
                                dve.wait_ge(s_tr, i - 1)
                            dve.tensor_scalar(hn[:, b, :], num[:, b, 0:P], cst[:, b, 5:6], None, ALU.mult).then_inc(s_hn, 1)
                        finish(N - 1)

        with ExitStack() as c2:
            wo = sbuf(c2, "w_out", [P, KT, D])
            mix = sbuf(c2, "mix", [P, 2, HALF])
            w_l, x_l, w_m, w_t, w_x = sem("o_w"), sem("o_x"), sem("o_mm"), sem("o_tmp"), sem("o_x1")
            with nc.Block() as block:
                @block.sync
                def _(sp):
                    sp.dma_start(wo[:], a["w_out"][0].rearrange("(k p) n -> p k n", p=P)).then_inc(w_l, 16)
                    sp.dma_start(x1[:], a["x"][0].rearrange("(t p) n -> p t n", p=P)).then_inc(x_l, 16)

                @block.tensor
                def _(pe):
                    pe.wait_ge(w_l, 16)
                    for i in range(2 * TT):
                        t, hf = divmod(i, 2)
                        if i >= 4:
                            pe.wait_ge(w_t, i - 3)
                        for k in range(KT):
                            ins = pe.matmul(bank[i % 4][:], yT[:, k, t * P:(t + 1) * P], wo[:, k, hf * HALF:(hf + 1) * HALF],
                                            start=(k == 0), stop=(k == KT - 1))
                        ins.then_inc(w_m, 1)

                @block.vector
                def _(dve):
                    dve.wait_ge(x_l, 16)
                    for i in range(2 * TT):
                        t, hf = divmod(i, 2)
                        at = slice(hf * HALF, (hf + 1) * HALF)
                        dve.wait_ge(w_m, i + 1)
                        dve.tensor_tensor(mix[:, i % 2, :], bank[i % 4][:], gates[:, 0, at], ALU.mult).then_inc(w_t, 1)
                        dve.wait_ge(w_t, i + 1)
                        dve.tensor_tensor(x1[:, t, at], x1[:, t, at], mix[:, i % 2, :], ALU.add).then_inc(w_x, 1)


def moe(nc, a, sbuf, sem, bank, ident, ones, mhalf, gates, colmod, x1, normed_dram, slots_dram, moe_dram, x2_out):
    NG = EG + NE
    with ExitStack() as ctx:
        rows_i = sbuf(ctx, "slot_rows", [P, TT, 2], I32)
        gate2 = sbuf(ctx, "token_gates", [P, TT, 2])
        slots = sbuf(ctx, "slots", [P, MAXB + 1], I32)
        bexp = sbuf(ctx, "block_expert", [1, MAXB], I32)
        npair = sbuf(ctx, "block_pairs", [1, 1], I32)
        logits = sbuf(ctx, "logits", [P, TT, NG])
        stat = sbuf(ctx, "moe_stat", [P, TT, 2])

        with ExitStack() as c2:
            sq = sbuf(c2, "moe_sq", [P, D])
            xn = sbuf(c2, "moe_xn", [P, 2, D])
            hTt = sbuf(c2, "moe_hT", [P, 2, KT, P])
            wr = sbuf(c2, "w_router", [P, KT, NG])
            br = sbuf(c2, "b_router", [1, NG])
            s_w, s_sq, s_e, s_rs, s_xn, s_tr, s_ht, s_lg, s_lc = [sem("g_" + n) for n in
                ("weights", "square", "eps", "rstd", "normed", "turned", "hT", "logits", "copied")]
            s_st = [sem("g_store0"), sem("g_store1")]
            with nc.Block() as block:
                @block.sync
                def _(sp):
                    sp.dma_start(wr[:, :, 0:EG], a["w_router_group"][0].rearrange("(p k) n -> p k n", k=KT)).then_inc(s_w, 16)
                    sp.dma_start(wr[:, :, EG:NG], a["w_router_expert"][0].rearrange("(p k) n -> p k n", k=KT)).then_inc(s_w, 16)
                    sp.dma_start(br[:, 0:EG], a["b_router_group"]).then_inc(s_w, 16)
                    sp.dma_start(br[:, EG:NG], a["b_router_expert"]).then_inc(s_w, 16)
                    for t in range(TT):
                        sp.wait_ge(s_xn, t + 1)
                        sp.dma_start(normed_dram[t * P:(t + 1) * P, :], xn[:, t % 2, :]).then_inc(s_st[t % 2], 16)
                    for u in range(2):
                        sp.wait_ge(s_st[u], 16 * (TT // 2))

                @block.scalar
                def _(act):
                    for t in range(TT):
                        if t >= 1:
                            act.wait_ge(s_sq, t)
                        act.activation(sq[:], x1[:, t, :], ACT.Square, accum_out=stat[:, t, 0:1]).then_inc(s_sq, 1)

                @block.gpsimd
                def _(pool):
                    for t in range(TT):
                        pool.wait_ge(s_sq, t + 1)
                        pool.tensor_scalar(stat[:, t, 0:1], stat[:, t, 0:1], D * EPS, None, ALU.add).then_inc(s_e, 1)
                        pool.wait_ge(s_e, t + 1)
                        pool.tensor_tensor(stat[:, t, 1:2], stat[:, t, 0:1], mhalf[:], ALU.pow).then_inc(s_rs, 1)

                @block.vector
                def _(dve):
                    def copy_logits(t):
                        dve.wait_ge(s_lg, t + 1)
                        dve.tensor_copy(logits[:, t, :], bank[4 + t % 2][:, 0:NG]).then_inc(s_lc, 1)

                    for t in range(TT):
                        dve.wait_ge(s_rs, t + 1)
                        if t >= 2:
                            dve.wait_ge(s_tr, 2 * (t - 1))
                            dve.wait_ge(s_st[t % 2], 16 * (t // 2))
                        dve.tensor_scalar(xn[:, t % 2, :], x1[:, t, :], stat[:, t, 1:2], ROOT_D, ALU.mult, ALU.mult).then_inc(s_xn, 1)
                        if t >= 2:
                            dve.wait_ge(s_lg, t - 1)
                        for g in range(2):
                            dve.wait_ge(s_tr, 2 * t + g + 1)
                            for k in range(4 * g, 4 * g + 4):
                                ins = dve.tensor_scalar(hTt[:, t % 2, k, :], bank[g + 2 * (t % 2)][:, (k % 4) * P:(k % 4 + 1) * P],
                                                        colmod[:, 0, 3, k:k + 1], colmod[:, 0, 2, k:k + 1], ALU.mult, ALU.add)
                            ins.then_inc(s_ht, 1)
                        if t >= 1:
                            copy_logits(t - 1)
                    copy_logits(TT - 1)

                @block.tensor
                def _(pe):
                    pe.wait_ge(s_w, 64)

                    def route(t):
                        pe.wait_ge(s_ht, 2 * t + 2)
                        if t >= 2:
                            pe.wait_ge(s_lc, t - 1)
                        for k in range(KT):
                            pe.matmul(bank[4 + t % 2][:, 0:NG], hTt[:, t % 2, k, :], wr[:, k, :], start=(k == 0), stop=False)
                        pe.matmul(bank[4 + t % 2][:, 0:NG], ones[0:1, :], br[:], start=False, stop=True).then_inc(s_lg, 1)

                    for t in range(TT):
                        pe.wait_ge(s_xn, t + 1)
                        if t >= 2:
                            pe.wait_ge(s_ht, 2 * (t - 1))
                        for g in range(2):
                            for k in range(4 * g, 4 * g + 4):
                                ins = pe.transpose(bank[g + 2 * (t % 2)][:, (k % 4) * P:(k % 4 + 1) * P], xn[:, t % 2, k:D:KT], ident[:])
                            ins.then_inc(s_tr, 1)
                        if t >= 1:
                            route(t - 1)
                    route(TT - 1)

        with ExitStack() as c2:
            gl8 = sbuf(c2, "group_logits", [P, TT, 8])
            gm8 = sbuf(c2, "group_max", [P, TT, 8])
            gi8 = sbuf(c2, "group_index", [P, TT, 8], U32)
            gif = sbuf(c2, "group_of_token", [P, TT])
            gex = sbuf(c2, "group_exp", [P, TT, EG])
            gs = sbuf(c2, "group_gate", [P, TT])
            io = sbuf(c2, "iota_32", [P, NE])
            iob = sbuf(c2, "iota_blocks", [1, MAXB])
            iop = sbuf(c2, "iota_pairs", [1, MAXB // 2])
            oh4 = sbuf(c2, "group_onehot", [P, TT, EG])
            prod = sbuf(c2, "group_product", [P, TT, EG, EPG])
            es = sbuf(c2, "expert_logits", [P, TT, EPG])
            em8 = sbuf(c2, "expert_max", [P, TT, 8])
            ei8 = sbuf(c2, "expert_index", [P, TT, 8], U32)
            eif = sbuf(c2, "expert_of_token", [P, TT, 2])
            ed = sbuf(c2, "second_exp", [P, TT])
            er = sbuf(c2, "first_share", [P, TT])
            oh = sbuf(c2, "expert_onehot", [P, 2, TT, NE])
            mem = sbuf(c2, "membership", [P, TT, NE], BF16)
            before = sbuf(c2, "before", [P, P], BF16)
            onesb = sbuf(c2, "ones_bf16", [P, P], BF16)
            rank = sbuf(c2, "rank_all", [P, TT, NE])
            cnt = sbuf(c2, "counts", [P, NE])
            nb = sbuf(c2, "expert_blocks", [P, NE])
            ends = sbuf(c2, "block_ends", [P, NE])
            starts = sbuf(c2, "block_starts", [P, NE])
            onerow = sbuf(c2, "ones_row", [P, NE])
            t3 = sbuf(c2, "onehot_product", [P, TT, NE])
            rk = sbuf(c2, "rank", [P, 2, TT])
            sb_ = sbuf(c2, "start_block", [P, 2, TT])
            jj = sbuf(c2, "block_in_expert", [P, 2, TT])
            fslot = sbuf(c2, "slot_float", [P, 2, TT])
            slot_i = sbuf(c2, "slot_int", [P, 2, TT], I32)
            tok_i = sbuf(c2, "token_id", [P, TT], I32)
            zer = sbuf(c2, "zero_slots", [P, MAXB], I32)
            cmp_ = sbuf(c2, "block_compare", [1, MAXB, NE])
            bf = sbuf(c2, "block_expert_float", [1, MAXB])
            pf = sbuf(c2, "pair_compare", [1, MAXB // 2])
            pn = sbuf(c2, "pair_float", [1, 1])
            s_c, s_ex, s_m, s_rk, s_ch, s_sl, s_z, s_sc, s_ld = [sem("t_" + n) for n in
                ("consts", "exps", "member", "ranks", "chain", "slots", "zeroed", "scattered", "loaded")]
            s_go = sem("t_go")
            with nc.Block() as block:
                @block.gpsimd
                def _(pool):
                    pool.iota(io[:], [[1, NE]], base=0, channel_multiplier=0, allow_small_or_imprecise_dtypes=True).then_inc(s_c, 1)
                    pool.iota(iob[:], [[1, MAXB]], base=0, channel_multiplier=0, allow_small_or_imprecise_dtypes=True).then_inc(s_c, 1)
                    pool.iota(iop[:], [[2, MAXB // 2]], base=0, channel_multiplier=0, allow_small_or_imprecise_dtypes=True).then_inc(s_c, 1)
                    pool.iota(tok_i[:], [[P, TT]], base=0, channel_multiplier=1).then_inc(s_c, 1)
                    pool.memset(before[:], 1.0).then_inc(s_c, 1)
                    pool.memset(onesb[:], 1.0).then_inc(s_c, 1)
                    pool.memset(onerow[:], 1.0).then_inc(s_c, 1)
                    pool.memset(zer[:], 0).then_inc(s_c, 1)
                    pool.memset(slots[:, MAXB:MAXB + 1], 0).then_inc(s_c, 1)
                    pool.wait_ge(s_c, 9)
                    pool.affine_select(out=before[:], in_=before[:], compare_op=ALU.is_gt, fill=0.0, base=0,
                                       pattern=[[1, P]], channel_multiplier=-1).then_inc(s_c, 1)
                    pool.wait_ge(s_z, 16)
                    pool.wait_ge(s_sl, 1)
                    for k in range(2):
                        for t in range(TT):
                            pool.indirect_dma_start(slots_dram, bass.IndirectOffsetOnAxis(ap=slot_i[:, k, t:t + 1], axis=0),
                                                    tok_i[:, t:t + 1], None).then_inc(s_sc, 16)

                @block.sync
                def _(sp):
                    sp.wait_ge(s_c, 9)
                    sp.dma_start(slots_dram.rearrange("(p b) o -> p (b o)", b=MAXB), zer[:]).then_inc(s_z, 16)
                    sp.wait_ge(s_sc, 16 * 2 * TT)
                    sp.dma_start(slots[:, 0:MAXB], slots_dram.rearrange("(p b) o -> p (b o)", b=MAXB)).then_inc(s_ld, 16)
                    sp.wait_ge(s_ld, 16)

                @block.scalar
                def _(act):
                    act.wait_ge(s_go, 1)
                    act.activation(gex[:], gex[:], ACT.Exp).then_inc(s_ex, 1)
                    act.wait_ge(s_go, 2)
                    act.activation(ed[:], ed[:], ACT.Exp).then_inc(s_ex, 1)

                @block.tensor
                def _(pe):
                    pe.wait_ge(s_c, 10)
                    pe.wait_ge(s_m, 1)
                    for t in range(TT):
                        for j in range(t + 1):
                            pe.matmul(bank[0][:, t * NE:(t + 1) * NE], before[:] if j == t else onesb[:], mem[:, j, :],
                                      start=(j == 0), stop=(j == t))
                    for t in range(TT):
                        ins = pe.matmul(bank[1][:, 0:NE], onesb[:], mem[:, t, :], start=(t == 0), stop=(t == TT - 1))
                    ins.then_inc(s_rk, 1)

                @block.vector
                def _(dve):
                    ch = [0]

                    def link(ins):
                        ins.then_inc(s_ch, 1)
                        ch[0] += 1
                        dve.wait_ge(s_ch, ch[0])

                    def over(x, n):
                        return x.unsqueeze(len(x.shape)).to_broadcast([*x.shape, n])

                    dve.wait_ge(s_c, 10)
                    link(dve.memset(gl8[:], NEG))
                    link(dve.tensor_copy(gl8[:, :, 0:EG], logits[:, :, 0:EG]))
                    for t in range(TT):
                        ins = dve.max(gm8[:, t, :], gl8[:, t, :])
                    link(ins)
                    for t in range(TT):
                        ins = dve.max_index(gi8[:, t, :], gm8[:, t, :], gl8[:, t, :])
                    link(ins)
                    dve.tensor_tensor(gex[:], gl8[:, :, 0:EG], over(gm8[:, :, 0], EG), ALU.subtract).then_inc(s_go, 1)
                    link(dve.tensor_copy(gif[:], gi8[:, :, 0]))
                    link(dve.tensor_tensor(oh4[:], io[:, 0:EG].unsqueeze(1).to_broadcast([P, TT, EG]), over(gif[:], EG), ALU.is_equal))
                    link(dve.tensor_tensor(prod[:], logits[:, :, EG:NG].rearrange("p t (g e) -> p t g e", g=EG), over(oh4[:], EPG), ALU.mult))
                    link(dve.tensor_tensor(es[:], prod[:, :, 0, :], prod[:, :, 1, :], ALU.add))
                    link(dve.tensor_tensor(es[:], es[:], prod[:, :, 2, :], ALU.add))
                    link(dve.tensor_tensor(es[:], es[:], prod[:, :, 3, :], ALU.add))
                    for t in range(TT):
                        ins = dve.max(em8[:, t, :], es[:, t, :])
                    link(ins)
                    for t in range(TT):
                        ins = dve.max_index(ei8[:, t, :], em8[:, t, :], es[:, t, :])
                    link(ins)
                    dve.tensor_tensor(ed[:], em8[:, :, 1], em8[:, :, 0], ALU.subtract).then_inc(s_go, 1)
                    link(dve.tensor_copy(eif[:], ei8[:, :, 0:2]))
                    link(dve.scalar_tensor_tensor(eif[:], over(gif[:], 2), float(EPG), eif[:], ALU.mult, ALU.add))
                    for k in range(2):
                        ins = dve.tensor_tensor(oh[:, k], io[:].unsqueeze(1).to_broadcast([P, TT, NE]), over(eif[:, :, k], NE), ALU.is_equal)
                        link(ins)
                    dve.tensor_tensor(mem[:], oh[:, 0], oh[:, 1], ALU.add).then_inc(s_m, 1)
                    dve.wait_ge(s_ex, 2)
                    link(dve.tensor_reduce(gs[:], gex[:], X, ALU.add))
                    link(dve.tensor_scalar(er[:], ed[:], 1.0, None, ALU.add))
                    link(dve.tensor_tensor(er[:], er[:], gs[:], ALU.mult))
                    link(dve.reciprocal(gate2[:, :, 0], er[:]))
                    link(dve.tensor_tensor(gate2[:, :, 1], gate2[:, :, 0], ed[:], ALU.mult))
                    dve.wait_ge(s_rk, 1)
                    link(dve.tensor_copy(rank[:], bank[0][:, 0:TT * NE].rearrange("p (t e) -> p t e", e=NE)))
                    link(dve.tensor_copy(cnt[:], bank[1][:, 0:NE]))
                    link(dve.tensor_scalar(nb[:], cnt[:], 0.0, None, ALU.is_gt))
                    for j in range(1, TT):
                        link(dve.scalar_tensor_tensor(nb[:], cnt[:], float(P * j), nb[:], ALU.is_gt, ALU.add))
                    link(dve.tensor_tensor_scan(ends[:], onerow[:], nb[:], 0.0, ALU.mult, ALU.add))
                    link(dve.tensor_tensor(starts[:], ends[:], nb[:], ALU.subtract))
                    for k in range(2):
                        link(dve.tensor_tensor(t3[:], oh[:, k], rank[:], ALU.mult))
                        link(dve.tensor_reduce(rk[:, k], t3[:], X, ALU.add))
                        link(dve.tensor_tensor(t3[:], oh[:, k], starts[:].unsqueeze(1).to_broadcast([P, TT, NE]), ALU.mult))
                        link(dve.tensor_reduce(sb_[:, k], t3[:], X, ALU.add))
                    link(dve.tensor_scalar(jj[:], rk[:], float(P), None, ALU.is_ge))
                    for j in range(2, TT):
                        link(dve.scalar_tensor_tensor(jj[:], rk[:], float(P * j), jj[:], ALU.is_ge, ALU.add))
                    link(dve.tensor_tensor(sb_[:], sb_[:], jj[:], ALU.add))
                    link(dve.scalar_tensor_tensor(rk[:], jj[:], -float(P), rk[:], ALU.mult, ALU.add))
                    link(dve.scalar_tensor_tensor(fslot[:], rk[:], float(MAXB), sb_[:], ALU.mult, ALU.add))
                    dve.tensor_copy(slot_i[:], fslot[:]).then_inc(s_sl, 1)
                    dve.wait_ge(s_sl, 1)
                    link(dve.scalar_tensor_tensor(fslot[:], sb_[:], float(P), rk[:], ALU.mult, ALU.add))
                    link(dve.tensor_copy(rows_i[:].rearrange("p t k -> p k t"), fslot[:]))
                    link(dve.tensor_tensor(cmp_[:], ends[0:1, :].unsqueeze(1).to_broadcast([1, MAXB, NE]), over(iob[:], NE), ALU.is_le))
                    link(dve.tensor_reduce(bf[:], cmp_[:], X, ALU.add))
                    link(dve.tensor_scalar(bf[:], bf[:], float(NE - 1), None, ALU.min))
                    link(dve.tensor_copy(bexp[:], bf[:]))
                    link(dve.tensor_scalar(pf[:], iop[:], ends[0:1, NE - 1:NE], None, ALU.is_lt))
                    link(dve.tensor_reduce(pn[:], pf[:], X, ALU.add))
                    link(dve.tensor_copy(npair[:], pn[:]))

        with ExitStack() as c2:
            wg = sbuf(c2, "w_gate", [P, 2, KT, DE])
            wu = sbuf(c2, "w_up", [P, 2, KT, DE])
            xg = sbuf(c2, "gathered", [P, 2, D])
            hTb = sbuf(c2, "block_hT", [P, KT, P])
            sg = sbuf(c2, "silu", [P, DE])
            gg = sbuf(c2, "gated", [P, DE])
            gT = sbuf(c2, "gatedT", [P, JT, P])
            ob = sbuf(c2, "block_out", [P, 2, D])
            wd = sbuf(c2, "w_down", [P, 1, JT, D])
            idx = sbuf(c2, "block_index", [P, 2], I32)
            l_g = [sem("b_wgate0"), sem("b_wgate1")]
            l_u = [sem("b_wup0"), sem("b_wup1")]
            l_d = sem("b_wdown")
            s_ix, s_tr, s_ht, s_gu, s_sg, s_gg, s_gt, s_gc, s_dn, s_ob = [sem("b_" + n) for n in
                ("index", "turned", "hT", "gate_up", "silu", "gated", "gatedT", "gatedT_copied", "down", "out_copied")]
            s_own, s_own2 = sem("b_carrier"), sem("b_carrier2")
            s_x = [sem("b_gather0"), sem("b_gather1")]
            s_out = [sem("b_store0"), sem("b_store1")]
            wgd = a["w_expert_gate"][0].rearrange("e (p k) n -> e p (k n)", k=KT)
            wud = a["w_expert_up"][0].rearrange("e (p k) n -> e p (k n)", k=KT)
            wdd = a["w_expert_down"][0].rearrange("e (p j) n -> e p (j n)", j=JT)

            def pairs(eng):
                return eng.value_load(npair[0:1, 0:1], min_val=1, max_val=MAXB // 2)

            with nc.Block() as block:
                @block.sync
                def _(sp):
                    with sp.Fori(0, pairs(sp)) as i:
                        for u in range(2):
                            e = sp.value_load(bexp[0:1, bass.ds(i * 2 + u, 1)], min_val=0, max_val=NE - 1)
                            sp.wait_ge(s_gu, i * 2 + u + 1)
                            sp.dma_start(wg[:, u].rearrange("p k n -> p (k n)"), wgd[bass.ds(e, 1)].rearrange("o p n -> (o p) n")).then_inc(l_g[u], 16)
                            sp.dma_start(wu[:, u].rearrange("p k n -> p (k n)"), wud[bass.ds(e, 1)].rearrange("o p n -> (o p) n")).then_inc(l_u[u], 16)
                            sp.wait_ge(s_dn, i * 2 + u + 1)
                            sp.dma_start(wd[:, 0].rearrange("p k n -> p (k n)"), wdd[bass.ds(e, 1)].rearrange("o p n -> (o p) n")).then_inc(l_d, 16)

                @block.gpsimd
                def _(pool):
                    pool.tensor_copy(idx[:, 0:1], slots[:, 0:1]).then_inc(s_ix, 1)
                    pool.wait_ge(s_ix, 1)
                    pool.indirect_dma_start(xg[:, 0, :], None, normed_dram, bass.IndirectOffsetOnAxis(ap=idx[:, 0:1], axis=0)).then_inc(s_x[0], 16)
                    with pool.Fori(0, pairs(pool)) as i:
                        for u in range(2):
                            v = 1 - u
                            pool.wait_ge(s_tr, i * 2 + u + 1)
                            pool.tensor_copy(idx[:, v:v + 1], slots[:, bass.ds(i * 2 + u + 1, 1)]).then_inc(s_ix, 1)
                            pool.wait_ge(s_ix, i * 2 + u + 2)
                            pool.sem_inc(s_own, 1)
                            pool.indirect_dma_start(xg[:, v, :], None, normed_dram,
                                                    bass.IndirectOffsetOnAxis(ap=idx[:, v:v + 1], axis=0)).then_inc(s_x[v], 16)

                @block.tensor
                def _(pe):
                    pe.sem_inc(s_gu, 2)
                    pe.sem_inc(s_dn, 1)

                    def turn(u):
                        for k in range(KT):
                            ins = pe.transpose(bank[k // 4][:, (k % 4) * P:(k % 4 + 1) * P], xg[:, u, k:D:KT], ident[:])
                        ins.then_inc(s_tr, 1)

                    pe.wait_ge(s_x[0], 16)
                    turn(0)
                    with pe.Fori(0, pairs(pe)) as i:
                        for u in range(2):
                            n = i * 2 + u
                            pe.wait_ge(s_ht, n + 1)
                            pe.wait_ge(s_gg, n + 1)
                            pe.wait_ge(l_g[u], i * 16 + 16)
                            for k in range(KT):
                                pe.matmul(bank[2], hTb[:, k, :], wg[:, u, k, :], start=(k == 0), stop=(k == KT - 1))
                            pe.wait_ge(l_u[u], i * 16 + 16)
                            for k in range(KT):
                                ins = pe.matmul(bank[3], hTb[:, k, :], wu[:, u, k, :], start=(k == 0), stop=(k == KT - 1))
                            ins.then_inc(s_gu, 1)
                            if u == 0:
                                pe.wait_ge(s_x[1], i * 16 + 16)
                            else:
                                pe.wait_ge(s_x[0], i * 16 + 32)
                            turn(1 - u)
                            pe.wait_ge(s_gg, n + 2)
                            pe.wait_ge(s_gc, n + 1)
                            for j in range(JT):
                                ins = pe.transpose(bank[4][:, j * P:(j + 1) * P], gg[:, j:DE:JT], ident[:])
                            ins.then_inc(s_gt, 1)
                            pe.wait_ge(s_gc, n + 2)
                            pe.wait_ge(s_ob, n + 1)
                            pe.wait_ge(l_d, i * 32 + 16 * (u + 1))
                            for hf in range(2):
                                for j in range(JT):
                                    ins = pe.matmul(bank[5 + hf], gT[:, j, :], wd[:, 0, j, hf * HALF:(hf + 1) * HALF], start=(j == 0), stop=(j == JT - 1))
                            ins.then_inc(s_dn, 1)

                @block.scalar
                def _(act):
                    act.sem_inc(s_gc, 1)
                    act.sem_inc(s_ob, 1)
                    act.sem_inc(s_out[0], 16)
                    act.sem_inc(s_out[1], 16)
                    n_pairs = pairs(act)
                    with act.Fori(0, n_pairs) as i:
                        for u in range(2):
                            n = i * 2 + u
                            act.wait_ge(s_gu, n + 3)
                            act.wait_ge(s_gg, n + 1)
                            act.activation(sg[:], bank[2], ACT.Silu).then_inc(s_sg, 1)
                            act.wait_ge(s_gt, n + 1)
                            act.wait_ge(s_dn, n + 1)
                            act.activation(gT[:], bank[4].rearrange("p (j t) -> p j t", t=P), ACT.Copy).then_inc(s_gc, 1)
                            act.wait_ge(s_dn, n + 2)
                            act.wait_ge(s_out[u], i * 16 + 16)
                            act.activation(ob[:, u, 0:HALF], bank[5], ACT.Copy)
                            act.activation(ob[:, u, HALF:D], bank[6], ACT.Copy).then_inc(s_ob, 1)
                            act.wait_ge(s_ob, n + 2)
                            act.dma_start(moe_dram[bass.ds((i * 2 + u) * P, P), :], ob[:, u, :]).then_inc(s_out[u], 16)
                    for u in range(2):
                        act.wait_ge(s_out[u], n_pairs * 16 + 16)
                        act.sem_inc(s_own2, 1)

                @block.vector
                def _(dve):
                    dve.sem_inc(s_gg, 1)

                    def leave():
                        for k in range(KT):
                            ins = dve.tensor_scalar(hTb[:, k, :], bank[k // 4][:, (k % 4) * P:(k % 4 + 1) * P],
                                                    colmod[:, 0, 3, k:k + 1], colmod[:, 0, 2, k:k + 1], ALU.mult, ALU.add)
                        ins.then_inc(s_ht, 1)

                    dve.wait_ge(s_tr, 1)
                    leave()
                    with dve.Fori(0, pairs(dve)) as i:
                        for u in range(2):
                            n = i * 2 + u
                            dve.wait_ge(s_sg, n + 1)
                            dve.tensor_tensor(gg[:], bank[3], sg[:], ALU.mult).then_inc(s_gg, 1)
                            dve.wait_ge(s_tr, n + 2)
                            leave()

        with ExitStack() as c2:
            r0 = sbuf(c2, "result0", [P, 2, D])
            r1 = sbuf(c2, "result1", [P, 2, D])
            yy = sbuf(c2, "combined", [P, 2, D])
            sq = sbuf(c2, "comb_sq", [P, D])
            xo = sbuf(c2, "x2_tile", [P, 2, D])
            fg = sbuf(c2, "final_gain", [P, D])
            s_fg, s_a, s_b, s_y, s_sq, s_e, s_rs, s_o, s_r = [sem("e_" + n) for n in ("gain", "first", "second", "sum", "square", "eps", "rstd", "out", "root")]
            s_g = [[sem(f"e_gather{k}{u}") for u in range(2)] for k in range(2)]
            s_st = [sem("e_store0"), sem("e_store1")]
            with nc.Block() as block:
                @block.sync
                def _(sp):
                    sp.dma_start(fg[:], a["final_g"].rearrange("(o n) -> o n", o=1).to_broadcast([P, D])).then_inc(s_fg, 16)
                    for t in range(TT):
                        sp.wait_ge(s_o, t + 1)
                        sp.dma_start(x2_out[t * P:(t + 1) * P, :], xo[:, t % 2, :]).then_inc(s_st[t % 2], 16)
                    for u in range(2):
                        sp.wait_ge(s_st[u], 16 * (TT // 2))

                @block.gpsimd
                def _(pool):
                    def root(t):
                        pool.wait_ge(s_sq, t + 1)
                        pool.tensor_scalar(stat[:, t, 0:1], stat[:, t, 0:1], D * EPS, None, ALU.add).then_inc(s_e, 1)
                        pool.wait_ge(s_e, 2 * t + 1)
                        pool.tensor_tensor(stat[:, t, 1:2], stat[:, t, 0:1], mhalf[:], ALU.pow).then_inc(s_e, 1)
                        pool.wait_ge(s_e, 2 * t + 2)
                        pool.tensor_scalar(stat[:, t, 1:2], stat[:, t, 1:2], ROOT_D, None, ALU.mult).then_inc(s_rs, 1)

                    for t in range(TT):
                        if t >= 2:
                            pool.wait_ge(s_b, t - 1)
                        for k, r in enumerate((r0, r1)):
                            pool.indirect_dma_start(r[:, t % 2, :], None, moe_dram,
                                                    bass.IndirectOffsetOnAxis(ap=rows_i[:, t, k:k + 1], axis=0)).then_inc(s_g[k][t % 2], 16)
                        if t >= 1:
                            root(t - 1)
                    root(TT - 1)

                @block.scalar
                def _(act):
                    for t in range(TT):
                        act.wait_ge(s_y, t + 1)
                        if t >= 1:
                            act.wait_ge(s_sq, t)
                        act.activation(sq[:], x1[:, t, :], ACT.Square, accum_out=stat[:, t, 0:1]).then_inc(s_sq, 1)

                @block.vector
                def _(dve):
                    def close(t):
                        dve.wait_ge(s_rs, t + 1)
                        if t == 0:
                            dve.wait_ge(s_fg, 16)
                        if t >= 2:
                            dve.wait_ge(s_st[t % 2], 16 * (t // 2))
                        dve.scalar_tensor_tensor(xo[:, t % 2, :], x1[:, t, :], stat[:, t, 1:2], fg[:], ALU.mult, ALU.mult).then_inc(s_o, 1)

                    for t in range(TT):
                        u = t % 2
                        dve.wait_ge(s_g[0][u], 16 * (t // 2 + 1))
                        dve.tensor_scalar(yy[:, u, :], r0[:, u, :], gate2[:, t, 0:1], None, ALU.mult).then_inc(s_a, 1)
                        dve.wait_ge(s_a, 2 * t + 1)
                        dve.wait_ge(s_g[1][u], 16 * (t // 2 + 1))
                        dve.scalar_tensor_tensor(yy[:, u, :], r1[:, u, :], gate2[:, t, 1:2], yy[:, u, :], ALU.mult, ALU.add).then_inc(s_b, 1)
                        dve.wait_ge(s_b, t + 1)
                        dve.tensor_tensor(yy[:, u, :], yy[:, u, :], gates[:, 1, :], ALU.mult).then_inc(s_a, 1)
                        dve.wait_ge(s_a, 2 * t + 2)
                        dve.tensor_tensor(x1[:, t, :], x1[:, t, :], yy[:, u, :], ALU.add).then_inc(s_y, 1)
                        if t >= 1:
                            close(t - 1)
                    close(TT - 1)


def norm_turn(nc, ctx, tag, sbuf, sem, bank, ident, mhalf, gain, shift, hT, src, src_dram):
    stat = sbuf(ctx, tag + "_stat", [P, TT, 2])
    sq = sbuf(ctx, tag + "_sq", [P, D])
    xn = sbuf(ctx, tag + "_xn", [P, 2, D])
    s_ld = [sem(tag + "_load0"), sem(tag + "_load1")]
    s_sq, s_e, s_rs, s_xn, s_tr, s_ht = [sem(tag + "_" + n) for n in ("square", "eps", "rstd", "normed", "turned", "hT")]
    ring = src.shape[1]
    with nc.Block() as block:
        if src_dram is not None:
            @block.sync
            def _(sp):
                for t in range(TT):
                    if t >= ring:
                        sp.wait_ge(s_xn, t - ring + 1)
                        sp.wait_ge(s_sq, t - ring + 1)
                    sp.dma_start(src[:, t % ring, :], src_dram[t * P:(t + 1) * P, :]).then_inc(s_ld[t % 2], 16)

        @block.scalar
        def _(act):
            for t in range(TT):
                if src_dram is not None:
                    act.wait_ge(s_ld[t % 2], 16 * (t // 2 + 1))
                if t >= 1:
                    act.wait_ge(s_sq, t)
                act.activation(sq[:], src[:, t % ring, :], ACT.Square, accum_out=stat[:, t, 0:1]).then_inc(s_sq, 1)

        @block.gpsimd
        def _(pool):
            for t in range(TT):
                pool.wait_ge(s_sq, t + 1)
                pool.tensor_scalar(stat[:, t, 0:1], stat[:, t, 0:1], D * EPS, None, ALU.add).then_inc(s_e, 1)
                pool.wait_ge(s_e, t + 1)
                pool.tensor_tensor(stat[:, t, 1:2], stat[:, t, 0:1], mhalf[:], ALU.pow).then_inc(s_rs, 1)

        @block.vector
        def _(dve):
            for t in range(TT):
                dve.wait_ge(s_rs, t + 1)
                if t >= 2:
                    dve.wait_ge(s_tr, 2 * (t - 1))
                dve.tensor_scalar(xn[:, t % 2, :], src[:, t % ring, :], stat[:, t, 1:2], ROOT_D, ALU.mult, ALU.mult).then_inc(s_xn, 1)
                for g in range(2):
                    dve.wait_ge(s_tr, 2 * t + g + 1)
                    for k in range(4 * g, 4 * g + 4):
                        ins = dve.tensor_scalar(hT[:, k, t * P:(t + 1) * P], bank[g + 2 * (t % 2)][:, (k % 4) * P:(k % 4 + 1) * P],
                                                gain[:, k:k + 1], shift[:, k:k + 1], ALU.mult, ALU.add)
                    ins.then_inc(s_ht, 1)

        @block.tensor
        def _(pe):
            for t in range(TT):
                pe.wait_ge(s_xn, t + 1)
                if t >= 2:
                    pe.wait_ge(s_ht, 2 * (t - 1))
                for g in range(2):
                    for k in range(4 * g, 4 * g + 4):
                        ins = pe.transpose(bank[g + 2 * (t % 2)][:, (k % 4) * P:(k % 4 + 1) * P], xn[:, t % 2, k:D:KT], ident[:])
                    ins.then_inc(s_tr, 1)


def attention(nc, a, sbuf, sem, bank, ident, ones, mhalf, gates, colmod, psum, x2_dram, negf_dram, x3, hT):
    w_pk = a["fox_w_in_2"][0].rearrange("(p k) n -> p k n", k=KT)
    with ExitStack() as outer:
        with ExitStack() as c2:
            xl = sbuf(c2, "fox_x_rows", [P, 2, D])
            norm_turn(nc, c2, "f", sbuf, sem, bank, ident, mhalf, colmod[:, 1, 1, :], colmod[:, 1, 0, :], hT, xl, x2_dram)
        with ExitStack() as ctx:
            vtok = sbuf(ctx, "v_rows", [P, TT, D])
            with ExitStack() as c2:
                wv = sbuf(c2, "w_value", [P, KT, D])
                wf = sbuf(c2, "w_forget", [P, KT, HF])
                fb = sbuf(c2, "forget_bias", [HF, 1])
                fr = sbuf(c2, "forget_rows", [HF, 3, S])
                s_w, s_wf, s_m, s_c, s_f, s_ch, s_st = [sem("v_" + n) for n in ("weights", "wforget", "mm", "copied", "frow", "chain", "stored")]
                with nc.Block() as block:
                    @block.sync
                    def _(sp):
                        sp.dma_start(wf[:], w_pk[:, :, 3 * D:3 * D + HF]).then_inc(s_wf, 16)
                        sp.dma_start(fb[:], a["fox_b_f_2"][0].rearrange("(h o) -> h o", o=1)).then_inc(s_wf, 16)
                        sp.dma_start(wv[:], w_pk[:, :, 2 * D:3 * D]).then_inc(s_w, 16)
                        sp.wait_ge(s_ch, 7)
                        sp.dma_start(negf_dram, fr[:, 1, :]).then_inc(s_st, 16)
                        sp.wait_ge(s_st, 16)

                    @block.tensor
                    def _(pe):
                        pe.wait_ge(s_wf, 32)
                        for hf in range(2):
                            for k in range(KT):
                                ins = pe.matmul(bank[4 + hf][0:HF, :], wf[:, k, :], hT[:, k, hf * HALF:(hf + 1) * HALF], start=(k == 0), stop=(k == KT - 1))
                            ins.then_inc(s_f, 1)
                        pe.wait_ge(s_w, 16)
                        for i in range(2 * TT):
                            t, hf = divmod(i, 2)
                            if i >= 4:
                                pe.wait_ge(s_c, i - 3)
                            for k in range(KT):
                                ins = pe.matmul(bank[i % 4], hT[:, k, t * P:(t + 1) * P], wv[:, k, hf * HALF:(hf + 1) * HALF], start=(k == 0), stop=(k == KT - 1))
                            ins.then_inc(s_m, 1)

                    @block.scalar
                    def _(act):
                        act.wait_ge(s_ch, 3)
                        act.activation(fr[:, 1, :], fr[:, 1, :], ACT.Exp, scale=-1.0).then_inc(s_ch, 1)
                        act.wait_ge(s_ch, 4)
                        act.activation(fr[:, 1, :], fr[:, 1, :], ACT.Ln, bias=1.0).then_inc(s_ch, 1)
                        for i in range(2 * TT):
                            t, hf = divmod(i, 2)
                            act.wait_ge(s_m, i + 1)
                            act.activation(vtok[:, t, hf * HALF:(hf + 1) * HALF], bank[i % 4], ACT.Copy).then_inc(s_c, 1)

                    @block.vector
                    def _(dve):
                        dve.wait_ge(s_wf, 32)
                        for hf in range(2):
                            dve.wait_ge(s_f, hf + 1)
                            dve.tensor_scalar(fr[:, 0, hf * HALF:(hf + 1) * HALF], bank[4 + hf][0:HF, :], fb[:], None, ALU.add).then_inc(s_ch, 1)
                        dve.wait_ge(s_ch, 2)
                        dve.scalar_tensor_tensor(fr[:, 1, :], fr[:, 0, :], -1.0, fr[:, 0, :], ALU.mult, ALU.max).then_inc(s_ch, 1)
                        dve.wait_ge(s_ch, 5)
                        dve.scalar_tensor_tensor(fr[:, 2, :], fr[:, 0, :], 0.0, fr[:, 1, :], ALU.min, ALU.subtract).then_inc(s_ch, 1)
                        dve.wait_ge(s_ch, 6)
                        dve.tensor_scalar(fr[:, 0, :], fr[:, 2, :], -1.0, None, ALU.mult).then_inc(s_f, 1)
                        dve.wait_ge(s_f, 3)
                        dve.tensor_tensor_scan(fr[:, 1, :], fr[:, 0, :], fr[:, 0, :], 0.0, ALU.add, ALU.bypass).then_inc(s_ch, 1)

            with ExitStack() as c2:
                wqk = sbuf(c2, "w_query_key", [P, 2, KT, P])
                qp = sbuf(c2, "q_padded", [P, 2, S])
                kT = sbuf(c2, "kT_pair", [P, S])
                vp = sbuf(c2, "v_pair", [P, TT, P])
                sq = sbuf(c2, "qk_square", [P, 4, HALF])
                nf = sbuf(c2, "minus_F", [P, 2, S])
                nfd = sbuf(c2, "minus_F_masked", [P, 2, S])
                lg = sbuf(c2, "probs", [P, 2, S])
                pT = sbuf(c2, "probsT", [P, 2, TT, P])
                bd = sbuf(c2, "head_mean", [P, P])
                cm = sbuf(c2, "causal_rows", [P, P])
                gq = sbuf(c2, "qk_gain", [P, 2])
                gqs = sbuf(c2, "q_gain_scaled", [P, 1])
                epc = sbuf(c2, "eps_col", [P, 1])
                mx = sbuf(c2, "row_max", [P, 2, 4])
                rsum = sbuf(c2, "row_sum", [P, 2, 2])
                NQ = 2 * TT
                names = ("weights", "minusf", "gain", "consts", "proj", "square", "mean", "root", "recip", "qkT", "masked", "vpair",
                         "logits", "max", "negmax", "exp", "turn", "turned0", "turned1", "pv", "out", "recsum")
                (s_w, s_nf, s_g, s_c, s_pj, s_sq, s_mn, s_rt, s_rc, s_qk, s_nfd, s_vp,
                 s_lg, s_mx, s_nm, s_ex, s_t, s_e0, s_e1, s_pv, s_o, s_rs) = [sem("a_" + n) for n in names]
                s_m1, s_own, s_own2 = sem("a_max1"), sem("a_carrier"), sem("a_carrier2")
                with nc.Block() as block:
                    @block.sync
                    def _(sp):
                        sp.dma_start(gq[0:DH, 0:1], a["fox_q_norm_2"][0].rearrange("(d o) -> d o", o=1)).then_inc(s_g, 16)
                        sp.dma_start(gq[DH:P, 0:1], a["fox_q_norm_2"][0].rearrange("(d o) -> d o", o=1)).then_inc(s_g, 16)
                        sp.dma_start(gq[0:DH, 1:2], a["fox_k_norm_2"][0].rearrange("(d o) -> d o", o=1)).then_inc(s_g, 16)
                        sp.dma_start(gq[DH:P, 1:2], a["fox_k_norm_2"][0].rearrange("(d o) -> d o", o=1)).then_inc(s_g, 16)
                        with sp.Fori(0, PAIRS) as i:
                            sp.wait_ge(s_pj, i * 4 + 1)
                            sp.sem_inc(s_own2, 1)
                            for g in range(2):
                                sp.dma_start(wqk[:, g], w_pk[:, :, bass.ds(i * P + g * D, P)]).then_inc(s_w, 16)
                            sp.wait_ge(s_mx, i * NQ + 1)
                            sp.sem_inc(s_own2, 1)
                            sp.wait_ge(s_nfd, i + 1)
                            sp.sem_inc(s_own2, 1)
                            for g in range(2):
                                sp.dma_start(nf[:, g, :], negf_dram[bass.ds(i * 2 + g, 1), :].to_broadcast([P, S])).then_inc(s_nf, 16)

                    @block.gpsimd
                    def _(pool):
                        pool.memset(bd[:], 0.0).then_inc(s_c, 1)
                        pool.memset(cm[:], 0.0).then_inc(s_c, 1)
                        pool.memset(qp[:], 0.0).then_inc(s_c, 1)
                        pool.memset(epc[:], EPS).then_inc(s_c, 1)
                        pool.wait_ge(s_c, 4)
                        pool.memset(bd[0:DH, 0:DH], 1.0 / DH).then_inc(s_c, 1)
                        pool.memset(bd[DH:P, DH:P], 1.0 / DH).then_inc(s_c, 1)
                        pool.wait_ge(s_c, 6)
                        pool.affine_select(out=cm[:], in_=cm[:], compare_op=ALU.is_ge, fill=NEG, base=0,
                                           pattern=[[-1, P]], channel_multiplier=1).then_inc(s_c, 1)
                        pool.wait_ge(s_c, 7)
                        pool.sem_inc(s_nfd, 1)
                        with pool.Fori(0, PAIRS) as i:
                            pool.wait_ge(s_pv, i * NQ + 1)
                            pool.tensor_copy(vp[:], vtok[:, :, bass.ds(i * P, P)]).then_inc(s_vp, 1)
                            pool.wait_ge(s_nf, i * 32 + 32)
                            pool.wait_ge(s_mx, i * NQ + 1)
                            pool.tensor_tensor(nfd[:].rearrange("p g (t s) -> p (g t) s", s=P), nf[:].rearrange("p g (t s) -> p (g t) s", s=P),
                                               cm[:].unsqueeze(1).to_broadcast([P, 2 * TT, P]), ALU.add).then_inc(s_nfd, 1)

                    @block.tensor
                    def _(pe):
                        pe.sem_inc(s_pj, 1)
                        pe.sem_inc(s_pv, 1)
                        pe.wait_ge(s_c, 7)
                        with pe.Fori(0, PAIRS) as i:
                            pe.wait_ge(s_w, i * 32 + 32)
                            pe.wait_ge(s_mx, i * NQ + 1)
                            for g in range(4):
                                for k in range(KT):
                                    ins = pe.matmul(bank[g], wqk[:, g // 2, k, :], hT[:, k, (g % 2) * HALF:(g % 2 + 1) * HALF], start=(k == 0), stop=(k == KT - 1))
                                ins.then_inc(s_pj, 1)
                                if g == 0:
                                    pe.wait_ge(s_e0, i * NQ + 1)
                                    pe.wait_ge(s_e1, i * TT + 1)
                                    pe.wait_ge(s_o, i * NQ + 1)
                                else:
                                    pe.wait_ge(s_sq, i * 4 + g)
                                    pe.matmul(bank[4 + g - 1], bd[:], sq[:, g - 1, :], start=True, stop=True).then_inc(s_mn, 1)
                            pe.wait_ge(s_sq, i * 4 + 4)
                            pe.matmul(bank[7], bd[:], sq[:, 3, :], start=True, stop=True).then_inc(s_mn, 1)
                            pe.wait_ge(s_qk, i * 4 + 4)
                            pe.wait_ge(s_rt, i * 4 + 4)

                            def logits(j):
                                h, t = divmod(j, TT)
                                b = 2 * (j % 2)
                                if j >= 2:
                                    pe.wait_ge(s_mx, i * NQ + j)
                                w = (t + 1) * P
                                for c in range(0, w, HALF):
                                    n = min(HALF, w - c)
                                    ins = pe.matmul(bank[b + c // HALF][:, 0:n], qp[:, h, t * P:(t + 1) * P], kT[:, c:c + n], start=True, stop=True)
                                ins.then_inc(s_lg, 1)

                            def turn(j):
                                h, t = divmod(j, TT)
                                pe.wait_ge(s_ex, i * NQ + j + 1)
                                pe.wait_ge(s_e0, i * NQ + j + 1)
                                for s in range(min(4, t + 1)):
                                    ins = pe.transpose(bank[4][:, s * P:(s + 1) * P], lg[:, j % 2, s * P:(s + 1) * P], ident[:])
                                ins.then_inc(s_t, 1)
                                if t >= 4:
                                    pe.wait_ge(s_e1, i * TT + 4 * h + t - 4 + 1)
                                    for s in range(4, t + 1):
                                        ins = pe.transpose(bank[5][:, (s - 4) * P:(s - 3) * P], lg[:, j % 2, s * P:(s + 1) * P], ident[:])
                                    ins.then_inc(s_t, 1)

                            def values(j):
                                h, t = divmod(j, TT)
                                if j == 0:
                                    pe.wait_ge(s_vp, i + 1)
                                pe.wait_ge(s_e0, i * NQ + j + 2)
                                if t >= 4:
                                    pe.wait_ge(s_e1, i * TT + 4 * h + t - 4 + 2)
                                pe.wait_ge(s_o, i * NQ + j)  if j >= 2 else None
                                for s in range(t + 1):
                                    ins = pe.matmul(bank[6 + j % 2][:, 0:DH], pT[:, j % 2, s, :], vp[:, s, h * DH:(h + 1) * DH], start=(s == 0), stop=(s == t))
                                ins.then_inc(s_pv, 1)

                            logits(0)
                            for j in range(NQ):
                                if j + 1 < NQ:
                                    logits(j + 1)
                                if j >= 1:
                                    values(j - 1)
                                turn(j)
                            values(NQ - 1)

                    @block.scalar
                    def _(act):
                        act.sem_inc(s_e0, 1)
                        act.wait_ge(s_c, 7)
                        with act.Fori(0, PAIRS) as i:
                            for g in range(4):
                                act.wait_ge(s_pj, i * 4 + g + 2)
                                act.activation(sq[:, g, :], bank[g], ACT.Square).then_inc(s_sq, 1)
                            for g in range(4):
                                act.wait_ge(s_mn, i * 4 + g + 1)
                                act.activation(sq[:, g, :], bank[4 + g], ACT.Sqrt, bias=epc[:]).then_inc(s_rt, 1)

                            def probs(j):
                                h, t = divmod(j, TT)
                                act.wait_ge(s_nm, i * NQ + j + 1)
                                act.wait_ge(s_rs, i * NQ + j + 1)
                                act.activation(lg[:, j % 2, 0:(t + 1) * P], lg[:, j % 2, 0:(t + 1) * P], ACT.Exp, bias=mx[:, j % 2, 2:3],
                                               accum_out=rsum[:, j % 2, 0:1]).then_inc(s_ex, 1)

                            def copy0(j):
                                h, t = divmod(j, TT)
                                act.wait_ge(s_t, i * (NQ + TT) + j + 4 * h + max(0, t - 4) + 1)
                                if j >= 2:
                                    act.wait_ge(s_pv, i * NQ + j)
                                n = min(4, t + 1)
                                act.activation(pT[:, j % 2, 0:n, :], bank[4][:, 0:n * P].rearrange("p (s t) -> p s t", t=P), ACT.Copy).then_inc(s_e0, 1)

                            for j in range(NQ):
                                probs(j)
                                if j >= 1:
                                    copy0(j - 1)
                            copy0(NQ - 1)

                    @block.vector
                    def _(dve):
                        dve.wait_ge(s_g, 64)
                        dve.tensor_scalar(gqs[:], gq[:, 0:1], DH ** -0.5, None, ALU.mult).then_inc(s_rs, 1)
                        dve.wait_ge(s_rs, 1)
                        dve.sem_inc(s_rs, 1)
                        dve.sem_inc(s_mx, 1)
                        dve.sem_inc(s_e1, 1)
                        dve.sem_inc(s_o, 1)
                        with dve.Fori(0, PAIRS) as i:
                            for g in range(4):
                                dve.wait_ge(s_rt, i * 4 + g + 1)
                                dve.reciprocal(sq[:, g, :], sq[:, g, :]).then_inc(s_rc, 1)
                                dve.wait_ge(s_rc, i * 4 + g + 1)
                                at = slice((g % 2) * HALF, (g % 2 + 1) * HALF)
                                if g < 2:
                                    dve.scalar_tensor_tensor(qp[0:DH, 0, at], bank[g][0:DH, :], gqs[0:DH], sq[0:DH, g, :], ALU.mult, ALU.mult)
                                    ins = dve.scalar_tensor_tensor(qp[DH:P, 1, at], bank[g][DH:P, :], gqs[DH:P], sq[DH:P, g, :], ALU.mult, ALU.mult)
                                else:
                                    ins = dve.scalar_tensor_tensor(kT[:, at], bank[g], gq[:, 1:2], sq[:, g, :], ALU.mult, ALU.mult)
                                ins.then_inc(s_qk, 1)
                            dve.wait_ge(s_nf, i * 32 + 32)
                            dve.wait_ge(s_nfd, i + 2)

                            def row_max(j):
                                h, t = divmod(j, TT)
                                b = 2 * (j % 2)
                                at = t * P
                                dve.wait_ge(s_lg, i * NQ + j + 1)
                                if j >= 2:
                                    dve.wait_ge(s_t, i * (NQ + TT) + (j - 1) + 4 * ((j - 2) // TT) + max(0, (j - 2) % TT - 3))
                                dve.sem_inc(s_own, 1)
                                row = psum[:, b:b + 2, :].rearrange("p b n -> p (b n)")
                                if t > 0:
                                    dve.tensor_tensor_reduce(lg[:, j % 2, 0:at], row[:, 0:at], nf[:, h, 0:at], 1.0, NEG, ALU.add, ALU.max, mx[:, j % 2, 0:1])
                                dve.tensor_tensor_reduce(lg[:, j % 2, at:at + P], row[:, at:at + P], nfd[:, h, at:at + P], 1.0,
                                                         NEG, ALU.add, ALU.max, mx[:, j % 2, 1:2]).then_inc(s_mx, 1)
                                dve.wait_ge(s_mx, i * NQ + j + 2)
                                if t > 0:
                                    dve.tensor_tensor(mx[:, j % 2, 3:4], mx[:, j % 2, 0:1], mx[:, j % 2, 1:2], ALU.max).then_inc(s_m1, 1)
                                    dve.wait_ge(s_m1, i * (NQ - 2) + j - h)
                                dve.tensor_scalar(mx[:, j % 2, 2:3], mx[:, j % 2, 3:4] if t > 0 else mx[:, j % 2, 1:2], -1.0, None, ALU.mult).then_inc(s_nm, 1)

                            def copy1(j):
                                h, t = divmod(j, TT)
                                if t >= 4:
                                    dve.wait_ge(s_t, i * (NQ + TT) + j + 4 * h + t - 4 + 2)
                                    if j >= 2:
                                        dve.wait_ge(s_pv, i * NQ + j)
                                    n = t - 3
                                    dve.tensor_copy(pT[:, j % 2, 4:4 + n, :], bank[5][:, 0:n * P].rearrange("p (s t) -> p s t", t=P)).then_inc(s_e1, 1)

                            def leave(j):
                                h, t = divmod(j, TT)
                                dve.wait_ge(s_ex, i * NQ + j + 1)
                                dve.reciprocal(rsum[:, j % 2, 1:2], rsum[:, j % 2, 0:1]).then_inc(s_rs, 1)
                                dve.wait_ge(s_rs, i * NQ + j + 3)
                                dve.wait_ge(s_pv, i * NQ + j + 2)
                                dve.tensor_scalar(x3[:, t, bass.ds(i * P + h * DH, DH)], bank[6 + j % 2][:, 0:DH], rsum[:, j % 2, 1:2], None, ALU.mult).then_inc(s_o, 1)

                            row_max(0)
                            for j in range(NQ):
                                if j + 1 < NQ:
                                    row_max(j + 1)
                                if j >= 1:
                                    leave(j - 1)
                                copy1(j)
                            leave(NQ - 1)

        with ExitStack() as c2:
            oT = hT
            wo = sbuf(c2, "fox_w_out", [P, KT, D])
            mix = sbuf(c2, "fox_mix", [P, 2, HALF])
            s_w, s_x, s_t, s_c, s_m, s_g, s_r = [sem("p_" + n) for n in ("weights", "x2", "turned", "copied", "mm", "gated", "residual")]
            with nc.Block() as block:
                @block.sync
                def _(sp):
                    sp.dma_start(wo[:], a["fox_w_out_2"][0].rearrange("(p k) n -> p k n", k=KT)).then_inc(s_w, 16)
                    sp.wait_ge(s_t, 2 * TT)
                    sp.dma_start(x3[:], x2_dram.rearrange("(t p) n -> p t n", p=P)).then_inc(s_x, 16)

                @block.tensor
                def _(pe):
                    for t in range(TT):
                        for g in range(2):
                            if t >= 2:
                                pe.wait_ge(s_c, 2 * (t - 2) + g + 1)
                            for k in range(4 * g, 4 * g + 4):
                                ins = pe.transpose(bank[g + 2 * (t % 2)][:, (k % 4) * P:(k % 4 + 1) * P], x3[:, t, k:D:KT], ident[:])
                            ins.then_inc(s_t, 1)
                    pe.wait_ge(s_c, 2 * TT)
                    pe.wait_ge(s_w, 16)
                    for i in range(2 * TT):
                        t, hf = divmod(i, 2)
                        if i >= 4:
                            pe.wait_ge(s_g, i - 3)
                        for k in range(KT):
                            ins = pe.matmul(bank[4 + i % 4], oT[:, k, t * P:(t + 1) * P], wo[:, k, hf * HALF:(hf + 1) * HALF], start=(k == 0), stop=(k == KT - 1))
                        ins.then_inc(s_m, 1)

                @block.vector
                def _(dve):
                    for t in range(TT):
                        for g in range(2):
                            dve.wait_ge(s_t, 2 * t + g + 1)
                            dve.tensor_copy(oT[:, 4 * g:4 * g + 4, t * P:(t + 1) * P],
                                            bank[g + 2 * (t % 2)].rearrange("p (k t) -> p k t", t=P)).then_inc(s_c, 1)
                    dve.wait_ge(s_x, 16)
                    for i in range(2 * TT):
                        t, hf = divmod(i, 2)
                        at = slice(hf * HALF, (hf + 1) * HALF)
                        dve.wait_ge(s_m, i + 1)
                        dve.tensor_tensor(mix[:, i % 2, :], bank[4 + i % 4], gates[:, 2, at], ALU.mult).then_inc(s_g, 1)
                        dve.wait_ge(s_g, i + 1)
                        dve.tensor_tensor(x3[:, t, at], x3[:, t, at], mix[:, i % 2, :], ALU.add).then_inc(s_r, 1)


def mlp(nc, a, sbuf, sem, bank, ident, ones, mhalf, gates, colmod, x3, hT, out):
    with ExitStack() as c2:
        with ExitStack() as c3:
            norm_turn(nc, c3, "n", sbuf, sem, bank, ident, mhalf, colmod[:, 1, 3, :], colmod[:, 1, 2, :], hT, x3, None)
        w1 = sbuf(c2, "w_mlp_in", [P, 2, KT, HALF])
        w2 = sbuf(c2, "w_mlp_out", [P, 2, 4, D])
        gT = sbuf(c2, "hiddenT", [P, 2, 4, S])
        tmp = sbuf(c2, "mlp_gated", [P, 2, HALF])
        s_own = sem("h_carrier")
        l1 = [sem("h_w1_0"), sem("h_w1_1")]
        l2 = [sem("h_w2_0"), sem("h_w2_1")]
        s_h, s_a, s_o, s_g, s_r, s_r2, s_out = [sem("h_" + n) for n in ("hidden", "relu2", "out", "gated", "residual", "relu", "stored")]
        w1_d = a["w_mlp_in_2"][0].rearrange("(p k) n -> p k n", k=KT)
        w2_d = a["w_mlp_out_2"][0].rearrange("(f p) n -> p f n", p=P)
        NO = 2 * TT
        with nc.Block() as block:
            @block.sync
            def _(sp):
                with sp.Fori(0, FB // 2) as i:
                    for u in range(2):
                        sp.wait_ge(s_h, i * 16 + 8 * u + 1)
                        sp.sem_inc(s_own, 1)
                        sp.dma_start(w1[:, u], w1_d[:, :, bass.ds(i * 2 * HALF + u * HALF, HALF)]).then_inc(l1[u], 16)
                        sp.wait_ge(s_o, i * 2 * NO + NO * u + 1)
                        sp.sem_inc(s_own, 1)
                        sp.dma_start(w2[:, u], w2_d[:, bass.ds(i * 8 + 4 * u, 4), :]).then_inc(l2[u], 16)
                sp.wait_ge(s_r, FB * NO)
                sp.dma_start(out[0].rearrange("(t p) n -> p t n", p=P), x3[:]).then_inc(s_out, 16)
                sp.wait_ge(s_out, 16)

            @block.tensor
            def _(pe):
                pe.sem_inc(s_h, 9)
                pe.sem_inc(s_o, NO + 1)
                with pe.Fori(0, FB // 2) as i:
                    for u in range(2):
                        pe.wait_ge(l1[u], i * 16 + 16)
                        for n in range(8):
                            m, hf = divmod(n, 2)
                            pe.wait_ge(s_a, i * 16 + 8 * u + n + 1)
                            for k in range(KT):
                                ins = pe.matmul(bank[n % 4], w1[:, u, k, m * P:(m + 1) * P], hT[:, k, hf * HALF:(hf + 1) * HALF], start=(k == 0), stop=(k == KT - 1))
                            ins.then_inc(s_h, 1)
                        pe.wait_ge(l2[u], i * 16 + 16)
                        pe.wait_ge(s_a, i * 16 + 8 * u + 8 + 4)
                        for n in range(NO):
                            t, hf = divmod(n, 2)
                            pe.wait_ge(s_g, i * 2 * NO + NO * u + n + 1)
                            for m in range(4):
                                ins = pe.matmul(bank[4 + n % 4], gT[:, u, m, t * P:(t + 1) * P], w2[:, u, m, hf * HALF:(hf + 1) * HALF], start=(m == 0), stop=(m == 3))
                            ins.then_inc(s_o, 1)

            @block.vector
            def _(dve):
                dve.sem_inc(s_a, 4)
                dve.sem_inc(s_g, 4)
                with dve.Fori(0, FB // 2) as i:
                    for u in range(2):
                        for n in range(8):
                            m, hf = divmod(n, 2)
                            dve.wait_ge(s_h, i * 16 + 8 * u + n + 10)
                            dve.tensor_scalar(tmp[:, n % 2, :], bank[n % 4], 0.0, None, ALU.max).then_inc(s_r2, 1)
                            dve.wait_ge(s_r2, i * 16 + 8 * u + n + 1)
                            dve.tensor_tensor(gT[:, u, m, hf * HALF:(hf + 1) * HALF], tmp[:, n % 2, :], tmp[:, n % 2, :], ALU.mult).then_inc(s_a, 1)
                        for n in range(NO):
                            t, hf = divmod(n, 2)
                            at = slice(hf * HALF, (hf + 1) * HALF)
                            dve.wait_ge(s_o, i * 2 * NO + NO * u + n + NO + 2)
                            dve.tensor_tensor(tmp[:, n % 2, :], bank[4 + n % 4], gates[:, 3, at], ALU.mult).then_inc(s_g, 1)
                            dve.wait_ge(s_g, i * 2 * NO + NO * u + n + 5)
                            dve.tensor_tensor(x3[:, t, at], x3[:, t, at], tmp[:, n % 2, :], ALU.add).then_inc(s_r, 1)


def kernel(**inputs):
    import concourse.bacc as bacc
    import numpy as np
    from concourse.bass_utils import run_bass_kernel_spmd

    nc = bacc.Bacc("TRN2", target_bir_lowering=False, num_devices=1)
    arrays, aps = {}, {}
    for name, value in inputs.items():
        value = np.ascontiguousarray(value)
        if not value.size:
            continue
        arrays["in_" + name] = value
        aps[name] = nc.dram_tensor("in_" + name, value.shape, mybir.dt.from_np(value.dtype), kind="ExternalInput").ap()
    out = nc.dram_tensor("out", [1, S, D], F32, kind="ExternalOutput").ap()
    build(nc, aps, out)
    return run_bass_kernel_spmd(nc, [arrays], core_ids=[0]).results[0]["out"]
```

```python
from contextlib import ExitStack

import concourse.bass as bass
from concourse import mybir

F32 = mybir.dt.float32
F32R = mybir.dt.float32r
I32 = mybir.dt.int32
U32 = mybir.dt.uint32
BF16 = mybir.dt.bfloat16
ALU = mybir.AluOpType
ACT = mybir.ActivationFunctionType
X = mybir.AxisListType.X

P = 128
S = 1024
D = 1024
TT = S // P
KT = D // P
HALF = 512
EPS = 1e-6
ROOT_D = float(D) ** 0.5
NEG = -3.0e38

HM = 4
POOL_PAD = 16
CW = 4

NE = 32
EG = 4
EPG = NE // EG
DE = 512
JT = DE // P
MINB = S * 2 // P
MAXB = S * 2 // P + NE

HF = 16
DH = 64
PAIRS = HF // 2
FF = 4096
FB = FF // HALF


def build(nc, a, out):
    top = ExitStack()
    with top:
        def sbuf(ctx, name, shape, dt=F32):
            return ctx.enter_context(nc.sbuf_tensor(name, shape, dt))

        def phase(f, *more):
            sems = []

            def sem(name):
                sems.append(nc.alloc_semaphore(name))
                return sems[-1]

            f(nc, a, sbuf, sem, bank, ident, ones, mhalf, gates, colmod, *more)
            nc.clear_and_free_semaphores(sems)
            nc.all_engine_barrier()

        psum = top.enter_context(nc.psum_tensor("psum", [P, 8, HALF], F32))
        bank = [psum[:, i, :] for i in range(8)]

        ident = sbuf(top, "ident", [P, P])
        ones = sbuf(top, "ones", [P, P])
        gates = sbuf(top, "gates", [P, 4, D])
        colmod = sbuf(top, "colmod", [P, 2, 4, KT])
        mhalf = sbuf(top, "minus_half", [P, 1])

        normed_dram = nc.dram_tensor("normed_rows", [S, D], F32, kind="Internal").ap()
        slots_dram = nc.dram_tensor("slot_tokens", [P * MAXB, 1], I32, kind="Internal").ap()
        moe_dram = nc.dram_tensor("expert_rows", [MAXB * P, D], F32, kind="Internal").ap()
        negf_dram = nc.dram_tensor("minus_log_forget", [HF, S], F32, kind="Internal").ap()
        x2_dram = nc.dram_tensor("second_residual", [S, D], F32, kind="Internal").ap()

        phase(modulation)
        with ExitStack() as xs:
            x1 = sbuf(xs, "x1", [P, TT, D])
            phase(mixer, x1, moe_dram)
            phase(moe, x1, normed_dram, slots_dram, moe_dram, x2_dram)
        with ExitStack() as xs:
            x3 = sbuf(xs, "x3", [P, TT, D])
            phase(attention, psum, x2_dram, negf_dram, x3)
            hTh = sbuf(xs, "hT_high", [P, KT, S], F32R)
            hTl = sbuf(xs, "hT_low", [P, KT, S], F32R)
            phase(mlp, x3, hTh, hTl, out)


def modulation(nc, a, sbuf, sem, bank, ident, ones, mhalf, gates, colmod):
    with ExitStack() as ctx:
        ws = sbuf(ctx, "ada_rows", [P, 2, 6 * D])
        acc = sbuf(ctx, "ada_acc", [P, 2, 6 * D])
        brow = sbuf(ctx, "ada_bias_row", [1, 2, 6 * D])
        ccol = sbuf(ctx, "c_col", [P, 2, KT])
        csil = sbuf(ctx, "c_silu", [P, 2, KT])
        bcol = sbuf(ctx, "ada_bias_col", [P, 2, 6, KT])
        gcol = sbuf(ctx, "norm_gain_col", [P, 2, 2, KT])
        tcol = sbuf(ctx, "mod_col", [P, 2, 4, KT])
        par, row0, row1 = sem("m_params"), sem("m_rows0"), sem("m_rows1")
        rows = [row0, row1]
        csilu, macc, red, modc, modg, idm = (sem("m_silu"), sem("m_acc"), sem("m_reduced"), sem("m_cols"), sem("m_gates"), sem("m_ident"))
        w = [a["ada_w"], a["w_ada_2"]]
        b = [a["ada_b"], a["b_ada_2"]]
        gains = [[a["norm1_g"], a["norm2_g"]], [a["norm_mix_2"], a["norm_mlp_2"]]]
        with nc.Block() as block:
            @block.sync
            def _(sp):
                for l, c in enumerate((a["c"], a["c_2"])):
                    sp.dma_start(ccol[:, l, :], c[0].rearrange("(p k) -> p k", k=KT)).then_inc(par, 16)
                for j in range(2 * KT):
                    l, k = divmod(j, KT)
                    if j >= 2:
                        sp.wait_ge(macc, j - 1)
                    sp.dma_start(ws[:, j % 2, :], w[l][0].rearrange("(p k) n -> p k n", k=KT)[:, k, :]).then_inc(rows[j % 2], 16)

            @block.scalar
            def _(act):
                for l in range(2):
                    act.dma_start(bcol[:, l], b[l][0].rearrange("(q p k) -> p q k", p=P, k=KT)).then_inc(par, 16)
                    act.dma_start(brow[:, l, :], b[l]).then_inc(par, 16)
                    for g in range(2):
                        act.dma_start(gcol[:, l, g, :], gains[l][g][0].rearrange("(p k) -> p k", k=KT)).then_inc(par, 16)
                act.wait_ge(par, 16 * 10)
                act.activation(csil[:], ccol[:], ACT.Silu).then_inc(csilu, 1)

            @block.gpsimd
            def _(pool):
                pool.memset(ident[:], 0.0).then_inc(idm, 1)
                pool.memset(ones[:], 1.0).then_inc(idm, 1)
                pool.memset(mhalf[:], -0.5).then_inc(idm, 1)
                pool.wait_ge(idm, 3)
                pool.affine_select(out=ident[:], in_=ident[:], compare_op=ALU.not_equal, fill=1.0, base=0,
                                   pattern=[[-1, P]], channel_multiplier=1).then_inc(idm, 1)

            @block.vector
            def _(dve):
                dve.wait_ge(csilu, 1)
                for j in range(2 * KT):
                    l, k = divmod(j, KT)
                    dve.wait_ge(rows[j % 2], 16 * (j // 2 + 1))
                    if k == 0:
                        dve.tensor_scalar(acc[:, l, :], ws[:, j % 2, :], csil[:, l, k:k + 1], None, ALU.mult).then_inc(macc, 1)
                    else:
                        dve.wait_ge(macc, j)
                        dve.scalar_tensor_tensor(acc[:, l, :], ws[:, j % 2, :], csil[:, l, k:k + 1], acc[:, l, :],
                                                 ALU.mult, ALU.add).then_inc(macc, 1)
                for l in range(2):
                    dve.wait_ge(red, 5 * l + 1)
                    dve.tensor_tensor(tcol[:, l, 0:2, :], bank[4 + l][:, l * 32:l * 32 + 16].rearrange("p (q k) -> p q k", k=KT),
                                      bcol[:, l, 0:2, :], ALU.add).then_inc(modc, 1)
                    dve.tensor_tensor(tcol[:, l, 2:4, :], bank[4 + l][:, l * 32 + 16:l * 32 + 32].rearrange("p (q k) -> p q k", k=KT),
                                      bcol[:, l, 3:5, :], ALU.add).then_inc(modc, 1)
                    dve.wait_ge(modc, 6 * l + 2)
                    for g in range(2):
                        dve.tensor_copy(colmod[:, l, 2 * g, :], tcol[:, l, 2 * g, :]).then_inc(modc, 1)
                        dve.scalar_tensor_tensor(colmod[:, l, 2 * g + 1, :], tcol[:, l, 2 * g + 1, :], 1.0, gcol[:, l, g, :],
                                                 ALU.add, ALU.mult).then_inc(modc, 1)
                    for n in range(4):
                        dve.wait_ge(red, 5 * l + 2 + n)
                        dve.tensor_copy(gates[:, 2 * l + n // 2, (n % 2) * HALF:(n % 2 + 1) * HALF], bank[n][:]).then_inc(modg, 1)

            @block.tensor
            def _(pe):
                pe.wait_ge(idm, 4)
                pe.wait_ge(par, 16 * 10)
                for l in range(2):
                    pe.wait_ge(macc, KT * (l + 1))
                    for qi, q in enumerate((0, 1, 3, 4)):
                        for k in range(KT):
                            m = pe.matmul(bank[4 + l][:, l * 32 + qi * KT + k:l * 32 + qi * KT + k + 1],
                                          acc[:, l, q * D + k:(q + 1) * D:KT], ones[:, 0:1], start=True, stop=True)
                    m.then_inc(red, 1)
                    for n in range(4):
                        if l == 1:
                            pe.wait_ge(modg, n + 1)
                        at = (2 + 3 * (n // 2)) * D + (n % 2) * HALF
                        pe.matmul(bank[n][:], ones[:], acc[:, l, at:at + HALF], start=True, stop=False)
                        pe.matmul(bank[n][:], ones[0:1, :], brow[:, l, at:at + HALF], start=False, stop=True).then_inc(red, 1)


def mixer(nc, a, sbuf, sem, bank, ident, ones, mhalf, gates, colmod, x1, moe_dram):
    w_in = a["w_in"][0]
    w_in_pk = w_in.rearrange("(p k) n -> p k n", k=KT)
    DM = HM * P
    with ExitStack() as ctx:
        ucT = sbuf(ctx, "ucT", [P, HM, S])
        sgo = sbuf(ctx, "sigmoid_oT", [P, HM, S])
        vaug = sbuf(ctx, "v_aug", [P, TT, HM, P + 1])
        yT = sbuf(ctx, "yT", [P, 2 * HM, S])
        prow = sbuf(ctx, "param_rows", [36, P])
        pcol = sbuf(ctx, "param_cols", [P, 36])
        zrow = x1[0:HM, 6:8, :]
        bif = sbuf(ctx, "gate_bias", [HM, 2])
        par = sem("x_params")
        with ExitStack() as c2:
            hT = sbuf(c2, "hT", [P, KT, S])
            wb = sbuf(c2, "w_in_block", [P, 2, KT, HALF])
            wg = sbuf(c2, "w_in_gates", [P, KT, 36])
            wgl = sbuf(c2, "w_in_gates_loaded", [P, KT, 8])
            uT = yT[:, 0:HM, :]
            pp = yT[:, HM:2 * HM, :]
            stat = sbuf(c2, "stat", [P, TT, 2])
            xn = ucT[:, 0:2, :]
            sq = ucT[:, 2, :]
            xl, xs, nr, tr, hv = [sem("x_load0"), sem("x_load1")], sem("x_square"), sem("x_normed"), sem("x_turned"), sem("x_hT")
            xst, xse = sem("x_stat"), sem("x_eps")
            wl = [sem("x_w0"), sem("x_w1")]
            wgd, mm, ev, z, cv, padz = sem("x_wgates"), sem("x_proj"), sem("x_evac"), sem("x_zero"), sem("x_conv"), sem("x_padz")
            pc = sem("x_pcol")
            cols = [0, 2 * DM, 4 * 128 * 3 + 8, DM]
            with nc.Block() as block:
                @block.sync
                def _(sp):
                    for t in range(TT):
                        if t >= 2:
                            sp.wait_ge(nr, t - 1)
                        sp.dma_start(x1[:, t, :], a["x"][0, t * P:(t + 1) * P, :]).then_inc(xl[t % 2], 16)
                    for n in range(4):
                        if n >= 2:
                            sp.wait_ge(mm, 8 * (n - 1))
                        sp.dma_start(wb[:, n % 2], w_in_pk[:, :, cols[n]:cols[n] + HALF]).then_inc(wl[n % 2], 16)

                @block.gpsimd
                def _(pool):
                    for t in range(TT):
                        pool.wait_ge(xs, t + 1)
                        pool.tensor_scalar(stat[:, t, 0:1], stat[:, t, 0:1], D * EPS, None, ALU.add).then_inc(xse, 1)
                        pool.wait_ge(xse, t + 1)
                        pool.tensor_tensor(stat[:, t, 1:2], stat[:, t, 0:1], mhalf[:], ALU.pow).then_inc(xst, 1)
                    pool.memset(wg[:], 0.0).then_inc(z, 1)
                    pool.memset(vaug[:, :, :, P:P + 1], 1.0).then_inc(z, 1)
                    pool.wait_ge(wgd, 16)
                    pool.wait_ge(z, 2)
                    pool.tensor_copy(wg[:, :, 0:HM], wgl[:, :, 0:HM]).then_inc(z, 1)
                    pool.tensor_copy(wg[:, :, 32:32 + HM], wgl[:, :, HM:2 * HM]).then_inc(z, 1)

                @block.scalar
                def _(act):
                    act.dma_start(prow[0:16, :], a["conv_w"][0].rearrange("w (t p) -> (w t) p", p=P)).then_inc(par, 16)
                    for n, name in enumerate(("conv_b", "mlstm_norm_g", "mlstm_skip", "b_pool", "pool_scale")):
                        act.dma_start(prow[16 + 4 * n:20 + 4 * n, :], a[name][0].rearrange("(t p) -> t p", p=P)).then_inc(par, 16)
                    act.dma_start(bif[:, 0:1], a["b_igate"][0].rearrange("(h o) -> h o", o=1)).then_inc(par, 16)
                    act.dma_start(bif[:, 1:2], a["b_fgate"][0].rearrange("(h o) -> h o", o=1)).then_inc(par, 16)
                    act.dma_start(wgl[:], w_in_pk[:, :, 3 * DM:3 * DM + 8]).then_inc(wgd, 16)
                    for t in range(TT):
                        act.wait_ge(xl[t % 2], 16 * (t // 2 + 1))
                        if t >= 1:
                            act.wait_ge(xs, t)
                        act.activation(sq, x1[:, t, :], ACT.Square, accum_out=stat[:, t, 0:1]).then_inc(xs, 1)
                    for n in range(4):
                        for i in range(8):
                            act.wait_ge(mm, 8 * n + i + 1)
                            src = bank[2 + (8 * n + i) % 4][:]
                            m, hf = divmod(i, 2)
                            if n == 0:
                                ins = act.activation(uT[:, m, hf * HALF:(hf + 1) * HALF], src, ACT.Copy)
                            elif n == 1:
                                ins = act.activation(sgo[:, m, hf * HALF:(hf + 1) * HALF], src, ACT.Sigmoid)
                            elif n == 2:
                                ins = act.activation(pp[:, m, hf * HALF:(hf + 1) * HALF], src, ACT.Copy)
                            else:
                                ins = act.activation(vaug[:, i, :, 0:P], src.rearrange("p (h e) -> p h e", h=HM), ACT.Copy)
                            ins.then_inc(ev, 1)
                    act.wait_ge(par, 16 * 8)
                    for hf in range(2):
                        act.wait_ge(mm, 33 + hf)
                        for g in range(2):
                            act.activation(zrow[:, g, hf * HALF:(hf + 1) * HALF], bank[hf][32 * g:32 * g + HM, :], ACT.Identity,
                                           bias=bif[:, g:g + 1]).then_inc(ev, 1)
                    for m in range(HM):
                        act.wait_ge(cv, 4 * (m + 1))
                        act.activation(ucT[:, m, :], ucT[:, m, :], ACT.Silu, bias=pcol[:, 16 + m:17 + m]).then_inc(ev, 1)

                @block.vector
                def _(dve):
                    for t in range(TT):
                        dve.wait_ge(xst, t + 1)
                        if t >= 2:
                            dve.wait_ge(tr, 2 * (t - 1))
                        dve.tensor_scalar(xn[:, t % 2, :], x1[:, t, :], stat[:, t, 1:2], ROOT_D, ALU.mult, ALU.mult).then_inc(nr, 1)
                        for g in range(2):
                            dve.wait_ge(tr, 2 * t + g + 1)
                            for k in range(4 * g, 4 * g + 4):
                                ins = dve.tensor_scalar(hT[:, k, t * P:(t + 1) * P], bank[g][:, (k % 4) * P:(k % 4 + 1) * P],
                                                        colmod[:, 0, 1, k:k + 1], colmod[:, 0, 0, k:k + 1], ALU.mult, ALU.add)
                            ins.then_inc(hv, 1)
                    dve.wait_ge(pc, 1)
                    dve.tensor_copy(pcol[:], bank[6][:, 0:36]).then_inc(pc, 1)
                    dve.wait_ge(pc, 2)
                    dve.wait_ge(ev, 8)
                    for m in range(HM):
                        for j in range(CW):
                            src = uT[:, m, 0:S - j]
                            tap = pcol[:, 4 * (CW - 1 - j) + m:4 * (CW - 1 - j) + m + 1]
                            if j == 0:
                                dve.tensor_scalar(ucT[:, m, :], src, tap, None, ALU.mult).then_inc(cv, 1)
                            else:
                                dve.wait_ge(cv, 4 * m + j)
                                dve.scalar_tensor_tensor(ucT[:, m, j:], src, tap, ucT[:, m, j:], ALU.mult, ALU.add).then_inc(cv, 1)

                @block.tensor
                def _(pe):
                    for t in range(TT):
                        pe.wait_ge(nr, t + 1)
                        for g in range(2):
                            if t >= 1:
                                pe.wait_ge(hv, 2 * (t - 1) + g + 1)
                            for k in range(4 * g, 4 * g + 4):
                                ins = pe.transpose(bank[g][:, (k % 4) * P:(k % 4 + 1) * P], xn[:, t % 2, k:D:KT], ident[:])
                            ins.then_inc(tr, 1)
                    pe.wait_ge(hv, 2 * TT)
                    pe.wait_ge(par, 16 * 8)
                    pe.transpose(bank[6][:, 0:36], prow[:], ident[0:36, 0:36]).then_inc(pc, 1)
                    for n in range(4):
                        pe.wait_ge(wl[n % 2], 16 * (n // 2 + 1))
                        for i in range(8):
                            g = 8 * n + i
                            if g >= 4:
                                pe.wait_ge(ev, g - 3)
                            m, hf = divmod(i, 2)
                            for k in range(KT):
                                if n < 3:
                                    ins = pe.matmul(bank[2 + g % 4][:], wb[:, n % 2, k, m * P:(m + 1) * P], hT[:, k, hf * HALF:(hf + 1) * HALF],
                                                    start=(k == 0), stop=(k == KT - 1))
                                else:
                                    ins = pe.matmul(bank[2 + g % 4][:], hT[:, k, i * P:(i + 1) * P], wb[:, n % 2, k, :],
                                                    start=(k == 0), stop=(k == KT - 1))
                            ins.then_inc(mm, 1)
                    pe.wait_ge(z, 4)
                    for hf in range(2):
                        for k in range(KT):
                            ins = pe.matmul(bank[hf][0:36, :], wg[:, k, :], hT[:, k, hf * HALF:(hf + 1) * HALF], start=(k == 0), stop=(k == KT - 1))
                        ins.then_inc(mm, 1)

        NC_ = TT
        with ExitStack() as c2:
            qT = sbuf(c2, "qT", [P, HM, S])
            kT = sbuf(c2, "kT", [P, HM, S])
            ktok = sbuf(c2, "k_tok", [P, TT, HM, P])
            wq = sbuf(c2, "wq", [P, HM, P])
            wk = sbuf(c2, "wk", [P, HM, P])
            wp = sbuf(c2, "wpool", [P, HM, P])
            rr = x1[0:HM, 0:6, :]
            negM = rr[:, 1, :]
            packed = sbuf(c2, "packed_rows", [P, S])
            pk = sbuf(c2, "packed_cols", [P, TT, P])
            mprev = sbuf(c2, "m_prev", [HM, NC_])
            aprev = sbuf(c2, "a_prev", [HM, NC_])
            aprb = sbuf(c2, "a_prev_all", [P, HM, NC_])
            sel = sbuf(c2, "select_head", [HM, HM, P])
            NM = x1[:, 2:6, :]
            cmask = sbuf(c2, "causal", [P, P])
            state = sbuf(c2, "state", [P, HM, P + 1])
            lw = sem("c_w")
            rw = sem("c_rows")
            rdy = sem("c_ready")
            q1, q2 = sem("c_qk"), sem("c_qkev")
            g1, g2 = sem("c_setup"), sem("c_setup_done")
            pl = sem("c_pool")
            pm, pe_v = sem("c_poolmm"), sem("c_poolev")
            rowexp = sem("c_rowexp")
            with ExitStack() as c3:
                ps2 = sbuf(c3, "pool_sums", [P, 2, POOL_PAD + S])
                fix = sbuf(c3, "pool_fix", [P, HM, 16])
                with nc.Block() as block:
                    @block.sync
                    def _(sp):
                        sp.dma_start(wq[:], a["w_q"][0].rearrange("h d e -> d h e")).then_inc(lw, 16)
                        sp.dma_start(wk[:], a["w_k"][0].rearrange("h d e -> d h e")).then_inc(lw, 16)
                        sp.dma_start(wp[:], a["w_pool"][0].rearrange("g c d -> c g d")).then_inc(lw, 16)

                    @block.tensor
                    def _(pe):
                        pe.wait_ge(lw, 48)
                        n = 0
                        for h in range(HM):
                            for w_, in ((wq,), (wk,)):
                                for hf in range(2):
                                    if n >= 4:
                                        pe.wait_ge(q2, n - 3)
                                    pe.matmul(bank[n % 4][:], w_[:, h, :], ucT[:, h, hf * HALF:(hf + 1) * HALF], start=True, stop=True).then_inc(q1, 1)
                                    n += 1
                        for t in range(TT):
                            pe.wait_ge(q2, n - 3)
                            for h in range(HM):
                                ins = pe.matmul(bank[n % 4][:, h * P:(h + 1) * P], ucT[:, h, t * P:(t + 1) * P], wk[:, h, :], start=True, stop=True)
                            ins.then_inc(q1, 1)
                            n += 1
                        pe.wait_ge(g1, 8)
                        for t in range(TT):
                            if t in (4,):
                                pe.wait_ge(g2, 1)
                            ins = pe.transpose(bank[4][:, (t % 4) * P:(t % 4 + 1) * P], packed[:, t * P:(t + 1) * P], ident[:])
                            if t % 4 == 3:
                                ins.then_inc(rdy, 1)
                        pe.wait_ge(g1, 9)
                        for h in range(HM):
                            ins = pe.matmul(bank[5][:, h * NC_:(h + 1) * NC_], sel[:, h, :], aprev[:], start=True, stop=True)
                        ins.then_inc(rdy, 1)
                        n = 0
                        for h in range(HM):
                            for hf in range(2):
                                if n >= 2:
                                    pe.wait_ge(g2, 3 + n - 1)
                                pe.matmul(bank[6 + n % 2][:], sel[:, h, :], negM[:, hf * HALF:(hf + 1) * HALF], start=True, stop=True).then_inc(rdy, 1)
                                n += 1
                        pe.wait_ge(q2, 24)
                        for g in range(HM):
                            pe.wait_ge(pl, g + 1)
                            for hf in range(2):
                                if g >= 1:
                                    pe.wait_ge(pe_v, 2 * (g - 1) + hf + 1)
                                pe.matmul(bank[2 + hf][:], wp[:, g, :], yT[:, HM + g, hf * HALF:(hf + 1) * HALF], start=True, stop=True).then_inc(pm, 1)

                    @block.gpsimd
                    def _(pool):
                        pool.memset(packed[:], 0.0).then_inc(rw, 1)
                        pool.memset(rr[:, 5, :], 1.0).then_inc(rw, 1)
                        pool.memset(sel[:], 0.0).then_inc(rw, 1)
                        pool.memset(cmask[:], 0.0).then_inc(rw, 1)
                        pool.memset(mprev[:], 0.0).then_inc(rw, 1)
                        pool.memset(ps2[:, :, 0:POOL_PAD], 0.0).then_inc(rw, 1)
                        pool.iota(fix[:], [[0, HM], [1, 16]], base=1, channel_multiplier=0, allow_small_or_imprecise_dtypes=True).then_inc(rw, 1)
                        pool.wait_ge(rw, 7)
                        pool.memset(rr[:, 5, 0:S:P], 0.0).then_inc(rw, 1)
                        pool.affine_select(out=sel[:], in_=sel[:], compare_op=ALU.not_equal, fill=1.0, base=0,
                                           pattern=[[-1, HM], [0, P]], channel_multiplier=1).then_inc(rw, 1)
                        pool.affine_select(out=cmask[:], in_=cmask[:], compare_op=ALU.is_ge, fill=NEG, base=0,
                                           pattern=[[1, P]], channel_multiplier=-1).then_inc(rw, 1)

                    @block.scalar
                    def _(act):
                        n = 0
                        for h in range(HM):
                            for dst, sc in ((qT, P ** -0.5), (kT, 1.0)):
                                for hf in range(2):
                                    act.wait_ge(q1, n + 1)
                                    act.activation(dst[:, h, hf * HALF:(hf + 1) * HALF], bank[n % 4][:], ACT.Copy, scale=sc).then_inc(q2, 1)
                                    n += 1
                            if h == 0:
                                act.wait_ge(g1, 1)
                                act.activation(rr[:, 1, :], rr[:, 0, :], ACT.Exp, scale=-1.0).then_inc(rowexp, 1)
                                act.wait_ge(rowexp, 1)
                                act.activation(rr[:, 0, :], rr[:, 1, :], ACT.Ln, bias=1.0).then_inc(rowexp, 1)
                            if h == 2:
                                act.wait_ge(g1, 5)
                                act.activation(packed[32:32 + HM, :], rr[:, 0, :], ACT.Exp).then_inc(g1, 1)
                                act.activation(packed[64:64 + HM, :], rr[:, 2, :], ACT.Exp, scale=-1.0).then_inc(g1, 1)
                                act.activation(packed[96:96 + HM, :], rr[:, 4, :], ACT.Exp).then_inc(g1, 1)
                                act.activation(aprev[:], aprev[:], ACT.Exp).then_inc(g1, 1)
                        for t in range(TT):
                            act.wait_ge(q1, n + 1)
                            act.activation(ktok[:, t], bank[n % 4][:].rearrange("p (h e) -> p h e", h=HM), ACT.Copy).then_inc(q2, 1)
                            n += 1
                        for g in range(HM):
                            for hf in range(2):
                                act.wait_ge(pm, 2 * g + hf + 1)
                                act.activation(yT[:, HM + g, hf * HALF:(hf + 1) * HALF], bank[2 + hf][:], ACT.Identity,
                                               bias=pcol[:, 28 + g:29 + g]).then_inc(pe_v, 1)

                    @block.vector
                    def _(dve):
                        ch = [0]

                        def link(ins):
                            ins.then_inc(chain, 1)
                            ch[0] += 1
                            dve.wait_ge(chain, ch[0])

                        chain = sem("c_chain")
                        dve.wait_ge(rw, 10)
                        zi, zf = zrow[:, 0, :], zrow[:, 1, :]
                        dve.scalar_tensor_tensor(rr[:, 0, :], zf, -1.0, zf, ALU.mult, ALU.max).then_inc(g1, 1)
                        dve.wait_ge(rowexp, 2)
                        link(dve.scalar_tensor_tensor(rr[:, 1, :], zf, 0.0, rr[:, 0, :], ALU.min, ALU.subtract))
                        dve.tensor_tensor_scan(rr[:, 0, :], rr[:, 5, :], rr[:, 1, :], 0.0, ALU.mult, ALU.add)
                        link(dve.tensor_tensor_scan(rr[:, 2, :], rr[:, 1, :], zi, 0.0, ALU.add, ALU.max))
                        dve.tensor_tensor(packed[0:HM, :], zi, rr[:, 0, :], ALU.subtract)
                        dve.tensor_copy(mprev[:, 1:NC_], rr[:, 2, P - 1:S - P:P])
                        link(dve.tensor_tensor(rr[:, 3, :], rr[:, 2, :], rr[:, 0, :], ALU.subtract))
                        dve.tensor_scalar(negM, rr[:, 3, :], -1.0, None, ALU.mult).then_inc(g1, 1)
                        M3 = rr[:, 3, :].rearrange("h (c t) -> h c t", t=P)
                        last = rr[:, 3, P - 1:S:P]
                        dve.tensor_tensor(rr[:, 0, :].rearrange("h (c t) -> h c t", t=P), mprev[:].unsqueeze(2).to_broadcast([HM, NC_, P]),
                                          M3, ALU.subtract).then_inc(g1, 1)
                        dve.tensor_tensor(rr[:, 4, :].rearrange("h (c t) -> h c t", t=P), packed[0:HM, :].rearrange("h (c t) -> h c t", t=P),
                                          last.unsqueeze(2).to_broadcast([HM, NC_, P]), ALU.subtract).then_inc(g1, 1)
                        dve.tensor_tensor(aprev[:], mprev[:], last, ALU.subtract).then_inc(g1, 1)
                        link(dve.reciprocal(fix[:], fix[:]))
                        for g in range(HM):
                            win = 2 << g
                            link(dve.tensor_scalar(fix[:, g, :], fix[:, g, :], float(win), 1.0, ALU.mult, ALU.max))
                            link(dve.tensor_copy(ps2[:, 0, POOL_PAD:], yT[:, HM + g, :]))
                            src = 0
                            for j in range(g + 1):
                                link(dve.tensor_tensor(ps2[:, 1 - src, POOL_PAD:], ps2[:, src, POOL_PAD:],
                                                       ps2[:, src, POOL_PAD - (1 << j):POOL_PAD + S - (1 << j)], ALU.add))
                                src = 1 - src
                            link(dve.tensor_tensor(ps2[:, src, POOL_PAD:POOL_PAD + 16], ps2[:, src, POOL_PAD:POOL_PAD + 16], fix[:, g, :], ALU.mult))
                            dve.scalar_tensor_tensor(yT[:, HM + g, :], ps2[:, src, POOL_PAD:], 1.0 / win, yT[:, HM + g, :],
                                                     ALU.mult, ALU.subtract).then_inc(pl, 1)
                            dve.wait_ge(pl, g + 1)
                        for half in range(2):
                            dve.wait_ge(rdy, half + 1)
                            dve.tensor_copy(pk[:, 4 * half:4 * half + 4, :], bank[4][:].rearrange("p (t r) -> p t r", r=P)).then_inc(g2, 1)
                        dve.wait_ge(rdy, 3)
                        dve.tensor_copy(aprb[:], bank[5][:, 0:HM * NC_].rearrange("p (h c) -> p h c", c=NC_)).then_inc(g2, 1)
                        for n in range(8):
                            dve.wait_ge(rdy, 4 + n)
                            dve.tensor_copy(NM[:, n // 2, (n % 2) * HALF:(n % 2 + 1) * HALF], bank[6 + n % 2][:]).then_inc(g2, 1)
                        for g in range(HM):
                            dve.wait_ge(pe_v, 2 * g + 2)
                            dve.tensor_scalar(yT[:, HM + g, :], yT[:, HM + g, :], pcol[:, 32 + g:33 + g], None, ALU.mult).then_inc(pl, 1)
            with ExitStack() as c3:
                dl = sbuf(c3, "decay_log", [P, 2, P])
                de = sbuf(c3, "decay", [P, 2, P])
                st = sbuf(c3, "scores", [P, 2, P])
                vw = sbuf(c3, "v_weighted", [P, 2, P + 1])
                num = sbuf(c3, "num", [P, 2, P + 1])
                hn = sbuf(c3, "h_normed", [P, 2, P])
                hsq = sbuf(c3, "h_square", [P, 2, P])
                cst = sbuf(c3, "cell_stats", [P, 2, 6])
                inter = sbuf(c3, "inter", [P, 2, P + 1])
                ymix = sbuf(c3, "ymix", [P, 2, P])
                zrows = x1[:, 7, :]
                s_dl, s_de, s_qk, s_st, s_vw = sem("r_decaylog"), sem("r_decay"), sem("r_qk"), sem("r_scores"), sem("r_vw")
                s_ni, s_num, s_sq, s_hn, s_tr, s_up, s_y = sem("r_ni"), sem("r_num"), sem("r_sq"), sem("r_hn"), sem("r_tr"), sem("r_state"), sem("r_y")
                s_den, s_int, s_yc, s_ch = sem("r_den"), sem("r_inter"), sem("r_yc"), sem("r_chain")
                s_rs, s_se = sem("r_rstd"), sem("r_eps")
                steps = [(c, h) for c in range(NC_) for h in range(HM)]
                N = len(steps)
                s_zf, s_zd = sem("r_zeros"), sem("r_zeros_stored")
                with nc.Block() as block:
                    @block.sync
                    def _(sp):
                        sp.wait_ge(s_zf, 1)
                        sp.dma_start(moe_dram[MINB * P:, :].rearrange("(b p) n -> p b n", p=P),
                                     zrows[:].unsqueeze(1).to_broadcast([P, MAXB - MINB, D])).then_inc(s_zd, 16)
                        sp.wait_ge(s_zd, 16)

                    @block.tensor
                    def _(pe):
                        def scores(i):
                            c, h = steps[i]
                            if i >= 2:
                                pe.wait_ge(s_st, i - 1)
                            pe.matmul(bank[i % 2][:, 0:P], kT[:, h, c * P:(c + 1) * P], qT[:, h, c * P:(c + 1) * P], start=True, stop=True).then_inc(s_qk, 1)

                        def turn(i):
                            if i >= 2:
                                pe.wait_ge(s_y, i - 1)
                            pe.wait_ge(s_hn, i + 1)
                            pe.transpose(bank[6 + i % 2][:, 0:P], hn[:, i % 2, :], ident[:]).then_inc(s_tr, 1)

                        scores(0)
                        for i, (c, h) in enumerate(steps):
                            if i + 1 < N:
                                scores(i + 1)
                            pe.wait_ge(s_vw, i + 1)
                            if i >= 2:
                                pe.wait_ge(s_num, i - 1)
                                pe.wait_ge(s_up, i - 1)
                            if c >= 1:
                                pe.wait_ge(s_up, i - HM + 1)
                                pe.matmul(bank[2 + i % 2][:, 256:256 + P + 1], qT[:, h, c * P:(c + 1) * P], state[:, h, :], start=True, stop=True)
                            pe.matmul(bank[4 + i % 2][:, 0:P + 1], ktok[:, c, h, :], vw[:, i % 2, :], start=True, stop=True)
                            pe.wait_ge(s_st, i + 1)
                            pe.matmul(bank[2 + i % 2][:, 0:P + 1], st[:, i % 2, :], vaug[:, c, h, :], start=True, stop=True).then_inc(s_ni, 1)
                            if i >= 1:
                                turn(i - 1)
                        turn(N - 1)

                    @block.scalar
                    def _(act):
                        def decay(i):
                            act.wait_ge(s_dl, i + 1)
                            if i >= 2:
                                act.wait_ge(s_st, i - 1)
                            act.activation(de[:, i % 2, :], dl[:, i % 2, :], ACT.Exp).then_inc(s_de, 1)
                            c, h = steps[i]
                            if i >= 2:
                                act.wait_ge(s_ni, i - 1)
                            act.activation(vw[:, i % 2, :], vaug[:, c, h, :], ACT.Copy, scale=pk[:, c, 96 + h:97 + h]).then_inc(s_vw, 1)

                        decay(0)
                        for i in range(N):
                            if i + 1 < N:
                                decay(i + 1)
                            act.wait_ge(s_den, i + 1)
                            act.activation(hsq[:, i % 2, :], num[:, i % 2, 0:P], ACT.Square, scale=cst[:, i % 2, 1:2],
                                           accum_out=cst[:, i % 2, 2:3]).then_inc(s_sq, 1)

                    @block.gpsimd
                    def _(pool):
                        pool.memset(zrows[:], 0.0).then_inc(s_zf, 1)
                        for i in range(N):
                            pool.wait_ge(s_sq, i + 1)
                            if i >= 2:
                                pool.wait_ge(s_ch, 3 * (i - 2) + 3)
                            pool.tensor_scalar(cst[:, i % 2, 3:4], cst[:, i % 2, 2:3], P * EPS, None, ALU.add).then_inc(s_se, 1)
                            pool.wait_ge(s_se, i + 1)
                            pool.tensor_tensor(cst[:, i % 2, 4:5], cst[:, i % 2, 3:4], mhalf[:], ALU.pow).then_inc(s_rs, 1)

                    @block.vector
                    def _(dve):
                        def decay_log(i):
                            c, h = steps[i]
                            if i >= 2:
                                dve.wait_ge(s_de, i - 1)
                            dve.scalar_tensor_tensor(dl[:, i % 2, :], NM[:, h, c * P:(c + 1) * P], pk[:, c, h:h + 1], cmask[:],
                                                     ALU.add, ALU.add).then_inc(s_dl, 1)

                        def weigh(i):
                            dve.wait_ge(s_de, i + 1)
                            dve.wait_ge(s_qk, i + 1)
                            if i >= 2:
                                dve.wait_ge(s_ni, i - 1)
                            dve.tensor_tensor(st[:, i % 2, :], bank[i % 2][:, 0:P], de[:, i % 2, :], ALU.mult).then_inc(s_st, 1)

                        def finish(i):
                            c, h = steps[i]
                            at = slice(c * P, (c + 1) * P)
                            dve.tensor_scalar(ymix[:, i % 2, :], ucT[:, h, at], pcol[:, 24 + h:25 + h], None, ALU.mult).then_inc(s_yc, 1)
                            dve.wait_ge(s_tr, i + 1)
                            dve.wait_ge(s_yc, 2 * i + 1)
                            dve.scalar_tensor_tensor(ymix[:, i % 2, :], bank[6 + i % 2][:, 0:P], pcol[:, 20 + h:21 + h], ymix[:, i % 2, :],
                                                     ALU.mult, ALU.add).then_inc(s_yc, 1)
                            dve.wait_ge(s_yc, 2 * i + 2)
                            dve.tensor_tensor(yT[:, h, at], ymix[:, i % 2, :], sgo[:, h, at], ALU.mult).then_inc(s_y, 1)

                        decay_log(0)
                        decay_log(1)
                        weigh(0)
                        for i, (c, h) in enumerate(steps):
                            if i + 2 < N:
                                decay_log(i + 2)
                            if i + 1 < N:
                                weigh(i + 1)
                            b = i % 2
                            dve.wait_ge(s_ni, i + 1)
                            if i >= 2:
                                dve.wait_ge(s_sq, i - 1)
                            intra = bank[2 + b][:, 0:P + 1]
                            if c == 0:
                                dve.tensor_copy(num[:, b, :], intra).then_inc(s_num, 1)
                                dve.tensor_copy(state[:, h, :], bank[4 + b][:, 0:P + 1]).then_inc(s_up, 1)
                            else:
                                dve.tensor_scalar(inter[:, b, :], bank[2 + b][:, 256:256 + P + 1], pk[:, c, 32 + h:33 + h], None, ALU.mult).then_inc(s_int, 1)
                                dve.wait_ge(s_int, i - HM + 1)
                                dve.tensor_tensor(num[:, b, :], intra, inter[:, b, :], ALU.add).then_inc(s_num, 1)
                                dve.scalar_tensor_tensor(state[:, h, :], state[:, h, :], aprb[:, h, c:c + 1], bank[4 + b][:, 0:P + 1],
                                                         ALU.mult, ALU.add).then_inc(s_up, 1)
                            dve.wait_ge(s_num, i + 1)
                            dve.scalar_tensor_tensor(cst[:, b, 0:1], num[:, b, P:P + 1], -1.0, pk[:, c, 64 + h:65 + h], ALU.mult, ALU.max).then_inc(s_ch, 1)
                            dve.wait_ge(s_ch, 3 * i + 1)
                            dve.tensor_tensor(cst[:, b, 0:1], cst[:, b, 0:1], num[:, b, P:P + 1], ALU.max).then_inc(s_ch, 1)
                            dve.wait_ge(s_ch, 3 * i + 2)
                            dve.reciprocal(cst[:, b, 1:2], cst[:, b, 0:1]).then_inc(s_den, 1)
                            if i >= 1:
                                finish(i - 1)
                            dve.wait_ge(s_rs, i + 1)
                            dve.scalar_tensor_tensor(cst[:, b, 5:6], cst[:, b, 4:5], float(P) ** 0.5, cst[:, b, 1:2],
                                                     ALU.mult, ALU.mult).then_inc(s_ch, 1)
                            dve.wait_ge(s_ch, 3 * i + 3)
                            if i >= 2:
                                dve.wait_ge(s_tr, i - 1)
                            dve.tensor_scalar(hn[:, b, :], num[:, b, 0:P], cst[:, b, 5:6], None, ALU.mult).then_inc(s_hn, 1)
                        finish(N - 1)

        with ExitStack() as c2:
            wo = sbuf(c2, "w_out", [P, KT, D])
            mix = sbuf(c2, "mix", [P, 2, HALF])
            w_l, x_l, w_m, w_t, w_x = sem("o_w"), sem("o_x"), sem("o_mm"), sem("o_tmp"), sem("o_x1")
            with nc.Block() as block:
                @block.sync
                def _(sp):
                    sp.dma_start(wo[:], a["w_out"][0].rearrange("(k p) n -> p k n", p=P)).then_inc(w_l, 16)
                    sp.dma_start(x1[:], a["x"][0].rearrange("(t p) n -> p t n", p=P)).then_inc(x_l, 16)

                @block.tensor
                def _(pe):
                    pe.wait_ge(w_l, 16)
                    for i in range(2 * TT):
                        t, hf = divmod(i, 2)
                        if i >= 4:
                            pe.wait_ge(w_t, i - 3)
                        for k in range(KT):
                            ins = pe.matmul(bank[i % 4][:], yT[:, k, t * P:(t + 1) * P], wo[:, k, hf * HALF:(hf + 1) * HALF],
                                            start=(k == 0), stop=(k == KT - 1))
                        ins.then_inc(w_m, 1)

                @block.vector
                def _(dve):
                    dve.wait_ge(x_l, 16)
                    for i in range(2 * TT):
                        t, hf = divmod(i, 2)
                        at = slice(hf * HALF, (hf + 1) * HALF)
                        dve.wait_ge(w_m, i + 1)
                        dve.tensor_tensor(mix[:, i % 2, :], bank[i % 4][:], gates[:, 0, at], ALU.mult).then_inc(w_t, 1)
                        dve.wait_ge(w_t, i + 1)
                        dve.tensor_tensor(x1[:, t, at], x1[:, t, at], mix[:, i % 2, :], ALU.add).then_inc(w_x, 1)


def moe(nc, a, sbuf, sem, bank, ident, ones, mhalf, gates, colmod, x1, normed_dram, slots_dram, moe_dram, x2_out):
    NG = EG + NE
    with ExitStack() as ctx:
        rows_i = sbuf(ctx, "slot_rows", [P, TT, 2], I32)
        gate2 = sbuf(ctx, "token_gates", [P, TT, 2])
        slots = sbuf(ctx, "slots", [P, MAXB + 1], I32)
        bexp = sbuf(ctx, "block_expert", [1, MAXB], I32)
        npair = sbuf(ctx, "block_pairs", [1, 1], I32)
        logits = sbuf(ctx, "logits", [P, TT, NG])
        stat = sbuf(ctx, "moe_stat", [P, TT, 2])

        with ExitStack() as c2:
            sq = sbuf(c2, "moe_sq", [P, D])
            xn = sbuf(c2, "moe_xn", [P, 2, D])
            hTt = sbuf(c2, "moe_hT", [P, 2, KT, P])
            wr = sbuf(c2, "w_router", [P, KT, NG])
            br = sbuf(c2, "b_router", [1, NG])
            s_w, s_sq, s_e, s_rs, s_xn, s_tr, s_ht, s_lg, s_lc = [sem("g_" + n) for n in
                ("weights", "square", "eps", "rstd", "normed", "turned", "hT", "logits", "copied")]
            s_st = [sem("g_store0"), sem("g_store1")]
            with nc.Block() as block:
                @block.sync
                def _(sp):
                    sp.dma_start(wr[:, :, 0:EG], a["w_router_group"][0].rearrange("(p k) n -> p k n", k=KT)).then_inc(s_w, 16)
                    sp.dma_start(wr[:, :, EG:NG], a["w_router_expert"][0].rearrange("(p k) n -> p k n", k=KT)).then_inc(s_w, 16)
                    sp.dma_start(br[:, 0:EG], a["b_router_group"]).then_inc(s_w, 16)
                    sp.dma_start(br[:, EG:NG], a["b_router_expert"]).then_inc(s_w, 16)
                    for t in range(TT):
                        sp.wait_ge(s_xn, t + 1)
                        sp.dma_start(normed_dram[t * P:(t + 1) * P, :], xn[:, t % 2, :]).then_inc(s_st[t % 2], 16)
                    for u in range(2):
                        sp.wait_ge(s_st[u], 16 * (TT // 2))

                @block.scalar
                def _(act):
                    for t in range(TT):
                        if t >= 1:
                            act.wait_ge(s_sq, t)
                        act.activation(sq[:], x1[:, t, :], ACT.Square, accum_out=stat[:, t, 0:1]).then_inc(s_sq, 1)

                @block.gpsimd
                def _(pool):
                    for t in range(TT):
                        pool.wait_ge(s_sq, t + 1)
                        pool.tensor_scalar(stat[:, t, 0:1], stat[:, t, 0:1], D * EPS, None, ALU.add).then_inc(s_e, 1)
                        pool.wait_ge(s_e, t + 1)
                        pool.tensor_tensor(stat[:, t, 1:2], stat[:, t, 0:1], mhalf[:], ALU.pow).then_inc(s_rs, 1)

                @block.vector
                def _(dve):
                    def copy_logits(t):
                        dve.wait_ge(s_lg, t + 1)
                        dve.tensor_copy(logits[:, t, :], bank[4 + t % 2][:, 0:NG]).then_inc(s_lc, 1)

                    for t in range(TT):
                        dve.wait_ge(s_rs, t + 1)
                        if t >= 2:
                            dve.wait_ge(s_tr, 2 * (t - 1))
                            dve.wait_ge(s_st[t % 2], 16 * (t // 2))
                        dve.tensor_scalar(xn[:, t % 2, :], x1[:, t, :], stat[:, t, 1:2], ROOT_D, ALU.mult, ALU.mult).then_inc(s_xn, 1)
                        if t >= 2:
                            dve.wait_ge(s_lg, t - 1)
                        for g in range(2):
                            dve.wait_ge(s_tr, 2 * t + g + 1)
                            for k in range(4 * g, 4 * g + 4):
                                ins = dve.tensor_scalar(hTt[:, t % 2, k, :], bank[g + 2 * (t % 2)][:, (k % 4) * P:(k % 4 + 1) * P],
                                                        colmod[:, 0, 3, k:k + 1], colmod[:, 0, 2, k:k + 1], ALU.mult, ALU.add)
                            ins.then_inc(s_ht, 1)
                        if t >= 1:
                            copy_logits(t - 1)
                    copy_logits(TT - 1)

                @block.tensor
                def _(pe):
                    pe.wait_ge(s_w, 64)

                    def route(t):
                        pe.wait_ge(s_ht, 2 * t + 2)
                        if t >= 2:
                            pe.wait_ge(s_lc, t - 1)
                        for k in range(KT):
                            pe.matmul(bank[4 + t % 2][:, 0:NG], hTt[:, t % 2, k, :], wr[:, k, :], start=(k == 0), stop=False)
                        pe.matmul(bank[4 + t % 2][:, 0:NG], ones[0:1, :], br[:], start=False, stop=True).then_inc(s_lg, 1)

                    for t in range(TT):
                        pe.wait_ge(s_xn, t + 1)
                        if t >= 2:
                            pe.wait_ge(s_ht, 2 * (t - 1))
                        for g in range(2):
                            for k in range(4 * g, 4 * g + 4):
                                ins = pe.transpose(bank[g + 2 * (t % 2)][:, (k % 4) * P:(k % 4 + 1) * P], xn[:, t % 2, k:D:KT], ident[:])
                            ins.then_inc(s_tr, 1)
                        if t >= 1:
                            route(t - 1)
                    route(TT - 1)

        with ExitStack() as c2:
            gl8 = sbuf(c2, "group_logits", [P, TT, 8])
            gm8 = sbuf(c2, "group_max", [P, TT, 8])
            gi8 = sbuf(c2, "group_index", [P, TT, 8], U32)
            gif = sbuf(c2, "group_of_token", [P, TT])
            gex = sbuf(c2, "group_exp", [P, TT, EG])
            gs = sbuf(c2, "group_gate", [P, TT])
            io = sbuf(c2, "iota_32", [P, NE])
            iob = sbuf(c2, "iota_blocks", [1, MAXB])
            iop = sbuf(c2, "iota_pairs", [1, MAXB // 2])
            oh4 = sbuf(c2, "group_onehot", [P, TT, EG])
            prod = sbuf(c2, "group_product", [P, TT, EG, EPG])
            es = sbuf(c2, "expert_logits", [P, TT, EPG])
            em8 = sbuf(c2, "expert_max", [P, TT, 8])
            ei8 = sbuf(c2, "expert_index", [P, TT, 8], U32)
            eif = sbuf(c2, "expert_of_token", [P, TT, 2])
            ed = sbuf(c2, "second_exp", [P, TT])
            er = sbuf(c2, "first_share", [P, TT])
            oh = sbuf(c2, "expert_onehot", [P, 2, TT, NE])
            mem = sbuf(c2, "membership", [P, TT, NE], BF16)
            before = sbuf(c2, "before", [P, P], BF16)
            onesb = sbuf(c2, "ones_bf16", [P, P], BF16)
            rank = sbuf(c2, "rank_all", [P, TT, NE])
            cnt = sbuf(c2, "counts", [P, NE])
            nb = sbuf(c2, "expert_blocks", [P, NE])
            ends = sbuf(c2, "block_ends", [P, NE])
            starts = sbuf(c2, "block_starts", [P, NE])
            onerow = sbuf(c2, "ones_row", [P, NE])
            t3 = sbuf(c2, "onehot_product", [P, TT, NE])
            rk = sbuf(c2, "rank", [P, 2, TT])
            sb_ = sbuf(c2, "start_block", [P, 2, TT])
            jj = sbuf(c2, "block_in_expert", [P, 2, TT])
            fslot = sbuf(c2, "slot_float", [P, 2, TT])
            slot_i = sbuf(c2, "slot_int", [P, 2, TT], I32)
            tok_i = sbuf(c2, "token_id", [P, TT], I32)
            zer = sbuf(c2, "zero_slots", [P, MAXB], I32)
            cmp_ = sbuf(c2, "block_compare", [1, MAXB, NE])
            bf = sbuf(c2, "block_expert_float", [1, MAXB])
            pf = sbuf(c2, "pair_compare", [1, MAXB // 2])
            pn = sbuf(c2, "pair_float", [1, 1])
            s_c, s_ex, s_m, s_rk, s_ch, s_sl, s_z, s_sc, s_ld = [sem("t_" + n) for n in
                ("consts", "exps", "member", "ranks", "chain", "slots", "zeroed", "scattered", "loaded")]
            s_go = sem("t_go")
            with nc.Block() as block:
                @block.gpsimd
                def _(pool):
                    pool.iota(io[:], [[1, NE]], base=0, channel_multiplier=0, allow_small_or_imprecise_dtypes=True).then_inc(s_c, 1)
                    pool.iota(iob[:], [[1, MAXB]], base=0, channel_multiplier=0, allow_small_or_imprecise_dtypes=True).then_inc(s_c, 1)
                    pool.iota(iop[:], [[2, MAXB // 2]], base=0, channel_multiplier=0, allow_small_or_imprecise_dtypes=True).then_inc(s_c, 1)
                    pool.iota(tok_i[:], [[P, TT]], base=0, channel_multiplier=1).then_inc(s_c, 1)
                    pool.memset(before[:], 1.0).then_inc(s_c, 1)
                    pool.memset(onesb[:], 1.0).then_inc(s_c, 1)
                    pool.memset(onerow[:], 1.0).then_inc(s_c, 1)
                    pool.memset(zer[:], 0).then_inc(s_c, 1)
                    pool.memset(slots[:, MAXB:MAXB + 1], 0).then_inc(s_c, 1)
                    pool.wait_ge(s_c, 9)
                    pool.affine_select(out=before[:], in_=before[:], compare_op=ALU.is_gt, fill=0.0, base=0,
                                       pattern=[[1, P]], channel_multiplier=-1).then_inc(s_c, 1)
                    pool.wait_ge(s_z, 16)
                    pool.wait_ge(s_sl, 1)
                    for k in range(2):
                        for t in range(TT):
                            pool.indirect_dma_start(slots_dram, bass.IndirectOffsetOnAxis(ap=slot_i[:, k, t:t + 1], axis=0),
                                                    tok_i[:, t:t + 1], None).then_inc(s_sc, 16)

                @block.sync
                def _(sp):
                    sp.wait_ge(s_c, 9)
                    sp.dma_start(slots_dram.rearrange("(p b) o -> p (b o)", b=MAXB), zer[:]).then_inc(s_z, 16)
                    sp.wait_ge(s_sc, 16 * 2 * TT)
                    sp.dma_start(slots[:, 0:MAXB], slots_dram.rearrange("(p b) o -> p (b o)", b=MAXB)).then_inc(s_ld, 16)
                    sp.wait_ge(s_ld, 16)

                @block.scalar
                def _(act):
                    act.wait_ge(s_go, 1)
                    act.activation(gex[:], gex[:], ACT.Exp).then_inc(s_ex, 1)
                    act.wait_ge(s_go, 2)
                    act.activation(ed[:], ed[:], ACT.Exp).then_inc(s_ex, 1)

                @block.tensor
                def _(pe):
                    pe.wait_ge(s_c, 10)
                    pe.wait_ge(s_m, 1)
                    for t in range(TT):
                        for j in range(t + 1):
                            pe.matmul(bank[0][:, t * NE:(t + 1) * NE], before[:] if j == t else onesb[:], mem[:, j, :],
                                      start=(j == 0), stop=(j == t))
                    for t in range(TT):
                        ins = pe.matmul(bank[1][:, 0:NE], onesb[:], mem[:, t, :], start=(t == 0), stop=(t == TT - 1))
                    ins.then_inc(s_rk, 1)

                @block.vector
                def _(dve):
                    ch = [0]

                    def link(ins):
                        ins.then_inc(s_ch, 1)
                        ch[0] += 1
                        dve.wait_ge(s_ch, ch[0])

                    def over(x, n):
                        return x.unsqueeze(len(x.shape)).to_broadcast([*x.shape, n])

                    dve.wait_ge(s_c, 10)
                    link(dve.memset(gl8[:], NEG))
                    link(dve.tensor_copy(gl8[:, :, 0:EG], logits[:, :, 0:EG]))
                    for t in range(TT):
                        ins = dve.max(gm8[:, t, :], gl8[:, t, :])
                    link(ins)
                    for t in range(TT):
                        ins = dve.max_index(gi8[:, t, :], gm8[:, t, :], gl8[:, t, :])
                    link(ins)
                    dve.tensor_tensor(gex[:], gl8[:, :, 0:EG], over(gm8[:, :, 0], EG), ALU.subtract).then_inc(s_go, 1)
                    link(dve.tensor_copy(gif[:], gi8[:, :, 0]))
                    link(dve.tensor_tensor(oh4[:], io[:, 0:EG].unsqueeze(1).to_broadcast([P, TT, EG]), over(gif[:], EG), ALU.is_equal))
                    link(dve.tensor_tensor(prod[:], logits[:, :, EG:NG].rearrange("p t (g e) -> p t g e", g=EG), over(oh4[:], EPG), ALU.mult))
                    link(dve.tensor_tensor(es[:], prod[:, :, 0, :], prod[:, :, 1, :], ALU.add))
                    link(dve.tensor_tensor(es[:], es[:], prod[:, :, 2, :], ALU.add))
                    link(dve.tensor_tensor(es[:], es[:], prod[:, :, 3, :], ALU.add))
                    for t in range(TT):
                        ins = dve.max(em8[:, t, :], es[:, t, :])
                    link(ins)
                    for t in range(TT):
                        ins = dve.max_index(ei8[:, t, :], em8[:, t, :], es[:, t, :])
                    link(ins)
                    dve.tensor_tensor(ed[:], em8[:, :, 1], em8[:, :, 0], ALU.subtract).then_inc(s_go, 1)
                    link(dve.tensor_copy(eif[:], ei8[:, :, 0:2]))
                    link(dve.scalar_tensor_tensor(eif[:], over(gif[:], 2), float(EPG), eif[:], ALU.mult, ALU.add))
                    for k in range(2):
                        ins = dve.tensor_tensor(oh[:, k], io[:].unsqueeze(1).to_broadcast([P, TT, NE]), over(eif[:, :, k], NE), ALU.is_equal)
                        link(ins)
                    dve.tensor_tensor(mem[:], oh[:, 0], oh[:, 1], ALU.add).then_inc(s_m, 1)
                    dve.wait_ge(s_ex, 2)
                    link(dve.tensor_reduce(gs[:], gex[:], X, ALU.add))
                    link(dve.tensor_scalar(er[:], ed[:], 1.0, None, ALU.add))
                    link(dve.tensor_tensor(er[:], er[:], gs[:], ALU.mult))
                    link(dve.reciprocal(gate2[:, :, 0], er[:]))
                    link(dve.tensor_tensor(gate2[:, :, 1], gate2[:, :, 0], ed[:], ALU.mult))
                    dve.wait_ge(s_rk, 1)
                    link(dve.tensor_copy(rank[:], bank[0][:, 0:TT * NE].rearrange("p (t e) -> p t e", e=NE)))
                    link(dve.tensor_copy(cnt[:], bank[1][:, 0:NE]))
                    link(dve.tensor_scalar(nb[:], cnt[:], 0.0, None, ALU.is_gt))
                    for j in range(1, TT):
                        link(dve.scalar_tensor_tensor(nb[:], cnt[:], float(P * j), nb[:], ALU.is_gt, ALU.add))
                    link(dve.tensor_tensor_scan(ends[:], onerow[:], nb[:], 0.0, ALU.mult, ALU.add))
                    link(dve.tensor_tensor(starts[:], ends[:], nb[:], ALU.subtract))
                    for k in range(2):
                        link(dve.tensor_tensor(t3[:], oh[:, k], rank[:], ALU.mult))
                        link(dve.tensor_reduce(rk[:, k], t3[:], X, ALU.add))
                        link(dve.tensor_tensor(t3[:], oh[:, k], starts[:].unsqueeze(1).to_broadcast([P, TT, NE]), ALU.mult))
                        link(dve.tensor_reduce(sb_[:, k], t3[:], X, ALU.add))
                    link(dve.tensor_scalar(jj[:], rk[:], float(P), None, ALU.is_ge))
                    for j in range(2, TT):
                        link(dve.scalar_tensor_tensor(jj[:], rk[:], float(P * j), jj[:], ALU.is_ge, ALU.add))
                    link(dve.tensor_tensor(sb_[:], sb_[:], jj[:], ALU.add))
                    link(dve.scalar_tensor_tensor(rk[:], jj[:], -float(P), rk[:], ALU.mult, ALU.add))
                    link(dve.scalar_tensor_tensor(fslot[:], rk[:], float(MAXB), sb_[:], ALU.mult, ALU.add))
                    dve.tensor_copy(slot_i[:], fslot[:]).then_inc(s_sl, 1)
                    dve.wait_ge(s_sl, 1)
                    link(dve.scalar_tensor_tensor(fslot[:], sb_[:], float(P), rk[:], ALU.mult, ALU.add))
                    link(dve.tensor_copy(rows_i[:].rearrange("p t k -> p k t"), fslot[:]))
                    link(dve.tensor_tensor(cmp_[:], ends[0:1, :].unsqueeze(1).to_broadcast([1, MAXB, NE]), over(iob[:], NE), ALU.is_le))
                    link(dve.tensor_reduce(bf[:], cmp_[:], X, ALU.add))
                    link(dve.tensor_scalar(bf[:], bf[:], float(NE - 1), None, ALU.min))
                    link(dve.tensor_copy(bexp[:], bf[:]))
                    link(dve.tensor_scalar(pf[:], iop[:], ends[0:1, NE - 1:NE], None, ALU.is_lt))
                    link(dve.tensor_reduce(pn[:], pf[:], X, ALU.add))
                    link(dve.tensor_scalar(pn[:], pn[:], -1.0, None, ALU.add))
                    link(dve.tensor_copy(npair[:], pn[:]))

        with ExitStack() as c2:
            WE = KT * DE
            raw = {m: sbuf(c2, "w_" + m, [P, WE]) for m in ("gate", "up", "down")}
            wh = sbuf(c2, "w_high", [P, 2, WE], F32R)
            wl = sbuf(c2, "w_low", [P, 2, WE], F32R)
            xg = sbuf(c2, "gathered", [P, 2, D])
            hf32 = sbuf(c2, "block_h", [P, KT, P])
            hTh = sbuf(c2, "block_hT_high", [P, KT, P], F32R)
            hTl = sbuf(c2, "block_hT_low", [P, KT, P], F32R)
            sg = sbuf(c2, "silu", [P, DE])
            gg = sbuf(c2, "gated", [P, DE])
            gTh = sbuf(c2, "gatedT_high", [P, JT, P], F32R)
            gTl = sbuf(c2, "gatedT_low", [P, JT, P], F32R)
            ob = sbuf(c2, "block_out", [P, 2, D])
            idx = sbuf(c2, "block_index", [P, 2], I32)
            ld = {m: sem("b_load_" + m) for m in raw}
            s_ix, s_tr, s_ht, s_hh, s_hl = [sem("b_" + n) for n in ("index", "turned", "h", "h_high", "h_low")]
            s_wh, s_wl, s_us = [sem("b_" + n) for n in ("w_high", "w_low", "w_used")]
            s_sg, s_gg, s_gt, s_gh, s_gl, s_ob = [sem("b_" + n) for n in ("silu", "gated", "gatedT", "g_high", "g_low", "out_copied")]
            s_own, s_own2 = sem("b_carrier"), sem("b_carrier2")
            s_x = [sem("b_gather0"), sem("b_gather1")]
            s_out = [sem("b_store0"), sem("b_store1")]
            dram = {"gate": a["w_expert_gate"][0].rearrange("e (p k) n -> e p (k n)", k=KT),
                    "up": a["w_expert_up"][0].rearrange("e (p k) n -> e p (k n)", k=KT),
                    "down": a["w_expert_down"][0].rearrange("e (p j) n -> e p (j n)", j=JT)}
            HW_ = WE // 2

            def gate_at(n):
                return n * 3 - 1

            def up_at(n):
                return n * 3

            def down_at(n, left):
                return n * 3 + (4 if left else 2)

            def over_blocks(eng, body):
                before_last = eng.value_load(npair[0:1, 0:1], min_val=MINB // 2 - 1, max_val=MAXB // 2 - 1)
                with eng.Fori(0, before_last) as i:
                    for u in range(2):
                        body(i * 2 + u, u, 2 if u else 3)
                for u in range(2):
                    body(before_last * 2 + u, u, 1 - u)
                return before_last + 1

            def split_high(act, kind, n, s, par):
                act.wait_ge(ld[kind], n * 16 + 16)
                for c in range(2):
                    if not isinstance(s, int) or s >= 2:
                        act.wait_ge(s_us, s * 2 + (c - 3))
                    half = slice(c * HW_, (c + 1) * HW_)
                    act.activation(wh[:, par, half], raw[kind][:, half], ACT.Copy).then_inc(s_wh, 1)

            def split_low(dve, kind, s, par):
                for c in range(2):
                    dve.wait_ge(s_wh, s * 2 + (c + 1))
                    half = slice(c * HW_, (c + 1) * HW_)
                    dve.tensor_tensor(wl[:, par, half], raw[kind][:, half], wh[:, par, half].bitcast(F32), ALU.subtract).then_inc(s_wl, 1)

            with nc.Block() as block:
                @block.sync
                def _(sp):
                    def load(kind, e):
                        sp.dma_start(raw[kind][:], dram[kind][bass.ds(e, 1)].rearrange("o p n -> (o p) n")).then_inc(ld[kind], 16)

                    e0 = sp.value_load(bexp[0:1, 0:1], min_val=0, max_val=NE - 1)
                    for kind in ("gate", "up", "down"):
                        load(kind, e0)
                    e1 = sp.value_load(bexp[0:1, 1:2], min_val=0, max_val=NE - 1)
                    for s, kind in enumerate(("gate", "up")):
                        sp.wait_ge(s_wl, 2 * s + 2)
                        load(kind, e1)

                    def loads(n, u, left):
                        if left >= 2:
                            e2 = sp.value_load(bexp[0:1, bass.ds(n + 2, 1)], min_val=0, max_val=NE - 1)
                            for kind, at in (("gate", gate_at), ("up", up_at)):
                                sp.wait_ge(s_wl, at(n + 1) * 2 + 2)
                                sp.sem_inc(s_own2, 1)
                                load(kind, e2)
                        if left >= 1:
                            e1 = sp.value_load(bexp[0:1, bass.ds(n + 1, 1)], min_val=0, max_val=NE - 1)
                            sp.wait_ge(s_wl, down_at(n, left) * 2 + 2)
                            sp.sem_inc(s_own2, 1)
                            load("down", e1)

                    over_blocks(sp, loads)

                @block.gpsimd
                def _(pool):
                    for m in range(3):
                        if m == 2:
                            pool.wait_ge(s_tr, 1)
                        pool.tensor_copy(idx[:, m % 2:m % 2 + 1], slots[:, m:m + 1]).then_inc(s_ix, 1)
                        pool.wait_ge(s_ix, m + 1)
                        pool.indirect_dma_start(xg[:, m % 2, :], None, normed_dram,
                                                bass.IndirectOffsetOnAxis(ap=idx[:, m % 2:m % 2 + 1], axis=0)).then_inc(s_x[m % 2], 16)

                    def gather(n, u, left):
                        if left >= 2:
                            v = 1 - u
                            pool.wait_ge(s_tr, n + 2)
                            pool.tensor_copy(idx[:, v:v + 1], slots[:, bass.ds(n + 3, 1)]).then_inc(s_ix, 1)
                            pool.wait_ge(s_ix, n + 4)
                            pool.sem_inc(s_own, 1)
                            pool.indirect_dma_start(xg[:, v, :], None, normed_dram,
                                                    bass.IndirectOffsetOnAxis(ap=idx[:, v:v + 1], axis=0)).then_inc(s_x[v], 16)

                    n_pairs = over_blocks(pool, gather)
                    pool.wait_ge(s_x[0], n_pairs * 16 + 16)
                    pool.sem_inc(s_own, 1)

                @block.tensor
                def _(pe):
                    pe.sem_inc(s_ob, 1)

                    def turn(u):
                        for k in range(KT):
                            ins = pe.transpose(bank[k // 4][:, (k % 4) * P:(k % 4 + 1) * P], xg[:, u, k:D:KT], ident[:])
                        ins.then_inc(s_tr, 1)

                    def project(b, s, par):
                        w = (wh[:, par].rearrange("p (k n) -> p k n", k=KT), wl[:, par].rearrange("p (k n) -> p k n", k=KT))
                        for k in range(KT):
                            if k % 4 == 0:
                                pe.wait_ge(s_wl, s * 2 + (k // 4 + 1))
                            ins = split_mm(pe, b, (hTh[:, k, :], hTl[:, k, :]), (w[0][:, k, :], w[1][:, k, :]), k == 0, k == KT - 1)
                            if k % 4 == 3:
                                ins.then_inc(s_us, 1)

                    def turn_gated():
                        for j in range(JT):
                            ins = pe.transpose(bank[4][:, j * P:(j + 1) * P], gg[:, j:DE:JT], ident[:])
                        ins.then_inc(s_gt, 1)

                    pe.wait_ge(s_x[0], 16)
                    turn(0)
                    pe.wait_ge(s_hl, 1)
                    project(bank[2], 0, 0)
                    project(bank[3], 1, 1)
                    pe.wait_ge(s_x[1], 16)
                    turn(1)
                    pe.wait_ge(s_gg, 1)
                    turn_gated()

                    def products(n, u, left):
                        if left >= 1:
                            pe.wait_ge(s_hl, n + 2)
                            pe.wait_ge(s_gg, n + 1)
                            project(bank[2], gate_at(n + 1), u)
                            project(bank[3], up_at(n + 1), 1 - u)
                        if left >= 2:
                            pe.wait_ge(s_x[u], n * 8 + (32 - 8 * u))
                            turn(u)
                        pe.wait_ge(s_gl, n + 1)
                        pe.wait_ge(s_ob, n + 1)
                        w = (wh[:, u].rearrange("p (j n) -> p j n", j=JT), wl[:, u].rearrange("p (j n) -> p j n", j=JT))
                        for j in range(JT):
                            if j % 2 == 0:
                                pe.wait_ge(s_wl, down_at(n, left) * 2 + (j // 2 + 1))
                            for hf in range(2):
                                at = slice(hf * HALF, (hf + 1) * HALF)
                                ins = split_mm(pe, bank[5 + hf], (gTh[:, j, :], gTl[:, j, :]), (w[0][:, j, at], w[1][:, j, at]), j == 0, j == JT - 1)
                            if j % 2 == 1:
                                ins.then_inc(s_us, 1)
                        if left >= 1:
                            pe.wait_ge(s_gg, n + 2)
                            turn_gated()

                    over_blocks(pe, products)

                @block.scalar
                def _(act):
                    act.sem_inc(s_out[0], 16)
                    act.sem_inc(s_out[1], 16)

                    def high_h(m):
                        act.wait_ge(s_ht, m + 1)
                        act.activation(hTh[:], hf32[:], ACT.Copy).then_inc(s_hh, 1)

                    high_h(0)
                    split_high(act, "gate", 0, 0, 0)
                    split_high(act, "up", 0, 1, 1)
                    act.wait_ge(s_us, 2)
                    act.activation(sg[:], bank[2], ACT.Silu).then_inc(s_sg, 1)
                    high_h(1)
                    split_high(act, "gate", 1, 2, 0)

                    def step(n, u, left):
                        if left >= 1:
                            split_high(act, "up", n + 1, up_at(n + 1), 1 - u)
                        act.wait_ge(s_gt, n + 1)
                        act.activation(gTh[:], bank[4].rearrange("p (j t) -> p j t", t=P), ACT.Copy).then_inc(s_gh, 1)
                        split_high(act, "down", n, down_at(n, left), u)
                        if left >= 1:
                            act.wait_ge(s_us, gate_at(n + 1) * 2 + 2)
                            act.wait_ge(s_gg, n + 1)
                            act.activation(sg[:], bank[2], ACT.Silu).then_inc(s_sg, 1)
                        if left >= 2:
                            high_h(n + 2)
                            split_high(act, "gate", n + 2, gate_at(n + 2), 1 - u)
                        act.wait_ge(s_us, down_at(n, left) * 2 + 2)
                        act.wait_ge(s_out[u], n * 8 + (16 - 8 * u))
                        act.activation(ob[:, u, 0:HALF], bank[5], ACT.Copy)
                        act.activation(ob[:, u, HALF:D], bank[6], ACT.Copy).then_inc(s_ob, 1)
                        act.wait_ge(s_ob, n + 2)
                        act.dma_start(moe_dram[bass.ds(n * P, P), :], ob[:, u, :]).then_inc(s_out[u], 16)

                    n_pairs = over_blocks(act, step)
                    for u in range(2):
                        act.wait_ge(s_out[u], n_pairs * 16 + 16)
                        act.sem_inc(s_own2, 1)

                @block.vector
                def _(dve):
                    def leave(m):
                        dve.wait_ge(s_tr, m + 1)
                        if not isinstance(m, int) or m >= 1:
                            dve.wait_ge(s_hl, m)
                        for k in range(KT):
                            ins = dve.tensor_scalar(hf32[:, k, :], bank[k // 4][:, (k % 4) * P:(k % 4 + 1) * P],
                                                    colmod[:, 0, 3, k:k + 1], colmod[:, 0, 2, k:k + 1], ALU.mult, ALU.add)
                        ins.then_inc(s_ht, 1)

                    def low_h(m):
                        dve.wait_ge(s_hh, m + 1)
                        dve.tensor_tensor(hTl[:], hf32[:], hTh[:].bitcast(F32), ALU.subtract).then_inc(s_hl, 1)

                    def gated(m, s):
                        dve.wait_ge(s_sg, m + 1)
                        dve.wait_ge(s_us, s * 2 + 2)
                        dve.tensor_tensor(gg[:], bank[3], sg[:], ALU.mult).then_inc(s_gg, 1)

                    leave(0)
                    low_h(0)
                    split_low(dve, "gate", 0, 0)
                    split_low(dve, "up", 1, 1)
                    leave(1)
                    gated(0, 1)
                    low_h(1)
                    split_low(dve, "gate", 2, 0)

                    def step(n, u, left):
                        if left >= 1:
                            split_low(dve, "up", up_at(n + 1), 1 - u)
                        dve.wait_ge(s_gh, n + 1)
                        dve.tensor_tensor(gTl[:], bank[4].rearrange("p (j t) -> p j t", t=P), gTh[:].bitcast(F32), ALU.subtract).then_inc(s_gl, 1)
                        split_low(dve, "down", down_at(n, left), u)
                        if left >= 2:
                            leave(n + 2)
                        if left >= 1:
                            gated(n + 1, up_at(n + 1))
                        if left >= 2:
                            low_h(n + 2)
                            split_low(dve, "gate", gate_at(n + 2), 1 - u)

                    over_blocks(dve, step)

        with ExitStack() as c2:
            r0 = sbuf(c2, "result0", [P, 2, D])
            r1 = sbuf(c2, "result1", [P, 2, D])
            yy = sbuf(c2, "combined", [P, 2, D])
            sq = sbuf(c2, "comb_sq", [P, D])
            xo = sbuf(c2, "x2_tile", [P, 2, D])
            fg = sbuf(c2, "final_gain", [P, D])
            s_fg, s_a, s_b, s_y, s_sq, s_e, s_rs, s_o, s_r = [sem("e_" + n) for n in ("gain", "first", "second", "sum", "square", "eps", "rstd", "out", "root")]
            s_g = [[sem(f"e_gather{k}{u}") for u in range(2)] for k in range(2)]
            s_st = [sem("e_store0"), sem("e_store1")]
            with nc.Block() as block:
                @block.sync
                def _(sp):
                    sp.dma_start(fg[:], a["final_g"].rearrange("(o n) -> o n", o=1).to_broadcast([P, D])).then_inc(s_fg, 16)
                    for t in range(TT):
                        sp.wait_ge(s_o, t + 1)
                        sp.dma_start(x2_out[t * P:(t + 1) * P, :], xo[:, t % 2, :]).then_inc(s_st[t % 2], 16)
                    for u in range(2):
                        sp.wait_ge(s_st[u], 16 * (TT // 2))

                @block.gpsimd
                def _(pool):
                    def root(t):
                        pool.wait_ge(s_sq, t + 1)
                        pool.tensor_scalar(stat[:, t, 0:1], stat[:, t, 0:1], D * EPS, None, ALU.add).then_inc(s_e, 1)
                        pool.wait_ge(s_e, 2 * t + 1)
                        pool.tensor_tensor(stat[:, t, 1:2], stat[:, t, 0:1], mhalf[:], ALU.pow).then_inc(s_e, 1)
                        pool.wait_ge(s_e, 2 * t + 2)
                        pool.tensor_scalar(stat[:, t, 1:2], stat[:, t, 1:2], ROOT_D, None, ALU.mult).then_inc(s_rs, 1)

                    for t in range(TT):
                        if t >= 2:
                            pool.wait_ge(s_b, t - 1)
                        for k, r in enumerate((r0, r1)):
                            pool.indirect_dma_start(r[:, t % 2, :], None, moe_dram,
                                                    bass.IndirectOffsetOnAxis(ap=rows_i[:, t, k:k + 1], axis=0)).then_inc(s_g[k][t % 2], 16)
                        if t >= 1:
                            root(t - 1)
                    root(TT - 1)

                @block.scalar
                def _(act):
                    for t in range(TT):
                        act.wait_ge(s_y, t + 1)
                        if t >= 1:
                            act.wait_ge(s_sq, t)
                        act.activation(sq[:], x1[:, t, :], ACT.Square, accum_out=stat[:, t, 0:1]).then_inc(s_sq, 1)

                @block.vector
                def _(dve):
                    def close(t):
                        dve.wait_ge(s_rs, t + 1)
                        if t == 0:
                            dve.wait_ge(s_fg, 16)
                        if t >= 2:
                            dve.wait_ge(s_st[t % 2], 16 * (t // 2))
                        dve.scalar_tensor_tensor(xo[:, t % 2, :], x1[:, t, :], stat[:, t, 1:2], fg[:], ALU.mult, ALU.mult).then_inc(s_o, 1)

                    for t in range(TT):
                        u = t % 2
                        dve.wait_ge(s_g[0][u], 16 * (t // 2 + 1))
                        dve.tensor_scalar(yy[:, u, :], r0[:, u, :], gate2[:, t, 0:1], None, ALU.mult).then_inc(s_a, 1)
                        dve.wait_ge(s_a, 2 * t + 1)
                        dve.wait_ge(s_g[1][u], 16 * (t // 2 + 1))
                        dve.scalar_tensor_tensor(yy[:, u, :], r1[:, u, :], gate2[:, t, 1:2], yy[:, u, :], ALU.mult, ALU.add).then_inc(s_b, 1)
                        dve.wait_ge(s_b, t + 1)
                        dve.tensor_tensor(yy[:, u, :], yy[:, u, :], gates[:, 1, :], ALU.mult).then_inc(s_a, 1)
                        dve.wait_ge(s_a, 2 * t + 2)
                        dve.tensor_tensor(x1[:, t, :], x1[:, t, :], yy[:, u, :], ALU.add).then_inc(s_y, 1)
                        if t >= 1:
                            close(t - 1)
                    close(TT - 1)


def split_mm(pe, out, stationary, moving, start, stop):
    (sh, sl), (mh, ml) = stationary, moving
    pe.matmul(out, sh, mh, start=start, stop=False)
    pe.matmul(out, sh, ml, start=False, stop=False)
    return pe.matmul(out, sl, mh, start=False, stop=stop)


def norm_turn_whole(nc, ctx, tag, sbuf, sem, bank, ident, mhalf, gain, shift, hT, src, src_dram):
    stat = sbuf(ctx, tag + "_stat", [P, TT, 2])
    sq = sbuf(ctx, tag + "_sq", [P, D])
    xn = sbuf(ctx, tag + "_xn", [P, 2, D])
    s_ld = [sem(tag + "_load0"), sem(tag + "_load1")]
    s_sq, s_e, s_rs, s_xn, s_tr, s_ht = [sem(tag + "_" + n) for n in ("square", "eps", "rstd", "normed", "turned", "hT")]
    ring = src.shape[1]
    with nc.Block() as block:
        if src_dram is not None:
            @block.sync
            def _(sp):
                for t in range(TT):
                    if t >= ring:
                        sp.wait_ge(s_xn, t - ring + 1)
                        sp.wait_ge(s_sq, t - ring + 1)
                    sp.dma_start(src[:, t % ring, :], src_dram[t * P:(t + 1) * P, :]).then_inc(s_ld[t % 2], 16)

        @block.scalar
        def _(act):
            for t in range(TT):
                if src_dram is not None:
                    act.wait_ge(s_ld[t % 2], 16 * (t // 2 + 1))
                if t >= 1:
                    act.wait_ge(s_sq, t)
                act.activation(sq[:], src[:, t % ring, :], ACT.Square, accum_out=stat[:, t, 0:1]).then_inc(s_sq, 1)

        @block.gpsimd
        def _(pool):
            for t in range(TT):
                pool.wait_ge(s_sq, t + 1)
                pool.tensor_scalar(stat[:, t, 0:1], stat[:, t, 0:1], D * EPS, None, ALU.add).then_inc(s_e, 1)
                pool.wait_ge(s_e, t + 1)
                pool.tensor_tensor(stat[:, t, 1:2], stat[:, t, 0:1], mhalf[:], ALU.pow).then_inc(s_rs, 1)

        @block.vector
        def _(dve):
            for t in range(TT):
                dve.wait_ge(s_rs, t + 1)
                if t >= 2:
                    dve.wait_ge(s_tr, 2 * (t - 1))
                dve.tensor_scalar(xn[:, t % 2, :], src[:, t % ring, :], stat[:, t, 1:2], ROOT_D, ALU.mult, ALU.mult).then_inc(s_xn, 1)
                for g in range(2):
                    dve.wait_ge(s_tr, 2 * t + g + 1)
                    for k in range(4 * g, 4 * g + 4):
                        ins = dve.tensor_scalar(hT[:, k, t * P:(t + 1) * P], bank[g + 2 * (t % 2)][:, (k % 4) * P:(k % 4 + 1) * P],
                                                gain[:, k:k + 1], shift[:, k:k + 1], ALU.mult, ALU.add)
                    ins.then_inc(s_ht, 1)

        @block.tensor
        def _(pe):
            for t in range(TT):
                pe.wait_ge(s_xn, t + 1)
                if t >= 2:
                    pe.wait_ge(s_ht, 2 * (t - 1))
                for g in range(2):
                    for k in range(4 * g, 4 * g + 4):
                        ins = pe.transpose(bank[g + 2 * (t % 2)][:, (k % 4) * P:(k % 4 + 1) * P], xn[:, t % 2, k:D:KT], ident[:])
                    ins.then_inc(s_tr, 1)


def norm_turn(nc, ctx, tag, sbuf, sem, bank, ident, mhalf, gain, shift, hTh, hTl, src, src_dram):
    stat = sbuf(ctx, tag + "_stat", [P, TT, 2])
    sq = sbuf(ctx, tag + "_sq", [P, D])
    xn = sbuf(ctx, tag + "_xn", [P, 2, D])
    hf32 = sbuf(ctx, tag + "_h", [P, 2, KT, P])
    s_ld = [sem(tag + "_load0"), sem(tag + "_load1")]
    s_sq, s_e, s_rs, s_xn, s_tr, s_ht, s_hi, s_lo = [sem(tag + "_" + n) for n in ("square", "eps", "rstd", "normed", "turned", "h", "high", "low")]
    ring = src.shape[1]
    with nc.Block() as block:
        if src_dram is not None:
            @block.sync
            def _(sp):
                for t in range(TT):
                    if t >= ring:
                        sp.wait_ge(s_xn, t - ring + 1)
                        sp.wait_ge(s_sq, t - ring + 1)
                    sp.dma_start(src[:, t % ring, :], src_dram[t * P:(t + 1) * P, :]).then_inc(s_ld[t % 2], 16)

        @block.scalar
        def _(act):
            def high(t):
                act.wait_ge(s_ht, 2 * t + 2)
                act.activation(hTh[:, :, t * P:(t + 1) * P], hf32[:, t % 2], ACT.Copy).then_inc(s_hi, 1)

            for t in range(TT):
                if src_dram is not None:
                    act.wait_ge(s_ld[t % 2], 16 * (t // 2 + 1))
                if t >= 1:
                    act.wait_ge(s_sq, t)
                act.activation(sq[:], src[:, t % ring, :], ACT.Square, accum_out=stat[:, t, 0:1]).then_inc(s_sq, 1)
                if t >= 2:
                    high(t - 2)
            high(TT - 2)
            high(TT - 1)

        @block.gpsimd
        def _(pool):
            for t in range(TT):
                pool.wait_ge(s_sq, t + 1)
                pool.tensor_scalar(stat[:, t, 0:1], stat[:, t, 0:1], D * EPS, None, ALU.add).then_inc(s_e, 1)
                pool.wait_ge(s_e, t + 1)
                pool.tensor_tensor(stat[:, t, 1:2], stat[:, t, 0:1], mhalf[:], ALU.pow).then_inc(s_rs, 1)

        @block.vector
        def _(dve):
            def normed(t):
                dve.wait_ge(s_rs, t + 1)
                if t >= 2:
                    dve.wait_ge(s_tr, 2 * (t - 1))
                dve.tensor_scalar(xn[:, t % 2, :], src[:, t % ring, :], stat[:, t, 1:2], ROOT_D, ALU.mult, ALU.mult).then_inc(s_xn, 1)

            def low(t):
                dve.wait_ge(s_hi, t + 1)
                dve.tensor_tensor(hTl[:, :, t * P:(t + 1) * P], hf32[:, t % 2], hTh[:, :, t * P:(t + 1) * P].bitcast(F32), ALU.subtract).then_inc(s_lo, 1)

            normed(0)
            for t in range(TT):
                if t + 1 < TT:
                    normed(t + 1)
                if t >= 2:
                    low(t - 2)
                    dve.wait_ge(s_lo, t - 1)
                for g in range(2):
                    dve.wait_ge(s_tr, 2 * t + g + 1)
                    for k in range(4 * g, 4 * g + 4):
                        ins = dve.tensor_scalar(hf32[:, t % 2, k, :], bank[g + 2 * (t % 2)][:, (k % 4) * P:(k % 4 + 1) * P],
                                                gain[:, k:k + 1], shift[:, k:k + 1], ALU.mult, ALU.add)
                    ins.then_inc(s_ht, 1)
            low(TT - 2)
            low(TT - 1)

        @block.tensor
        def _(pe):
            for t in range(TT):
                pe.wait_ge(s_xn, t + 1)
                if t >= 2:
                    pe.wait_ge(s_ht, 2 * (t - 1))
                for g in range(2):
                    for k in range(4 * g, 4 * g + 4):
                        ins = pe.transpose(bank[g + 2 * (t % 2)][:, (k % 4) * P:(k % 4 + 1) * P], xn[:, t % 2, k:D:KT], ident[:])
                    ins.then_inc(s_tr, 1)


def attention(nc, a, sbuf, sem, bank, ident, ones, mhalf, gates, colmod, psum, x2_dram, negf_dram, x3):
    w_pk = a["fox_w_in_2"][0].rearrange("(p k) n -> p k n", k=KT)
    with ExitStack() as outer:
        hT = sbuf(outer, "fox_hT", [P, KT, S])
        with ExitStack() as c2:
            xl = sbuf(c2, "fox_x_rows", [P, 2, D])
            norm_turn_whole(nc, c2, "f", sbuf, sem, bank, ident, mhalf, colmod[:, 1, 1, :], colmod[:, 1, 0, :], hT, xl, x2_dram)
        with ExitStack() as ctx:
            vtok = sbuf(ctx, "v_rows", [P, TT, D])
            with ExitStack() as c2:
                wv = sbuf(c2, "w_value", [P, KT, D])
                wf = sbuf(c2, "w_forget", [P, KT, HF])
                fb = sbuf(c2, "forget_bias", [HF, 1])
                fr = sbuf(c2, "forget_rows", [HF, 3, S])
                s_w, s_wf, s_m, s_c, s_f, s_ch, s_st = [sem("v_" + n) for n in ("weights", "wforget", "mm", "copied", "frow", "chain", "stored")]
                with nc.Block() as block:
                    @block.sync
                    def _(sp):
                        sp.dma_start(wf[:], w_pk[:, :, 3 * D:3 * D + HF]).then_inc(s_wf, 16)
                        sp.dma_start(fb[:], a["fox_b_f_2"][0].rearrange("(h o) -> h o", o=1)).then_inc(s_wf, 16)
                        sp.dma_start(wv[:], w_pk[:, :, 2 * D:3 * D]).then_inc(s_w, 16)
                        sp.wait_ge(s_ch, 7)
                        sp.dma_start(negf_dram, fr[:, 1, :]).then_inc(s_st, 16)
                        sp.wait_ge(s_st, 16)

                    @block.tensor
                    def _(pe):
                        pe.wait_ge(s_wf, 32)
                        for hf in range(2):
                            for k in range(KT):
                                ins = pe.matmul(bank[4 + hf][0:HF, :], wf[:, k, :], hT[:, k, hf * HALF:(hf + 1) * HALF], start=(k == 0), stop=(k == KT - 1))
                            ins.then_inc(s_f, 1)
                        pe.wait_ge(s_w, 16)
                        for i in range(2 * TT):
                            t, hf = divmod(i, 2)
                            if i >= 4:
                                pe.wait_ge(s_c, i - 3)
                            for k in range(KT):
                                ins = pe.matmul(bank[i % 4], hT[:, k, t * P:(t + 1) * P], wv[:, k, hf * HALF:(hf + 1) * HALF], start=(k == 0), stop=(k == KT - 1))
                            ins.then_inc(s_m, 1)

                    @block.scalar
                    def _(act):
                        act.wait_ge(s_ch, 3)
                        act.activation(fr[:, 1, :], fr[:, 1, :], ACT.Exp, scale=-1.0).then_inc(s_ch, 1)
                        act.wait_ge(s_ch, 4)
                        act.activation(fr[:, 1, :], fr[:, 1, :], ACT.Ln, bias=1.0).then_inc(s_ch, 1)
                        for i in range(2 * TT):
                            t, hf = divmod(i, 2)
                            act.wait_ge(s_m, i + 1)
                            act.activation(vtok[:, t, hf * HALF:(hf + 1) * HALF], bank[i % 4], ACT.Copy).then_inc(s_c, 1)

                    @block.vector
                    def _(dve):
                        dve.wait_ge(s_wf, 32)
                        for hf in range(2):
                            dve.wait_ge(s_f, hf + 1)
                            dve.tensor_scalar(fr[:, 0, hf * HALF:(hf + 1) * HALF], bank[4 + hf][0:HF, :], fb[:], None, ALU.add).then_inc(s_ch, 1)
                        dve.wait_ge(s_ch, 2)
                        dve.scalar_tensor_tensor(fr[:, 1, :], fr[:, 0, :], -1.0, fr[:, 0, :], ALU.mult, ALU.max).then_inc(s_ch, 1)
                        dve.wait_ge(s_ch, 5)
                        dve.scalar_tensor_tensor(fr[:, 2, :], fr[:, 0, :], 0.0, fr[:, 1, :], ALU.min, ALU.subtract).then_inc(s_ch, 1)
                        dve.wait_ge(s_ch, 6)
                        dve.tensor_scalar(fr[:, 0, :], fr[:, 2, :], -1.0, None, ALU.mult).then_inc(s_f, 1)
                        dve.wait_ge(s_f, 3)
                        dve.tensor_tensor_scan(fr[:, 1, :], fr[:, 0, :], fr[:, 0, :], 0.0, ALU.add, ALU.bypass).then_inc(s_ch, 1)

            with ExitStack() as c2:
                wqk = sbuf(c2, "w_query_key", [P, 2, KT, P])
                qp = sbuf(c2, "q_padded", [P, 2, S])
                kT = sbuf(c2, "kT_pair", [P, S])
                vp = sbuf(c2, "v_pair", [P, TT, P])
                sq = sbuf(c2, "qk_square", [P, 4, HALF])
                nf = sbuf(c2, "minus_F", [P, 2, S])
                nfd = sbuf(c2, "minus_F_masked", [P, 2, S])
                lg = sbuf(c2, "probs", [P, 2, S])
                pT = sbuf(c2, "probsT", [P, 2, TT, P])
                bd = sbuf(c2, "head_mean", [P, P])
                cm = sbuf(c2, "causal_rows", [P, P])
                gq = sbuf(c2, "qk_gain", [P, 2])
                gqs = sbuf(c2, "q_gain_scaled", [P, 1])
                epc = sbuf(c2, "eps_col", [P, 1])
                mx = sbuf(c2, "row_max", [P, 2, 4])
                rsum = sbuf(c2, "row_sum", [P, 2, 2])
                NQ = 2 * TT
                names = ("weights", "minusf", "gain", "consts", "proj", "square", "mean", "root", "recip", "qkT", "masked", "vpair",
                         "logits", "max", "negmax", "exp", "turn", "turned0", "turned1", "pv", "out", "recsum")
                (s_w, s_nf, s_g, s_c, s_pj, s_sq, s_mn, s_rt, s_rc, s_qk, s_nfd, s_vp,
                 s_lg, s_mx, s_nm, s_ex, s_t, s_e0, s_e1, s_pv, s_o, s_rs) = [sem("a_" + n) for n in names]
                s_m1, s_own, s_own2 = sem("a_max1"), sem("a_carrier"), sem("a_carrier2")
                with nc.Block() as block:
                    @block.sync
                    def _(sp):
                        sp.dma_start(gq[0:DH, 0:1], a["fox_q_norm_2"][0].rearrange("(d o) -> d o", o=1)).then_inc(s_g, 16)
                        sp.dma_start(gq[DH:P, 0:1], a["fox_q_norm_2"][0].rearrange("(d o) -> d o", o=1)).then_inc(s_g, 16)
                        sp.dma_start(gq[0:DH, 1:2], a["fox_k_norm_2"][0].rearrange("(d o) -> d o", o=1)).then_inc(s_g, 16)
                        sp.dma_start(gq[DH:P, 1:2], a["fox_k_norm_2"][0].rearrange("(d o) -> d o", o=1)).then_inc(s_g, 16)
                        with sp.Fori(0, PAIRS) as i:
                            sp.wait_ge(s_pj, i * 4 + 1)
                            sp.sem_inc(s_own2, 1)
                            for g in range(2):
                                sp.dma_start(wqk[:, g], w_pk[:, :, bass.ds(i * P + g * D, P)]).then_inc(s_w, 16)
                            sp.wait_ge(s_mx, i * NQ + 1)
                            sp.sem_inc(s_own2, 1)
                            sp.wait_ge(s_nfd, i + 1)
                            sp.sem_inc(s_own2, 1)
                            for g in range(2):
                                sp.dma_start(nf[:, g, :], negf_dram[bass.ds(i * 2 + g, 1), :].to_broadcast([P, S])).then_inc(s_nf, 16)

                    @block.gpsimd
                    def _(pool):
                        pool.memset(bd[:], 0.0).then_inc(s_c, 1)
                        pool.memset(cm[:], 0.0).then_inc(s_c, 1)
                        pool.memset(qp[:], 0.0).then_inc(s_c, 1)
                        pool.memset(epc[:], EPS).then_inc(s_c, 1)
                        pool.wait_ge(s_c, 4)
                        pool.memset(bd[0:DH, 0:DH], 1.0 / DH).then_inc(s_c, 1)
                        pool.memset(bd[DH:P, DH:P], 1.0 / DH).then_inc(s_c, 1)
                        pool.wait_ge(s_c, 6)
                        pool.affine_select(out=cm[:], in_=cm[:], compare_op=ALU.is_ge, fill=NEG, base=0,
                                           pattern=[[-1, P]], channel_multiplier=1).then_inc(s_c, 1)
                        pool.wait_ge(s_c, 7)
                        pool.sem_inc(s_nfd, 1)
                        with pool.Fori(0, PAIRS) as i:
                            pool.wait_ge(s_pv, i * NQ + 1)
                            pool.tensor_copy(vp[:], vtok[:, :, bass.ds(i * P, P)]).then_inc(s_vp, 1)
                            pool.wait_ge(s_nf, i * 32 + 32)
                            pool.wait_ge(s_mx, i * NQ + 1)
                            pool.tensor_tensor(nfd[:].rearrange("p g (t s) -> p (g t) s", s=P), nf[:].rearrange("p g (t s) -> p (g t) s", s=P),
                                               cm[:].unsqueeze(1).to_broadcast([P, 2 * TT, P]), ALU.add).then_inc(s_nfd, 1)

                    @block.tensor
                    def _(pe):
                        pe.sem_inc(s_pj, 1)
                        pe.sem_inc(s_pv, 1)
                        pe.wait_ge(s_c, 7)
                        with pe.Fori(0, PAIRS) as i:
                            pe.wait_ge(s_w, i * 32 + 32)
                            pe.wait_ge(s_mx, i * NQ + 1)
                            for g in range(4):
                                for k in range(KT):
                                    ins = pe.matmul(bank[g], wqk[:, g // 2, k, :], hT[:, k, (g % 2) * HALF:(g % 2 + 1) * HALF], start=(k == 0), stop=(k == KT - 1))
                                ins.then_inc(s_pj, 1)
                                if g == 0:
                                    pe.wait_ge(s_e0, i * NQ + 1)
                                    pe.wait_ge(s_e1, i * TT + 1)
                                    pe.wait_ge(s_o, i * NQ + 1)
                                else:
                                    pe.wait_ge(s_sq, i * 4 + g)
                                    pe.matmul(bank[4 + g - 1], bd[:], sq[:, g - 1, :], start=True, stop=True).then_inc(s_mn, 1)
                            pe.wait_ge(s_sq, i * 4 + 4)
                            pe.matmul(bank[7], bd[:], sq[:, 3, :], start=True, stop=True).then_inc(s_mn, 1)
                            pe.wait_ge(s_qk, i * 4 + 4)
                            pe.wait_ge(s_rt, i * 4 + 4)

                            def logits(j):
                                h, t = divmod(j, TT)
                                b = 2 * (j % 2)
                                if j >= 2:
                                    pe.wait_ge(s_mx, i * NQ + j)
                                w = (t + 1) * P
                                for c in range(0, w, HALF):
                                    n = min(HALF, w - c)
                                    ins = pe.matmul(bank[b + c // HALF][:, 0:n], qp[:, h, t * P:(t + 1) * P], kT[:, c:c + n], start=True, stop=True)
                                ins.then_inc(s_lg, 1)

                            def turn(j):
                                h, t = divmod(j, TT)
                                pe.wait_ge(s_ex, i * NQ + j + 1)
                                pe.wait_ge(s_e0, i * NQ + j + 1)
                                for s in range(min(4, t + 1)):
                                    ins = pe.transpose(bank[4][:, s * P:(s + 1) * P], lg[:, j % 2, s * P:(s + 1) * P], ident[:])
                                ins.then_inc(s_t, 1)
                                if t >= 4:
                                    pe.wait_ge(s_e1, i * TT + 4 * h + t - 4 + 1)
                                    for s in range(4, t + 1):
                                        ins = pe.transpose(bank[5][:, (s - 4) * P:(s - 3) * P], lg[:, j % 2, s * P:(s + 1) * P], ident[:])
                                    ins.then_inc(s_t, 1)

                            def values(j):
                                h, t = divmod(j, TT)
                                if j == 0:
                                    pe.wait_ge(s_vp, i + 1)
                                pe.wait_ge(s_e0, i * NQ + j + 2)
                                if t >= 4:
                                    pe.wait_ge(s_e1, i * TT + 4 * h + t - 4 + 2)
                                pe.wait_ge(s_o, i * NQ + j)  if j >= 2 else None
                                for s in range(t + 1):
                                    ins = pe.matmul(bank[6 + j % 2][:, 0:DH], pT[:, j % 2, s, :], vp[:, s, h * DH:(h + 1) * DH], start=(s == 0), stop=(s == t))
                                ins.then_inc(s_pv, 1)

                            logits(0)
                            for j in range(NQ):
                                if j + 1 < NQ:
                                    logits(j + 1)
                                if j >= 1:
                                    values(j - 1)
                                turn(j)
                            values(NQ - 1)

                    @block.scalar
                    def _(act):
                        act.sem_inc(s_e0, 1)
                        act.wait_ge(s_c, 7)
                        with act.Fori(0, PAIRS) as i:
                            for g in range(4):
                                act.wait_ge(s_pj, i * 4 + g + 2)
                                act.activation(sq[:, g, :], bank[g], ACT.Square).then_inc(s_sq, 1)
                            for g in range(4):
                                act.wait_ge(s_mn, i * 4 + g + 1)
                                act.activation(sq[:, g, :], bank[4 + g], ACT.Sqrt, bias=epc[:]).then_inc(s_rt, 1)

                            def probs(j):
                                h, t = divmod(j, TT)
                                act.wait_ge(s_nm, i * NQ + j + 1)
                                act.wait_ge(s_rs, i * NQ + j + 1)
                                act.activation(lg[:, j % 2, 0:(t + 1) * P], lg[:, j % 2, 0:(t + 1) * P], ACT.Exp, bias=mx[:, j % 2, 2:3],
                                               accum_out=rsum[:, j % 2, 0:1]).then_inc(s_ex, 1)

                            def copy0(j):
                                h, t = divmod(j, TT)
                                act.wait_ge(s_t, i * (NQ + TT) + j + 4 * h + max(0, t - 4) + 1)
                                if j >= 2:
                                    act.wait_ge(s_pv, i * NQ + j)
                                n = min(4, t + 1)
                                act.activation(pT[:, j % 2, 0:n, :], bank[4][:, 0:n * P].rearrange("p (s t) -> p s t", t=P), ACT.Copy).then_inc(s_e0, 1)

                            for j in range(NQ):
                                probs(j)
                                if j >= 1:
                                    copy0(j - 1)
                            copy0(NQ - 1)

                    @block.vector
                    def _(dve):
                        dve.wait_ge(s_g, 64)
                        dve.tensor_scalar(gqs[:], gq[:, 0:1], DH ** -0.5, None, ALU.mult).then_inc(s_rs, 1)
                        dve.wait_ge(s_rs, 1)
                        dve.sem_inc(s_rs, 1)
                        dve.sem_inc(s_mx, 1)
                        dve.sem_inc(s_e1, 1)
                        dve.sem_inc(s_o, 1)
                        with dve.Fori(0, PAIRS) as i:
                            for g in range(4):
                                dve.wait_ge(s_rt, i * 4 + g + 1)
                                dve.reciprocal(sq[:, g, :], sq[:, g, :]).then_inc(s_rc, 1)
                                dve.wait_ge(s_rc, i * 4 + g + 1)
                                at = slice((g % 2) * HALF, (g % 2 + 1) * HALF)
                                if g < 2:
                                    dve.scalar_tensor_tensor(qp[0:DH, 0, at], bank[g][0:DH, :], gqs[0:DH], sq[0:DH, g, :], ALU.mult, ALU.mult)
                                    ins = dve.scalar_tensor_tensor(qp[DH:P, 1, at], bank[g][DH:P, :], gqs[DH:P], sq[DH:P, g, :], ALU.mult, ALU.mult)
                                else:
                                    ins = dve.scalar_tensor_tensor(kT[:, at], bank[g], gq[:, 1:2], sq[:, g, :], ALU.mult, ALU.mult)
                                ins.then_inc(s_qk, 1)
                            dve.wait_ge(s_nf, i * 32 + 32)
                            dve.wait_ge(s_nfd, i + 2)

                            def row_max(j):
                                h, t = divmod(j, TT)
                                b = 2 * (j % 2)
                                at = t * P
                                dve.wait_ge(s_lg, i * NQ + j + 1)
                                if j >= 2:
                                    dve.wait_ge(s_t, i * (NQ + TT) + (j - 1) + 4 * ((j - 2) // TT) + max(0, (j - 2) % TT - 3))
                                dve.sem_inc(s_own, 1)
                                row = psum[:, b:b + 2, :].rearrange("p b n -> p (b n)")
                                if t > 0:
                                    dve.tensor_tensor_reduce(lg[:, j % 2, 0:at], row[:, 0:at], nf[:, h, 0:at], 1.0, NEG, ALU.add, ALU.max, mx[:, j % 2, 0:1])
                                dve.tensor_tensor_reduce(lg[:, j % 2, at:at + P], row[:, at:at + P], nfd[:, h, at:at + P], 1.0,
                                                         NEG, ALU.add, ALU.max, mx[:, j % 2, 1:2]).then_inc(s_mx, 1)
                                dve.wait_ge(s_mx, i * NQ + j + 2)
                                if t > 0:
                                    dve.tensor_tensor(mx[:, j % 2, 3:4], mx[:, j % 2, 0:1], mx[:, j % 2, 1:2], ALU.max).then_inc(s_m1, 1)
                                    dve.wait_ge(s_m1, i * (NQ - 2) + j - h)
                                dve.tensor_scalar(mx[:, j % 2, 2:3], mx[:, j % 2, 3:4] if t > 0 else mx[:, j % 2, 1:2], -1.0, None, ALU.mult).then_inc(s_nm, 1)

                            def copy1(j):
                                h, t = divmod(j, TT)
                                if t >= 4:
                                    dve.wait_ge(s_t, i * (NQ + TT) + j + 4 * h + t - 4 + 2)
                                    if j >= 2:
                                        dve.wait_ge(s_pv, i * NQ + j)
                                    n = t - 3
                                    dve.tensor_copy(pT[:, j % 2, 4:4 + n, :], bank[5][:, 0:n * P].rearrange("p (s t) -> p s t", t=P)).then_inc(s_e1, 1)

                            def leave(j):
                                h, t = divmod(j, TT)
                                dve.wait_ge(s_ex, i * NQ + j + 1)
                                dve.reciprocal(rsum[:, j % 2, 1:2], rsum[:, j % 2, 0:1]).then_inc(s_rs, 1)
                                dve.wait_ge(s_rs, i * NQ + j + 3)
                                dve.wait_ge(s_pv, i * NQ + j + 2)
                                dve.tensor_scalar(x3[:, t, bass.ds(i * P + h * DH, DH)], bank[6 + j % 2][:, 0:DH], rsum[:, j % 2, 1:2], None, ALU.mult).then_inc(s_o, 1)

                            row_max(0)
                            for j in range(NQ):
                                if j + 1 < NQ:
                                    row_max(j + 1)
                                if j >= 1:
                                    leave(j - 1)
                                copy1(j)
                            leave(NQ - 1)

        with ExitStack() as c2:
            oT = hT
            wo = sbuf(c2, "fox_w_out", [P, KT, D])
            mix = sbuf(c2, "fox_mix", [P, 2, HALF])
            s_w, s_x, s_t, s_c, s_m, s_g, s_r = [sem("p_" + n) for n in ("weights", "x2", "turned", "copied", "mm", "gated", "residual")]
            with nc.Block() as block:
                @block.sync
                def _(sp):
                    sp.dma_start(wo[:], a["fox_w_out_2"][0].rearrange("(p k) n -> p k n", k=KT)).then_inc(s_w, 16)
                    sp.wait_ge(s_t, 2 * TT)
                    sp.dma_start(x3[:], x2_dram.rearrange("(t p) n -> p t n", p=P)).then_inc(s_x, 16)

                @block.tensor
                def _(pe):
                    for t in range(TT):
                        for g in range(2):
                            if t >= 2:
                                pe.wait_ge(s_c, 2 * (t - 2) + g + 1)
                            for k in range(4 * g, 4 * g + 4):
                                ins = pe.transpose(bank[g + 2 * (t % 2)][:, (k % 4) * P:(k % 4 + 1) * P], x3[:, t, k:D:KT], ident[:])
                            ins.then_inc(s_t, 1)
                    pe.wait_ge(s_c, 2 * TT)
                    pe.wait_ge(s_w, 16)
                    for i in range(2 * TT):
                        t, hf = divmod(i, 2)
                        if i >= 4:
                            pe.wait_ge(s_g, i - 3)
                        for k in range(KT):
                            ins = pe.matmul(bank[4 + i % 4], oT[:, k, t * P:(t + 1) * P], wo[:, k, hf * HALF:(hf + 1) * HALF], start=(k == 0), stop=(k == KT - 1))
                        ins.then_inc(s_m, 1)

                @block.vector
                def _(dve):
                    for t in range(TT):
                        for g in range(2):
                            dve.wait_ge(s_t, 2 * t + g + 1)
                            dve.tensor_copy(oT[:, 4 * g:4 * g + 4, t * P:(t + 1) * P],
                                            bank[g + 2 * (t % 2)].rearrange("p (k t) -> p k t", t=P)).then_inc(s_c, 1)
                    dve.wait_ge(s_x, 16)
                    for i in range(2 * TT):
                        t, hf = divmod(i, 2)
                        at = slice(hf * HALF, (hf + 1) * HALF)
                        dve.wait_ge(s_m, i + 1)
                        dve.tensor_tensor(mix[:, i % 2, :], bank[4 + i % 4], gates[:, 2, at], ALU.mult).then_inc(s_g, 1)
                        dve.wait_ge(s_g, i + 1)
                        dve.tensor_tensor(x3[:, t, at], x3[:, t, at], mix[:, i % 2, :], ALU.add).then_inc(s_r, 1)


def mlp(nc, a, sbuf, sem, bank, ident, ones, mhalf, gates, colmod, x3, hTh, hTl, out):
    W = 2 * P
    NB = FF // W
    NO = 2 * TT
    with ExitStack() as c2:
        with ExitStack() as c3:
            norm_turn(nc, c3, "n", sbuf, sem, bank, ident, mhalf, colmod[:, 1, 3, :], colmod[:, 1, 2, :], hTh, hTl, x3, None)
        w1 = sbuf(c2, "w_mlp_in", [P, KT, W])
        w1h = sbuf(c2, "w_mlp_in_high", [P, 2, KT, W], F32R)
        w1l = sbuf(c2, "w_mlp_in_low", [P, 2, KT, W], F32R)
        w2 = sbuf(c2, "w_mlp_out", [P, 2, D])
        w2h = sbuf(c2, "w_mlp_out_high", [P, 2, D], F32R)
        w2l = sbuf(c2, "w_mlp_out_low", [P, 2, D], F32R)
        gTh = sbuf(c2, "hiddenT_high", [P, 2, S], F32R)
        gTl = sbuf(c2, "hiddenT_low", [P, 2, S], F32R)
        rl = sbuf(c2, "relu", [P, 2, HALF])
        gf = sbuf(c2, "relu_squared", [P, 2, HALF])
        s_own, s_out = sem("h_carrier"), sem("h_stored")
        l1, l2 = sem("h_w1"), sem("h_w2")
        s_w1h, s_w1l, s_w2s, s_w2h, s_w2l = [sem("h_" + n) for n in ("w1_high", "w1_low", "w2_scaled", "w2_high", "w2_low")]
        s_h, s_rl, s_sq, s_gh, s_gl, s_o, s_r = [sem("h_" + n) for n in ("hidden", "relu", "squared", "g_high", "g_low", "out", "residual")]
        w1_d = a["w_mlp_in_2"][0].rearrange("(p k) n -> p k n", k=KT)
        w2_d = a["w_mlp_out_2"][0].rearrange("(f p) n -> p f n", p=P)
        groups = [(0, 0), (1, 0), (0, 1), (1, 1)]

        def over_blocks(eng, body):
            with eng.Fori(0, NB // 2 - 1) as i:
                for u in range(2):
                    body(i * 2 + u, u, False)
            for u in range(2):
                body(NB - 2 + u, u, u == 1)

        with nc.Block() as block:
            @block.sync
            def _(sp):
                def load(n, u, last):
                    sp.wait_ge(s_w1l, n + 1)
                    sp.sem_inc(s_own, 1)
                    sp.dma_start(w1[:], w1_d[:, :, bass.ds(n * W, W)]).then_inc(l1, 16)
                    sp.wait_ge(s_w2l, n + 1)
                    sp.sem_inc(s_own, 1)
                    sp.dma_start(w2[:], w2_d[:, bass.ds(n * 2, 2), :]).then_inc(l2, 16)

                over_blocks(sp, load)
                for t in range(TT):
                    sp.wait_ge(s_r, (NB - 1) * NO + 2 * t + 2 + 4)
                    sp.dma_start(out[0, t * P:(t + 1) * P, :], x3[:, t, :]).then_inc(s_out, 16)
                sp.wait_ge(s_out, 16 * TT)

            @block.tensor
            def _(pe):
                pe.sem_inc(s_h, 1)
                pe.sem_inc(s_o, 1)

                def products(n, u, last):
                    pe.wait_ge(s_w1l, n + 2)
                    for g, (m, hf) in enumerate(groups):
                        pe.wait_ge(s_rl, n * 4 + g + 1)
                        at = slice(hf * HALF, (hf + 1) * HALF)
                        for k in range(KT):
                            ins = split_mm(pe, bank[g], (w1h[:, u, k, m * P:(m + 1) * P], w1l[:, u, k, m * P:(m + 1) * P]),
                                           (hTh[:, k, at], hTl[:, k, at]), k == 0, k == KT - 1)
                        ins.then_inc(s_h, 1)
                    pe.wait_ge(s_w2l, n + 2)
                    for j in range(NO):
                        t, hf = divmod(j, 2)
                        if j == 0:
                            pe.wait_ge(s_gl, n * 4 + 2 + 4)
                        if t == 4 and hf == 0:
                            pe.wait_ge(s_gl, n * 4 + 4 + 4)
                        pe.wait_ge(s_r, n * NO + j + 1)
                        for m in range(2):
                            ins = split_mm(pe, bank[4 + j % 4], (gTh[:, m, t * P:(t + 1) * P], gTl[:, m, t * P:(t + 1) * P]),
                                           (w2h[:, m, hf * HALF:(hf + 1) * HALF], w2l[:, m, hf * HALF:(hf + 1) * HALF]), m == 0, m == 1)
                        ins.then_inc(s_o, 1)

                over_blocks(pe, products)

            @block.scalar
            def _(act):
                act.sem_inc(s_rl, 4)

                def high1(n, u):
                    act.wait_ge(l1, n * 16 + 16)
                    act.activation(w1h[:, u], w1[:], ACT.Copy).then_inc(s_w1h, 1)

                def step(n, u, last):
                    act.wait_ge(s_w2s, n + 1)
                    act.wait_ge(s_o, n * NO + 1)
                    act.activation(w2h[:], w2[:], ACT.Copy).then_inc(s_w2h, 1)
                    for g in range(5):
                        if g < 4:
                            act.wait_ge(s_h, n * 4 + g + 2)
                            act.wait_ge(s_sq, n * 4 + g + 1)
                            act.activation(rl[:, g % 2, :], bank[g], ACT.Relu).then_inc(s_rl, 1)
                        if g >= 1:
                            m, hf = groups[g - 1]
                            act.wait_ge(s_sq, n * 4 + g + 2)
                            act.activation(gTh[:, m, hf * HALF:(hf + 1) * HALF], gf[:, (g - 1) % 2, :], ACT.Copy).then_inc(s_gh, 1)
                    if not last:
                        high1(n + 1, 1 - u)

                high1(0, 0)
                over_blocks(act, step)

            @block.vector
            def _(dve):
                dve.sem_inc(s_w1l, 1)
                dve.sem_inc(s_w2l, 1)
                dve.sem_inc(s_sq, 2)
                dve.sem_inc(s_gl, 4)
                dve.sem_inc(s_r, 4)

                def low1(n, u):
                    dve.wait_ge(s_w1h, n + 1)
                    dve.tensor_tensor(w1l[:, u], w1[:], w1h[:, u].bitcast(F32), ALU.subtract).then_inc(s_w1l, 1)

                def step(n, u, last):
                    dve.wait_ge(l2, n * 16 + 16)
                    dve.tensor_tensor(w2[:], w2[:], gates[:, 3, :].unsqueeze(1).to_broadcast([P, 2, D]), ALU.mult).then_inc(s_w2s, 1)
                    dve.wait_ge(s_w2h, n + 1)
                    dve.tensor_tensor(w2l[:], w2[:], w2h[:].bitcast(F32), ALU.subtract).then_inc(s_w2l, 1)
                    for g in range(5):
                        if g < 4:
                            dve.wait_ge(s_rl, n * 4 + g + 5)
                            dve.wait_ge(s_gl, n * 4 + g + 3)
                            dve.tensor_tensor(gf[:, g % 2, :], rl[:, g % 2, :], rl[:, g % 2, :], ALU.mult).then_inc(s_sq, 1)
                        if g >= 1:
                            m, hf = groups[g - 1]
                            dve.wait_ge(s_gh, n * 4 + g)
                            dve.tensor_tensor(gTl[:, m, hf * HALF:(hf + 1) * HALF], gf[:, (g - 1) % 2, :],
                                              gTh[:, m, hf * HALF:(hf + 1) * HALF].bitcast(F32), ALU.subtract).then_inc(s_gl, 1)
                    if not last:
                        low1(n + 1, 1 - u)
                    for j in range(NO):
                        t, hf = divmod(j, 2)
                        at = slice(hf * HALF, (hf + 1) * HALF)
                        dve.wait_ge(s_o, n * NO + j + 2)
                        dve.tensor_tensor(x3[:, t, at], x3[:, t, at], bank[4 + j % 4], ALU.add).then_inc(s_r, 1)

                low1(0, 0)
                over_blocks(dve, step)


def kernel(**inputs):
    import concourse.bacc as bacc
    import numpy as np
    from concourse.bass_utils import run_bass_kernel_spmd

    nc = bacc.Bacc("TRN2", target_bir_lowering=False, num_devices=1)
    arrays, aps = {}, {}
    for name, value in inputs.items():
        value = np.ascontiguousarray(value)
        if not value.size:
            continue
        arrays["in_" + name] = value
        aps[name] = nc.dram_tensor("in_" + name, value.shape, mybir.dt.from_np(value.dtype), kind="ExternalInput").ap()
    out = nc.dram_tensor("out", [1, S, D], F32, kind="ExternalOutput").ap()
    build(nc, aps, out)
    return run_bass_kernel_spmd(nc, [arrays], core_ids=[0]).results[0]["out"]
```

```python
from contextlib import ExitStack

import concourse.bass as bass
from concourse import mybir

F32 = mybir.dt.float32
F32R = mybir.dt.float32r
I32 = mybir.dt.int32
U32 = mybir.dt.uint32
BF16 = mybir.dt.bfloat16
ALU = mybir.AluOpType
ACT = mybir.ActivationFunctionType
X = mybir.AxisListType.X

P = 128
S = 1024
D = 1024
TT = S // P
KT = D // P
HALF = 512
EPS = 1e-6
ROOT_D = float(D) ** 0.5
NEG = -3.0e38

HM = 4
POOL_PAD = 16
CW = 4

NE = 32
EG = 4
EPG = NE // EG
DE = 512
JT = DE // P
MINB = S * 2 // P
MAXB = S * 2 // P + NE

HF = 16
DH = 64
PAIRS = HF // 2
FF = 4096
FB = FF // HALF


def build(nc, a, out):
    top = ExitStack()
    with top:
        def sbuf(ctx, name, shape, dt=F32):
            return ctx.enter_context(nc.sbuf_tensor(name, shape, dt))

        def phase(f, *more):
            sems = []

            def sem(name):
                sems.append(nc.alloc_semaphore(name))
                return sems[-1]

            f(nc, a, sbuf, sem, bank, ident, ones, mhalf, gates, colmod, *more)
            nc.clear_and_free_semaphores(sems)
            nc.all_engine_barrier()

        psum = top.enter_context(nc.psum_tensor("psum", [P, 8, HALF], F32))
        bank = [psum[:, i, :] for i in range(8)]

        ident = sbuf(top, "ident", [P, P])
        ones = sbuf(top, "ones", [P, P])
        gates = sbuf(top, "gates", [P, 4, D])
        colmod = sbuf(top, "colmod", [P, 2, 4, KT])
        mhalf = sbuf(top, "minus_half", [P, 1])

        normed_dram = nc.dram_tensor("normed_rows", [S, D], F32, kind="Internal").ap()
        slots_dram = nc.dram_tensor("slot_tokens", [P * MAXB, 1], I32, kind="Internal").ap()
        moe_dram = nc.dram_tensor("expert_rows", [MAXB * P, D], F32, kind="Internal").ap()
        negf_dram = nc.dram_tensor("minus_log_forget", [HF, S], F32, kind="Internal").ap()
        heads_dram = nc.dram_tensor("heads_outputs", [D, S], F32, kind="Internal").ap()
        x2_dram = nc.dram_tensor("second_residual", [S, D], F32, kind="Internal").ap()

        phase(modulation)
        with ExitStack() as xs:
            x1 = sbuf(xs, "x1", [P, TT, D])
            phase(mixer, x1, moe_dram)
            phase(moe, x1, normed_dram, slots_dram, moe_dram, x2_dram)
        phase(attention, psum, x2_dram, negf_dram, heads_dram)
        with ExitStack() as xs:
            x3 = sbuf(xs, "x3", [P, TT, D])
            phase(fox_out, x2_dram, heads_dram, x3)
            hTh = sbuf(xs, "hT_high", [P, KT, S], F32R)
            hTl = sbuf(xs, "hT_low", [P, KT, S], F32R)
            phase(mlp, x3, hTh, hTl, out)


def modulation(nc, a, sbuf, sem, bank, ident, ones, mhalf, gates, colmod):
    with ExitStack() as ctx:
        ws = sbuf(ctx, "ada_rows", [P, 2, 6 * D])
        acc = sbuf(ctx, "ada_acc", [P, 2, 6 * D])
        brow = sbuf(ctx, "ada_bias_row", [1, 2, 6 * D])
        ccol = sbuf(ctx, "c_col", [P, 2, KT])
        csil = sbuf(ctx, "c_silu", [P, 2, KT])
        bcol = sbuf(ctx, "ada_bias_col", [P, 2, 6, KT])
        gcol = sbuf(ctx, "norm_gain_col", [P, 2, 2, KT])
        tcol = sbuf(ctx, "mod_col", [P, 2, 4, KT])
        par, row0, row1 = sem("m_params"), sem("m_rows0"), sem("m_rows1")
        rows = [row0, row1]
        csilu, macc, red, modc, modg, idm = (sem("m_silu"), sem("m_acc"), sem("m_reduced"), sem("m_cols"), sem("m_gates"), sem("m_ident"))
        w = [a["ada_w"], a["w_ada_2"]]
        b = [a["ada_b"], a["b_ada_2"]]
        gains = [[a["norm1_g"], a["norm2_g"]], [a["norm_mix_2"], a["norm_mlp_2"]]]
        with nc.Block() as block:
            @block.sync
            def _(sp):
                for l, c in enumerate((a["c"], a["c_2"])):
                    sp.dma_start(ccol[:, l, :], c[0].rearrange("(p k) -> p k", k=KT)).then_inc(par, 16)
                for j in range(2 * KT):
                    l, k = divmod(j, KT)
                    if j >= 2:
                        sp.wait_ge(macc, j - 1)
                    sp.dma_start(ws[:, j % 2, :], w[l][0].rearrange("(p k) n -> p k n", k=KT)[:, k, :]).then_inc(rows[j % 2], 16)

            @block.scalar
            def _(act):
                for l in range(2):
                    act.dma_start(bcol[:, l], b[l][0].rearrange("(q p k) -> p q k", p=P, k=KT)).then_inc(par, 16)
                    act.dma_start(brow[:, l, :], b[l]).then_inc(par, 16)
                    for g in range(2):
                        act.dma_start(gcol[:, l, g, :], gains[l][g][0].rearrange("(p k) -> p k", k=KT)).then_inc(par, 16)
                act.wait_ge(par, 16 * 10)
                act.activation(csil[:], ccol[:], ACT.Silu).then_inc(csilu, 1)

            @block.gpsimd
            def _(pool):
                pool.memset(ident[:], 0.0).then_inc(idm, 1)
                pool.memset(ones[:], 1.0).then_inc(idm, 1)
                pool.memset(mhalf[:], -0.5).then_inc(idm, 1)
                pool.wait_ge(idm, 3)
                pool.affine_select(out=ident[:], in_=ident[:], compare_op=ALU.not_equal, fill=1.0, base=0,
                                   pattern=[[-1, P]], channel_multiplier=1).then_inc(idm, 1)

            @block.vector
            def _(dve):
                dve.wait_ge(csilu, 1)
                for j in range(2 * KT):
                    l, k = divmod(j, KT)
                    dve.wait_ge(rows[j % 2], 16 * (j // 2 + 1))
                    if k == 0:
                        dve.tensor_scalar(acc[:, l, :], ws[:, j % 2, :], csil[:, l, k:k + 1], None, ALU.mult).then_inc(macc, 1)
                    else:
                        dve.wait_ge(macc, j)
                        dve.scalar_tensor_tensor(acc[:, l, :], ws[:, j % 2, :], csil[:, l, k:k + 1], acc[:, l, :],
                                                 ALU.mult, ALU.add).then_inc(macc, 1)
                for l in range(2):
                    dve.wait_ge(red, 5 * l + 1)
                    dve.tensor_tensor(tcol[:, l, 0:2, :], bank[4 + l][:, l * 32:l * 32 + 16].rearrange("p (q k) -> p q k", k=KT),
                                      bcol[:, l, 0:2, :], ALU.add).then_inc(modc, 1)
                    dve.tensor_tensor(tcol[:, l, 2:4, :], bank[4 + l][:, l * 32 + 16:l * 32 + 32].rearrange("p (q k) -> p q k", k=KT),
                                      bcol[:, l, 3:5, :], ALU.add).then_inc(modc, 1)
                    dve.wait_ge(modc, 6 * l + 2)
                    for g in range(2):
                        dve.tensor_copy(colmod[:, l, 2 * g, :], tcol[:, l, 2 * g, :]).then_inc(modc, 1)
                        dve.scalar_tensor_tensor(colmod[:, l, 2 * g + 1, :], tcol[:, l, 2 * g + 1, :], 1.0, gcol[:, l, g, :],
                                                 ALU.add, ALU.mult).then_inc(modc, 1)
                    for n in range(4):
                        dve.wait_ge(red, 5 * l + 2 + n)
                        dve.tensor_copy(gates[:, 2 * l + n // 2, (n % 2) * HALF:(n % 2 + 1) * HALF], bank[n][:]).then_inc(modg, 1)

            @block.tensor
            def _(pe):
                pe.wait_ge(idm, 4)
                pe.wait_ge(par, 16 * 10)
                for l in range(2):
                    pe.wait_ge(macc, KT * (l + 1))
                    for qi, q in enumerate((0, 1, 3, 4)):
                        for k in range(KT):
                            m = pe.matmul(bank[4 + l][:, l * 32 + qi * KT + k:l * 32 + qi * KT + k + 1],
                                          acc[:, l, q * D + k:(q + 1) * D:KT], ones[:, 0:1], start=True, stop=True)
                    m.then_inc(red, 1)
                    for n in range(4):
                        if l == 1:
                            pe.wait_ge(modg, n + 1)
                        at = (2 + 3 * (n // 2)) * D + (n % 2) * HALF
                        pe.matmul(bank[n][:], ones[:], acc[:, l, at:at + HALF], start=True, stop=False)
                        pe.matmul(bank[n][:], ones[0:1, :], brow[:, l, at:at + HALF], start=False, stop=True).then_inc(red, 1)


def mixer(nc, a, sbuf, sem, bank, ident, ones, mhalf, gates, colmod, x1, moe_dram):
    w_in = a["w_in"][0]
    w_in_pk = w_in.rearrange("(p k) n -> p k n", k=KT)
    DM = HM * P
    with ExitStack() as ctx:
        ucT = sbuf(ctx, "ucT", [P, HM, S])
        sgo = sbuf(ctx, "sigmoid_oT", [P, HM, S])
        vaug = sbuf(ctx, "v_aug", [P, TT, HM, P + 1])
        yT = sbuf(ctx, "yT", [P, 2 * HM, S])
        prow = sbuf(ctx, "param_rows", [36, P])
        pcol = sbuf(ctx, "param_cols", [P, 36])
        zrow = x1[0:HM, 6:8, :]
        bif = sbuf(ctx, "gate_bias", [HM, 2])
        par = sem("x_params")
        with ExitStack() as c2:
            hT = sbuf(c2, "hT", [P, KT, S])
            wb = sbuf(c2, "w_in_block", [P, 2, KT, HALF])
            wg = sbuf(c2, "w_in_gates", [P, KT, 36])
            wgl = sbuf(c2, "w_in_gates_loaded", [P, KT, 8])
            uT = yT[:, 0:HM, :]
            pp = yT[:, HM:2 * HM, :]
            stat = sbuf(c2, "stat", [P, TT, 2])
            xn = ucT[:, 0:2, :]
            sq = ucT[:, 2, :]
            xl, xs, nr, tr, hv = [sem("x_load0"), sem("x_load1")], sem("x_square"), sem("x_normed"), sem("x_turned"), sem("x_hT")
            xst, xse = sem("x_stat"), sem("x_eps")
            wl = [sem("x_w0"), sem("x_w1")]
            wgd, mm, ev, z, cv, padz = sem("x_wgates"), sem("x_proj"), sem("x_evac"), sem("x_zero"), sem("x_conv"), sem("x_padz")
            pc = sem("x_pcol")
            cols = [0, 2 * DM, 4 * 128 * 3 + 8, DM]
            with nc.Block() as block:
                @block.sync
                def _(sp):
                    for t in range(TT):
                        if t >= 2:
                            sp.wait_ge(nr, t - 1)
                        sp.dma_start(x1[:, t, :], a["x"][0, t * P:(t + 1) * P, :]).then_inc(xl[t % 2], 16)
                    for n in range(4):
                        if n >= 2:
                            sp.wait_ge(mm, 8 * (n - 1))
                        sp.dma_start(wb[:, n % 2], w_in_pk[:, :, cols[n]:cols[n] + HALF]).then_inc(wl[n % 2], 16)

                @block.gpsimd
                def _(pool):
                    for t in range(TT):
                        pool.wait_ge(xs, t + 1)
                        pool.tensor_scalar(stat[:, t, 0:1], stat[:, t, 0:1], D * EPS, None, ALU.add).then_inc(xse, 1)
                        pool.wait_ge(xse, t + 1)
                        pool.tensor_tensor(stat[:, t, 1:2], stat[:, t, 0:1], mhalf[:], ALU.pow).then_inc(xst, 1)
                    pool.memset(wg[:], 0.0).then_inc(z, 1)
                    pool.memset(vaug[:, :, :, P:P + 1], 1.0).then_inc(z, 1)
                    pool.wait_ge(wgd, 16)
                    pool.wait_ge(z, 2)
                    pool.tensor_copy(wg[:, :, 0:HM], wgl[:, :, 0:HM]).then_inc(z, 1)
                    pool.tensor_copy(wg[:, :, 32:32 + HM], wgl[:, :, HM:2 * HM]).then_inc(z, 1)

                @block.scalar
                def _(act):
                    act.dma_start(prow[0:16, :], a["conv_w"][0].rearrange("w (t p) -> (w t) p", p=P)).then_inc(par, 16)
                    for n, name in enumerate(("conv_b", "mlstm_norm_g", "mlstm_skip", "b_pool", "pool_scale")):
                        act.dma_start(prow[16 + 4 * n:20 + 4 * n, :], a[name][0].rearrange("(t p) -> t p", p=P)).then_inc(par, 16)
                    act.dma_start(bif[:, 0:1], a["b_igate"][0].rearrange("(h o) -> h o", o=1)).then_inc(par, 16)
                    act.dma_start(bif[:, 1:2], a["b_fgate"][0].rearrange("(h o) -> h o", o=1)).then_inc(par, 16)
                    act.dma_start(wgl[:], w_in_pk[:, :, 3 * DM:3 * DM + 8]).then_inc(wgd, 16)
                    for t in range(TT):
                        act.wait_ge(xl[t % 2], 16 * (t // 2 + 1))
                        if t >= 1:
                            act.wait_ge(xs, t)
                        act.activation(sq, x1[:, t, :], ACT.Square, accum_out=stat[:, t, 0:1]).then_inc(xs, 1)
                    for n in range(4):
                        for i in range(8):
                            act.wait_ge(mm, 8 * n + i + 1)
                            src = bank[2 + (8 * n + i) % 4][:]
                            m, hf = divmod(i, 2)
                            if n == 0:
                                ins = act.activation(uT[:, m, hf * HALF:(hf + 1) * HALF], src, ACT.Copy)
                            elif n == 1:
                                ins = act.activation(sgo[:, m, hf * HALF:(hf + 1) * HALF], src, ACT.Sigmoid)
                            elif n == 2:
                                ins = act.activation(pp[:, m, hf * HALF:(hf + 1) * HALF], src, ACT.Copy)
                            else:
                                ins = act.activation(vaug[:, i, :, 0:P], src.rearrange("p (h e) -> p h e", h=HM), ACT.Copy)
                            ins.then_inc(ev, 1)
                    act.wait_ge(par, 16 * 8)
                    for hf in range(2):
                        act.wait_ge(mm, 33 + hf)
                        for g in range(2):
                            act.activation(zrow[:, g, hf * HALF:(hf + 1) * HALF], bank[hf][32 * g:32 * g + HM, :], ACT.Identity,
                                           bias=bif[:, g:g + 1]).then_inc(ev, 1)
                    for m in range(HM):
                        act.wait_ge(cv, 4 * (m + 1))
                        act.activation(ucT[:, m, :], ucT[:, m, :], ACT.Silu, bias=pcol[:, 16 + m:17 + m]).then_inc(ev, 1)

                @block.vector
                def _(dve):
                    for t in range(TT):
                        dve.wait_ge(xst, t + 1)
                        if t >= 2:
                            dve.wait_ge(tr, 2 * (t - 1))
                        dve.tensor_scalar(xn[:, t % 2, :], x1[:, t, :], stat[:, t, 1:2], ROOT_D, ALU.mult, ALU.mult).then_inc(nr, 1)
                        for g in range(2):
                            dve.wait_ge(tr, 2 * t + g + 1)
                            for k in range(4 * g, 4 * g + 4):
                                ins = dve.tensor_scalar(hT[:, k, t * P:(t + 1) * P], bank[g][:, (k % 4) * P:(k % 4 + 1) * P],
                                                        colmod[:, 0, 1, k:k + 1], colmod[:, 0, 0, k:k + 1], ALU.mult, ALU.add)
                            ins.then_inc(hv, 1)
                    dve.wait_ge(pc, 1)
                    dve.tensor_copy(pcol[:], bank[6][:, 0:36]).then_inc(pc, 1)
                    dve.wait_ge(pc, 2)
                    dve.wait_ge(ev, 8)
                    for m in range(HM):
                        for j in range(CW):
                            src = uT[:, m, 0:S - j]
                            tap = pcol[:, 4 * (CW - 1 - j) + m:4 * (CW - 1 - j) + m + 1]
                            if j == 0:
                                dve.tensor_scalar(ucT[:, m, :], src, tap, None, ALU.mult).then_inc(cv, 1)
                            else:
                                dve.wait_ge(cv, 4 * m + j)
                                dve.scalar_tensor_tensor(ucT[:, m, j:], src, tap, ucT[:, m, j:], ALU.mult, ALU.add).then_inc(cv, 1)

                @block.tensor
                def _(pe):
                    for t in range(TT):
                        pe.wait_ge(nr, t + 1)
                        for g in range(2):
                            if t >= 1:
                                pe.wait_ge(hv, 2 * (t - 1) + g + 1)
                            for k in range(4 * g, 4 * g + 4):
                                ins = pe.transpose(bank[g][:, (k % 4) * P:(k % 4 + 1) * P], xn[:, t % 2, k:D:KT], ident[:])
                            ins.then_inc(tr, 1)
                    pe.wait_ge(hv, 2 * TT)
                    pe.wait_ge(par, 16 * 8)
                    pe.transpose(bank[6][:, 0:36], prow[:], ident[0:36, 0:36]).then_inc(pc, 1)
                    for n in range(4):
                        pe.wait_ge(wl[n % 2], 16 * (n // 2 + 1))
                        for i in range(8):
                            g = 8 * n + i
                            if g >= 4:
                                pe.wait_ge(ev, g - 3)
                            m, hf = divmod(i, 2)
                            for k in range(KT):
                                if n < 3:
                                    ins = pe.matmul(bank[2 + g % 4][:], wb[:, n % 2, k, m * P:(m + 1) * P], hT[:, k, hf * HALF:(hf + 1) * HALF],
                                                    start=(k == 0), stop=(k == KT - 1))
                                else:
                                    ins = pe.matmul(bank[2 + g % 4][:], hT[:, k, i * P:(i + 1) * P], wb[:, n % 2, k, :],
                                                    start=(k == 0), stop=(k == KT - 1))
                            ins.then_inc(mm, 1)
                    pe.wait_ge(z, 4)
                    for hf in range(2):
                        for k in range(KT):
                            ins = pe.matmul(bank[hf][0:36, :], wg[:, k, :], hT[:, k, hf * HALF:(hf + 1) * HALF], start=(k == 0), stop=(k == KT - 1))
                        ins.then_inc(mm, 1)

        NC_ = TT
        with ExitStack() as c2:
            qT = sbuf(c2, "qT", [P, HM, S])
            kT = sbuf(c2, "kT", [P, HM, S])
            ktok = sbuf(c2, "k_tok", [P, TT, HM, P])
            wq = sbuf(c2, "wq", [P, HM, P])
            wk = sbuf(c2, "wk", [P, HM, P])
            wp = sbuf(c2, "wpool", [P, HM, P])
            rr = x1[0:HM, 0:6, :]
            negM = rr[:, 1, :]
            packed = sbuf(c2, "packed_rows", [P, S])
            pk = sbuf(c2, "packed_cols", [P, TT, P])
            mprev = sbuf(c2, "m_prev", [HM, NC_])
            aprev = sbuf(c2, "a_prev", [HM, NC_])
            aprb = sbuf(c2, "a_prev_all", [P, HM, NC_])
            sel = sbuf(c2, "select_head", [HM, HM, P])
            NM = x1[:, 2:6, :]
            cmask = sbuf(c2, "causal", [P, P])
            state = sbuf(c2, "state", [P, HM, P + 1])
            lw = sem("c_w")
            rw = sem("c_rows")
            rdy = sem("c_ready")
            q1, q2 = sem("c_qk"), sem("c_qkev")
            g1, g2 = sem("c_setup"), sem("c_setup_done")
            pl = sem("c_pool")
            pm, pe_v = sem("c_poolmm"), sem("c_poolev")
            rowexp = sem("c_rowexp")
            with ExitStack() as c3:
                ps2 = sbuf(c3, "pool_sums", [P, 2, POOL_PAD + S])
                fix = sbuf(c3, "pool_fix", [P, HM, 16])
                with nc.Block() as block:
                    @block.sync
                    def _(sp):
                        sp.dma_start(wq[:], a["w_q"][0].rearrange("h d e -> d h e")).then_inc(lw, 16)
                        sp.dma_start(wk[:], a["w_k"][0].rearrange("h d e -> d h e")).then_inc(lw, 16)
                        sp.dma_start(wp[:], a["w_pool"][0].rearrange("g c d -> c g d")).then_inc(lw, 16)

                    @block.tensor
                    def _(pe):
                        pe.wait_ge(lw, 48)
                        n = 0
                        for h in range(HM):
                            for w_, in ((wq,), (wk,)):
                                for hf in range(2):
                                    if n >= 4:
                                        pe.wait_ge(q2, n - 3)
                                    pe.matmul(bank[(n + 2) % 4][:], w_[:, h, :], ucT[:, h, hf * HALF:(hf + 1) * HALF], start=True, stop=True).then_inc(q1, 1)
                                    n += 1
                        for t in range(TT):
                            pe.wait_ge(q2, n - 3)
                            for h in range(HM):
                                ins = pe.matmul(bank[(n + 2) % 4][:, h * P:(h + 1) * P], ucT[:, h, t * P:(t + 1) * P], wk[:, h, :], start=True, stop=True)
                            ins.then_inc(q1, 1)
                            n += 1
                        pe.wait_ge(g1, 8)
                        for t in range(TT):
                            if t in (4,):
                                pe.wait_ge(g2, 1)
                            ins = pe.transpose(bank[4][:, (t % 4) * P:(t % 4 + 1) * P], packed[:, t * P:(t + 1) * P], ident[:])
                            if t % 4 == 3:
                                ins.then_inc(rdy, 1)
                        pe.wait_ge(g1, 9)
                        for h in range(HM):
                            ins = pe.matmul(bank[5][:, h * NC_:(h + 1) * NC_], sel[:, h, :], aprev[:], start=True, stop=True)
                        ins.then_inc(rdy, 1)
                        n = 0
                        for h in range(HM):
                            for hf in range(2):
                                if n >= 2:
                                    pe.wait_ge(g2, 3 + n - 1)
                                pe.matmul(bank[6 + n % 2][:], sel[:, h, :], negM[:, hf * HALF:(hf + 1) * HALF], start=True, stop=True).then_inc(rdy, 1)
                                n += 1
                        pe.wait_ge(q2, 24)
                        for g in range(HM):
                            pe.wait_ge(pl, g + 1)
                            for hf in range(2):
                                if g >= 1:
                                    pe.wait_ge(pe_v, 2 * (g - 1) + hf + 1)
                                pe.matmul(bank[2 + hf][:], wp[:, g, :], yT[:, HM + g, hf * HALF:(hf + 1) * HALF], start=True, stop=True).then_inc(pm, 1)

                    @block.gpsimd
                    def _(pool):
                        pool.memset(packed[:], 0.0).then_inc(rw, 1)
                        pool.memset(rr[:, 5, :], 1.0).then_inc(rw, 1)
                        pool.memset(sel[:], 0.0).then_inc(rw, 1)
                        pool.memset(cmask[:], 0.0).then_inc(rw, 1)
                        pool.memset(mprev[:], 0.0).then_inc(rw, 1)
                        pool.memset(ps2[:, :, 0:POOL_PAD], 0.0).then_inc(rw, 1)
                        pool.iota(fix[:], [[0, HM], [1, 16]], base=1, channel_multiplier=0, allow_small_or_imprecise_dtypes=True).then_inc(rw, 1)
                        pool.wait_ge(rw, 7)
                        pool.memset(rr[:, 5, 0:S:P], 0.0).then_inc(rw, 1)
                        pool.affine_select(out=sel[:], in_=sel[:], compare_op=ALU.not_equal, fill=1.0, base=0,
                                           pattern=[[-1, HM], [0, P]], channel_multiplier=1).then_inc(rw, 1)
                        pool.affine_select(out=cmask[:], in_=cmask[:], compare_op=ALU.is_ge, fill=NEG, base=0,
                                           pattern=[[1, P]], channel_multiplier=-1).then_inc(rw, 1)

                    @block.scalar
                    def _(act):
                        n = 0
                        for h in range(HM):
                            for dst, sc in ((qT, P ** -0.5), (kT, 1.0)):
                                for hf in range(2):
                                    act.wait_ge(q1, n + 1)
                                    act.activation(dst[:, h, hf * HALF:(hf + 1) * HALF], bank[(n + 2) % 4][:], ACT.Copy, scale=sc).then_inc(q2, 1)
                                    n += 1
                            if h == 0:
                                act.wait_ge(g1, 1)
                                act.activation(rr[:, 1, :], rr[:, 0, :], ACT.Exp, scale=-1.0).then_inc(rowexp, 1)
                                act.wait_ge(rowexp, 1)
                                act.activation(rr[:, 0, :], rr[:, 1, :], ACT.Ln, bias=1.0).then_inc(rowexp, 1)
                            if h == 2:
                                act.wait_ge(g1, 5)
                                act.activation(packed[32:32 + HM, :], rr[:, 0, :], ACT.Exp).then_inc(g1, 1)
                                act.activation(packed[64:64 + HM, :], rr[:, 2, :], ACT.Exp, scale=-1.0).then_inc(g1, 1)
                                act.activation(packed[96:96 + HM, :], rr[:, 4, :], ACT.Exp).then_inc(g1, 1)
                                act.activation(aprev[:], aprev[:], ACT.Exp).then_inc(g1, 1)
                        for t in range(TT):
                            act.wait_ge(q1, n + 1)
                            act.activation(ktok[:, t], bank[(n + 2) % 4][:].rearrange("p (h e) -> p h e", h=HM), ACT.Copy).then_inc(q2, 1)
                            n += 1
                        for g in range(HM):
                            for hf in range(2):
                                act.wait_ge(pm, 2 * g + hf + 1)
                                act.activation(yT[:, HM + g, hf * HALF:(hf + 1) * HALF], bank[2 + hf][:], ACT.Identity,
                                               bias=pcol[:, 28 + g:29 + g]).then_inc(pe_v, 1)

                    @block.vector
                    def _(dve):
                        ch = [0]

                        def link(ins):
                            ins.then_inc(chain, 1)
                            ch[0] += 1
                            dve.wait_ge(chain, ch[0])

                        chain = sem("c_chain")
                        dve.wait_ge(rw, 10)
                        zi, zf = zrow[:, 0, :], zrow[:, 1, :]
                        dve.scalar_tensor_tensor(rr[:, 0, :], zf, -1.0, zf, ALU.mult, ALU.max).then_inc(g1, 1)
                        dve.wait_ge(rowexp, 2)
                        link(dve.scalar_tensor_tensor(rr[:, 1, :], zf, 0.0, rr[:, 0, :], ALU.min, ALU.subtract))
                        dve.tensor_tensor_scan(rr[:, 0, :], rr[:, 5, :], rr[:, 1, :], 0.0, ALU.mult, ALU.add)
                        link(dve.tensor_tensor_scan(rr[:, 2, :], rr[:, 1, :], zi, 0.0, ALU.add, ALU.max))
                        dve.tensor_tensor(packed[0:HM, :], zi, rr[:, 0, :], ALU.subtract)
                        dve.tensor_copy(mprev[:, 1:NC_], rr[:, 2, P - 1:S - P:P])
                        link(dve.tensor_tensor(rr[:, 3, :], rr[:, 2, :], rr[:, 0, :], ALU.subtract))
                        dve.tensor_scalar(negM, rr[:, 3, :], -1.0, None, ALU.mult).then_inc(g1, 1)
                        M3 = rr[:, 3, :].rearrange("h (c t) -> h c t", t=P)
                        last = rr[:, 3, P - 1:S:P]
                        dve.tensor_tensor(rr[:, 0, :].rearrange("h (c t) -> h c t", t=P), mprev[:].unsqueeze(2).to_broadcast([HM, NC_, P]),
                                          M3, ALU.subtract).then_inc(g1, 1)
                        dve.tensor_tensor(rr[:, 4, :].rearrange("h (c t) -> h c t", t=P), packed[0:HM, :].rearrange("h (c t) -> h c t", t=P),
                                          last.unsqueeze(2).to_broadcast([HM, NC_, P]), ALU.subtract).then_inc(g1, 1)
                        dve.tensor_tensor(aprev[:], mprev[:], last, ALU.subtract).then_inc(g1, 1)
                        link(dve.reciprocal(fix[:], fix[:]))
                        for g in range(HM):
                            win = 2 << g
                            link(dve.tensor_scalar(fix[:, g, :], fix[:, g, :], float(win), 1.0, ALU.mult, ALU.max))
                            link(dve.tensor_copy(ps2[:, 0, POOL_PAD:], yT[:, HM + g, :]))
                            src = 0
                            for j in range(g + 1):
                                link(dve.tensor_tensor(ps2[:, 1 - src, POOL_PAD:], ps2[:, src, POOL_PAD:],
                                                       ps2[:, src, POOL_PAD - (1 << j):POOL_PAD + S - (1 << j)], ALU.add))
                                src = 1 - src
                            link(dve.tensor_tensor(ps2[:, src, POOL_PAD:POOL_PAD + 16], ps2[:, src, POOL_PAD:POOL_PAD + 16], fix[:, g, :], ALU.mult))
                            dve.scalar_tensor_tensor(yT[:, HM + g, :], ps2[:, src, POOL_PAD:], 1.0 / win, yT[:, HM + g, :],
                                                     ALU.mult, ALU.subtract).then_inc(pl, 1)
                            dve.wait_ge(pl, g + 1)
                        for half in range(2):
                            dve.wait_ge(rdy, half + 1)
                            dve.tensor_copy(pk[:, 4 * half:4 * half + 4, :], bank[4][:].rearrange("p (t r) -> p t r", r=P)).then_inc(g2, 1)
                        dve.wait_ge(rdy, 3)
                        dve.tensor_copy(aprb[:], bank[5][:, 0:HM * NC_].rearrange("p (h c) -> p h c", c=NC_)).then_inc(g2, 1)
                        for n in range(8):
                            dve.wait_ge(rdy, 4 + n)
                            dve.tensor_copy(NM[:, n // 2, (n % 2) * HALF:(n % 2 + 1) * HALF], bank[6 + n % 2][:]).then_inc(g2, 1)
                        for g in range(HM):
                            dve.wait_ge(pe_v, 2 * g + 2)
                            dve.tensor_scalar(yT[:, HM + g, :], yT[:, HM + g, :], pcol[:, 32 + g:33 + g], None, ALU.mult).then_inc(pl, 1)
            with ExitStack() as c3:
                dl = sbuf(c3, "decay_log", [P, 2, P])
                de = sbuf(c3, "decay", [P, 2, P])
                st = sbuf(c3, "scores", [P, 2, P])
                vw = sbuf(c3, "v_weighted", [P, 2, P + 1])
                num = sbuf(c3, "num", [P, 2, P + 1])
                hn = sbuf(c3, "h_normed", [P, 2, P])
                hsq = sbuf(c3, "h_square", [P, 2, P])
                cst = sbuf(c3, "cell_stats", [P, 2, 6])
                inter = sbuf(c3, "inter", [P, 2, P + 1])
                ymix = sbuf(c3, "ymix", [P, 2, P])
                zrows = x1[:, 7, :]
                s_dl, s_de, s_qk, s_st, s_vw = sem("r_decaylog"), sem("r_decay"), sem("r_qk"), sem("r_scores"), sem("r_vw")
                s_ni, s_num, s_sq, s_hn, s_tr, s_up, s_y = sem("r_ni"), sem("r_num"), sem("r_sq"), sem("r_hn"), sem("r_tr"), sem("r_state"), sem("r_y")
                s_den, s_int, s_yc, s_ch = sem("r_den"), sem("r_inter"), sem("r_yc"), sem("r_chain")
                s_rs, s_se = sem("r_rstd"), sem("r_eps")
                steps = [(c, h) for c in range(NC_) for h in range(HM)]
                N = len(steps)
                s_zf, s_zd = sem("r_zeros"), sem("r_zeros_stored")
                with nc.Block() as block:
                    @block.sync
                    def _(sp):
                        sp.wait_ge(s_zf, 1)
                        sp.dma_start(moe_dram[MINB * P:, :].rearrange("(b p) n -> p b n", p=P),
                                     zrows[:].unsqueeze(1).to_broadcast([P, MAXB - MINB, D])).then_inc(s_zd, 16)
                        sp.wait_ge(s_zd, 16)

                    @block.tensor
                    def _(pe):
                        def scores(i):
                            c, h = steps[i]
                            if i >= 2:
                                pe.wait_ge(s_st, i - 1)
                            pe.matmul(bank[i % 2][:, 0:P], kT[:, h, c * P:(c + 1) * P], qT[:, h, c * P:(c + 1) * P], start=True, stop=True).then_inc(s_qk, 1)

                        def turn(i):
                            if i >= 2:
                                pe.wait_ge(s_y, i - 1)
                            pe.wait_ge(s_hn, i + 1)
                            pe.transpose(bank[6 + i % 2][:, 0:P], hn[:, i % 2, :], ident[:]).then_inc(s_tr, 1)

                        scores(0)
                        for i, (c, h) in enumerate(steps):
                            if i + 1 < N:
                                scores(i + 1)
                            pe.wait_ge(s_vw, i + 1)
                            if i >= 2:
                                pe.wait_ge(s_num, i - 1)
                                pe.wait_ge(s_up, i - 1)
                            if c >= 1:
                                pe.wait_ge(s_up, i - HM + 1)
                                pe.matmul(bank[2 + i % 2][:, 256:256 + P + 1], qT[:, h, c * P:(c + 1) * P], state[:, h, :], start=True, stop=True)
                            pe.matmul(bank[4 + i % 2][:, 0:P + 1], ktok[:, c, h, :], vw[:, i % 2, :], start=True, stop=True)
                            pe.wait_ge(s_st, i + 1)
                            pe.matmul(bank[2 + i % 2][:, 0:P + 1], st[:, i % 2, :], vaug[:, c, h, :], start=True, stop=True).then_inc(s_ni, 1)
                            if i >= 1:
                                turn(i - 1)
                        turn(N - 1)

                    @block.scalar
                    def _(act):
                        def decay(i):
                            act.wait_ge(s_dl, i + 1)
                            if i >= 2:
                                act.wait_ge(s_st, i - 1)
                            act.activation(de[:, i % 2, :], dl[:, i % 2, :], ACT.Exp).then_inc(s_de, 1)
                            c, h = steps[i]
                            if i >= 2:
                                act.wait_ge(s_ni, i - 1)
                            act.activation(vw[:, i % 2, :], vaug[:, c, h, :], ACT.Copy, scale=pk[:, c, 96 + h:97 + h]).then_inc(s_vw, 1)

                        decay(0)
                        for i in range(N):
                            if i + 1 < N:
                                decay(i + 1)
                            act.wait_ge(s_den, i + 1)
                            act.activation(hsq[:, i % 2, :], num[:, i % 2, 0:P], ACT.Square, scale=cst[:, i % 2, 1:2],
                                           accum_out=cst[:, i % 2, 2:3]).then_inc(s_sq, 1)

                    @block.gpsimd
                    def _(pool):
                        pool.memset(zrows[:], 0.0).then_inc(s_zf, 1)
                        for i in range(N):
                            pool.wait_ge(s_sq, i + 1)
                            if i >= 2:
                                pool.wait_ge(s_ch, 3 * (i - 2) + 3)
                            pool.tensor_scalar(cst[:, i % 2, 3:4], cst[:, i % 2, 2:3], P * EPS, None, ALU.add).then_inc(s_se, 1)
                            pool.wait_ge(s_se, i + 1)
                            pool.tensor_tensor(cst[:, i % 2, 4:5], cst[:, i % 2, 3:4], mhalf[:], ALU.pow).then_inc(s_rs, 1)

                    @block.vector
                    def _(dve):
                        def decay_log(i):
                            c, h = steps[i]
                            if i >= 2:
                                dve.wait_ge(s_de, i - 1)
                            dve.scalar_tensor_tensor(dl[:, i % 2, :], NM[:, h, c * P:(c + 1) * P], pk[:, c, h:h + 1], cmask[:],
                                                     ALU.add, ALU.add).then_inc(s_dl, 1)

                        def weigh(i):
                            dve.wait_ge(s_de, i + 1)
                            dve.wait_ge(s_qk, i + 1)
                            if i >= 2:
                                dve.wait_ge(s_ni, i - 1)
                            dve.tensor_tensor(st[:, i % 2, :], bank[i % 2][:, 0:P], de[:, i % 2, :], ALU.mult).then_inc(s_st, 1)

                        def finish(i):
                            c, h = steps[i]
                            at = slice(c * P, (c + 1) * P)
                            dve.tensor_scalar(ymix[:, i % 2, :], ucT[:, h, at], pcol[:, 24 + h:25 + h], None, ALU.mult).then_inc(s_yc, 1)
                            dve.wait_ge(s_tr, i + 1)
                            dve.wait_ge(s_yc, 2 * i + 1)
                            dve.scalar_tensor_tensor(ymix[:, i % 2, :], bank[6 + i % 2][:, 0:P], pcol[:, 20 + h:21 + h], ymix[:, i % 2, :],
                                                     ALU.mult, ALU.add).then_inc(s_yc, 1)
                            dve.wait_ge(s_yc, 2 * i + 2)
                            dve.tensor_tensor(yT[:, h, at], ymix[:, i % 2, :], sgo[:, h, at], ALU.mult).then_inc(s_y, 1)

                        decay_log(0)
                        decay_log(1)
                        weigh(0)
                        for i, (c, h) in enumerate(steps):
                            if i + 2 < N:
                                decay_log(i + 2)
                            if i + 1 < N:
                                weigh(i + 1)
                            b = i % 2
                            dve.wait_ge(s_ni, i + 1)
                            if i >= 2:
                                dve.wait_ge(s_sq, i - 1)
                            intra = bank[2 + b][:, 0:P + 1]
                            if c == 0:
                                dve.tensor_copy(num[:, b, :], intra).then_inc(s_num, 1)
                                dve.tensor_copy(state[:, h, :], bank[4 + b][:, 0:P + 1]).then_inc(s_up, 1)
                            else:
                                dve.tensor_scalar(inter[:, b, :], bank[2 + b][:, 256:256 + P + 1], pk[:, c, 32 + h:33 + h], None, ALU.mult).then_inc(s_int, 1)
                                dve.wait_ge(s_int, i - HM + 1)
                                dve.tensor_tensor(num[:, b, :], intra, inter[:, b, :], ALU.add).then_inc(s_num, 1)
                                dve.scalar_tensor_tensor(state[:, h, :], state[:, h, :], aprb[:, h, c:c + 1], bank[4 + b][:, 0:P + 1],
                                                         ALU.mult, ALU.add).then_inc(s_up, 1)
                            dve.wait_ge(s_num, i + 1)
                            dve.scalar_tensor_tensor(cst[:, b, 0:1], num[:, b, P:P + 1], -1.0, pk[:, c, 64 + h:65 + h], ALU.mult, ALU.max).then_inc(s_ch, 1)
                            dve.wait_ge(s_ch, 3 * i + 1)
                            dve.tensor_tensor(cst[:, b, 0:1], cst[:, b, 0:1], num[:, b, P:P + 1], ALU.max).then_inc(s_ch, 1)
                            dve.wait_ge(s_ch, 3 * i + 2)
                            dve.reciprocal(cst[:, b, 1:2], cst[:, b, 0:1]).then_inc(s_den, 1)
                            if i >= 1:
                                finish(i - 1)
                            dve.wait_ge(s_rs, i + 1)
                            dve.scalar_tensor_tensor(cst[:, b, 5:6], cst[:, b, 4:5], float(P) ** 0.5, cst[:, b, 1:2],
                                                     ALU.mult, ALU.mult).then_inc(s_ch, 1)
                            dve.wait_ge(s_ch, 3 * i + 3)
                            if i >= 2:
                                dve.wait_ge(s_tr, i - 1)
                            dve.tensor_scalar(hn[:, b, :], num[:, b, 0:P], cst[:, b, 5:6], None, ALU.mult).then_inc(s_hn, 1)
                        finish(N - 1)

        with ExitStack() as c2:
            wo = sbuf(c2, "w_out", [P, KT, D])
            mix = sbuf(c2, "mix", [P, 2, HALF])
            w_l, x_l, w_m, w_t, w_x = sem("o_w"), sem("o_x"), sem("o_mm"), sem("o_tmp"), sem("o_x1")
            with nc.Block() as block:
                @block.sync
                def _(sp):
                    sp.dma_start(wo[:], a["w_out"][0].rearrange("(k p) n -> p k n", p=P)).then_inc(w_l, 16)
                    sp.dma_start(x1[:], a["x"][0].rearrange("(t p) n -> p t n", p=P)).then_inc(x_l, 16)

                @block.tensor
                def _(pe):
                    pe.wait_ge(w_l, 16)
                    for i in range(2 * TT):
                        t, hf = divmod(i, 2)
                        if i >= 4:
                            pe.wait_ge(w_t, i - 3)
                        for k in range(KT):
                            ins = pe.matmul(bank[i % 4][:], yT[:, k, t * P:(t + 1) * P], wo[:, k, hf * HALF:(hf + 1) * HALF],
                                            start=(k == 0), stop=(k == KT - 1))
                        ins.then_inc(w_m, 1)

                @block.vector
                def _(dve):
                    dve.wait_ge(x_l, 16)
                    for i in range(2 * TT):
                        t, hf = divmod(i, 2)
                        at = slice(hf * HALF, (hf + 1) * HALF)
                        dve.wait_ge(w_m, i + 1)
                        dve.tensor_tensor(mix[:, i % 2, :], bank[i % 4][:], gates[:, 0, at], ALU.mult).then_inc(w_t, 1)
                        dve.wait_ge(w_t, i + 1)
                        dve.tensor_tensor(x1[:, t, at], x1[:, t, at], mix[:, i % 2, :], ALU.add).then_inc(w_x, 1)


def moe(nc, a, sbuf, sem, bank, ident, ones, mhalf, gates, colmod, x1, normed_dram, slots_dram, moe_dram, x2_out):
    NG = EG + NE
    with ExitStack() as ctx:
        rows_i = sbuf(ctx, "slot_rows", [P, TT, 2], I32)
        gate2 = sbuf(ctx, "token_gates", [P, TT, 2])
        slots = sbuf(ctx, "slots", [P, MAXB + 1], I32)
        bexp = sbuf(ctx, "block_expert", [1, MAXB], I32)
        npair = sbuf(ctx, "block_pairs", [1, 1], I32)
        logits = sbuf(ctx, "logits", [P, TT, NG])
        stat = sbuf(ctx, "moe_stat", [P, TT, 2])

        with ExitStack() as c2:
            sq = sbuf(c2, "moe_sq", [P, D])
            xn = sbuf(c2, "moe_xn", [P, 2, D])
            hTt = sbuf(c2, "moe_hT", [P, 2, KT, P])
            wr = sbuf(c2, "w_router", [P, KT, NG])
            br = sbuf(c2, "b_router", [1, NG])
            s_w, s_sq, s_e, s_rs, s_xn, s_tr, s_ht, s_lg, s_lc = [sem("g_" + n) for n in
                ("weights", "square", "eps", "rstd", "normed", "turned", "hT", "logits", "copied")]
            s_st = [sem("g_store0"), sem("g_store1")]
            with nc.Block() as block:
                @block.sync
                def _(sp):
                    sp.dma_start(wr[:, :, 0:EG], a["w_router_group"][0].rearrange("(p k) n -> p k n", k=KT)).then_inc(s_w, 16)
                    sp.dma_start(wr[:, :, EG:NG], a["w_router_expert"][0].rearrange("(p k) n -> p k n", k=KT)).then_inc(s_w, 16)
                    sp.dma_start(br[:, 0:EG], a["b_router_group"]).then_inc(s_w, 16)
                    sp.dma_start(br[:, EG:NG], a["b_router_expert"]).then_inc(s_w, 16)
                    for t in range(TT):
                        sp.wait_ge(s_xn, t + 1)
                        sp.dma_start(normed_dram[t * P:(t + 1) * P, :], xn[:, t % 2, :]).then_inc(s_st[t % 2], 16)
                    for u in range(2):
                        sp.wait_ge(s_st[u], 16 * (TT // 2))

                @block.scalar
                def _(act):
                    for t in range(TT):
                        if t >= 1:
                            act.wait_ge(s_sq, t)
                        act.activation(sq[:], x1[:, t, :], ACT.Square, accum_out=stat[:, t, 0:1]).then_inc(s_sq, 1)

                @block.gpsimd
                def _(pool):
                    for t in range(TT):
                        pool.wait_ge(s_sq, t + 1)
                        pool.tensor_scalar(stat[:, t, 0:1], stat[:, t, 0:1], D * EPS, None, ALU.add).then_inc(s_e, 1)
                        pool.wait_ge(s_e, t + 1)
                        pool.tensor_tensor(stat[:, t, 1:2], stat[:, t, 0:1], mhalf[:], ALU.pow).then_inc(s_rs, 1)

                @block.vector
                def _(dve):
                    def copy_logits(t):
                        dve.wait_ge(s_lg, t + 1)
                        dve.tensor_copy(logits[:, t, :], bank[4 + t % 2][:, 0:NG]).then_inc(s_lc, 1)

                    for t in range(TT):
                        dve.wait_ge(s_rs, t + 1)
                        if t >= 2:
                            dve.wait_ge(s_tr, 2 * (t - 1))
                            dve.wait_ge(s_st[t % 2], 16 * (t // 2))
                        dve.tensor_scalar(xn[:, t % 2, :], x1[:, t, :], stat[:, t, 1:2], ROOT_D, ALU.mult, ALU.mult).then_inc(s_xn, 1)
                        if t >= 2:
                            dve.wait_ge(s_lg, t - 1)
                        for g in range(2):
                            dve.wait_ge(s_tr, 2 * t + g + 1)
                            for k in range(4 * g, 4 * g + 4):
                                ins = dve.tensor_scalar(hTt[:, t % 2, k, :], bank[g + 2 * (t % 2)][:, (k % 4) * P:(k % 4 + 1) * P],
                                                        colmod[:, 0, 3, k:k + 1], colmod[:, 0, 2, k:k + 1], ALU.mult, ALU.add)
                            ins.then_inc(s_ht, 1)
                        if t >= 1:
                            copy_logits(t - 1)
                    copy_logits(TT - 1)

                @block.tensor
                def _(pe):
                    pe.wait_ge(s_w, 64)

                    def route(t):
                        pe.wait_ge(s_ht, 2 * t + 2)
                        if t >= 2:
                            pe.wait_ge(s_lc, t - 1)
                        for k in range(KT):
                            pe.matmul(bank[4 + t % 2][:, 0:NG], hTt[:, t % 2, k, :], wr[:, k, :], start=(k == 0), stop=False)
                        pe.matmul(bank[4 + t % 2][:, 0:NG], ones[0:1, :], br[:], start=False, stop=True).then_inc(s_lg, 1)

                    for t in range(TT):
                        pe.wait_ge(s_xn, t + 1)
                        if t >= 2:
                            pe.wait_ge(s_ht, 2 * (t - 1))
                        for g in range(2):
                            for k in range(4 * g, 4 * g + 4):
                                ins = pe.transpose(bank[g + 2 * (t % 2)][:, (k % 4) * P:(k % 4 + 1) * P], xn[:, t % 2, k:D:KT], ident[:])
                            ins.then_inc(s_tr, 1)
                        if t >= 1:
                            route(t - 1)
                    route(TT - 1)

        with ExitStack() as c2:
            gl8 = sbuf(c2, "group_logits", [P, TT, 8])
            gm8 = sbuf(c2, "group_max", [P, TT, 8])
            gi8 = sbuf(c2, "group_index", [P, TT, 8], U32)
            gif = sbuf(c2, "group_of_token", [P, TT])
            gex = sbuf(c2, "group_exp", [P, TT, EG])
            gs = sbuf(c2, "group_gate", [P, TT])
            io = sbuf(c2, "iota_32", [P, NE])
            iob = sbuf(c2, "iota_blocks", [1, MAXB])
            iop = sbuf(c2, "iota_pairs", [1, MAXB // 2])
            oh4 = sbuf(c2, "group_onehot", [P, TT, EG])
            prod = sbuf(c2, "group_product", [P, TT, EG, EPG])
            es = sbuf(c2, "expert_logits", [P, TT, EPG])
            em8 = sbuf(c2, "expert_max", [P, TT, 8])
            ei8 = sbuf(c2, "expert_index", [P, TT, 8], U32)
            eif = sbuf(c2, "expert_of_token", [P, TT, 2])
            ed = sbuf(c2, "second_exp", [P, TT])
            er = sbuf(c2, "first_share", [P, TT])
            oh = sbuf(c2, "expert_onehot", [P, 2, TT, NE])
            mem = sbuf(c2, "membership", [P, TT, NE], BF16)
            before = sbuf(c2, "before", [P, P], BF16)
            onesb = sbuf(c2, "ones_bf16", [P, P], BF16)
            rank = sbuf(c2, "rank_all", [P, TT, NE])
            cnt = sbuf(c2, "counts", [P, NE])
            nb = sbuf(c2, "expert_blocks", [P, NE])
            ends = sbuf(c2, "block_ends", [P, NE])
            starts = sbuf(c2, "block_starts", [P, NE])
            onerow = sbuf(c2, "ones_row", [P, NE])
            t3 = sbuf(c2, "onehot_product", [P, TT, NE])
            rk = sbuf(c2, "rank", [P, 2, TT])
            sb_ = sbuf(c2, "start_block", [P, 2, TT])
            jj = sbuf(c2, "block_in_expert", [P, 2, TT])
            fslot = sbuf(c2, "slot_float", [P, 2, TT])
            slot_i = sbuf(c2, "slot_int", [P, 2, TT], I32)
            tok_i = sbuf(c2, "token_id", [P, TT], I32)
            zer = sbuf(c2, "zero_slots", [P, MAXB], I32)
            cmp_ = sbuf(c2, "block_compare", [1, MAXB, NE])
            bf = sbuf(c2, "block_expert_float", [1, MAXB])
            pf = sbuf(c2, "pair_compare", [1, MAXB // 2])
            pn = sbuf(c2, "pair_float", [1, 1])
            s_c, s_ex, s_m, s_rk, s_ch, s_sl, s_z, s_sc, s_ld = [sem("t_" + n) for n in
                ("consts", "exps", "member", "ranks", "chain", "slots", "zeroed", "scattered", "loaded")]
            s_go = sem("t_go")
            with nc.Block() as block:
                @block.gpsimd
                def _(pool):
                    pool.iota(io[:], [[1, NE]], base=0, channel_multiplier=0, allow_small_or_imprecise_dtypes=True).then_inc(s_c, 1)
                    pool.iota(iob[:], [[1, MAXB]], base=0, channel_multiplier=0, allow_small_or_imprecise_dtypes=True).then_inc(s_c, 1)
                    pool.iota(iop[:], [[2, MAXB // 2]], base=0, channel_multiplier=0, allow_small_or_imprecise_dtypes=True).then_inc(s_c, 1)
                    pool.iota(tok_i[:], [[P, TT]], base=0, channel_multiplier=1).then_inc(s_c, 1)
                    pool.memset(before[:], 1.0).then_inc(s_c, 1)
                    pool.memset(onesb[:], 1.0).then_inc(s_c, 1)
                    pool.memset(onerow[:], 1.0).then_inc(s_c, 1)
                    pool.memset(zer[:], 0).then_inc(s_c, 1)
                    pool.memset(slots[:, MAXB:MAXB + 1], 0).then_inc(s_c, 1)
                    pool.wait_ge(s_c, 9)
                    pool.affine_select(out=before[:], in_=before[:], compare_op=ALU.is_gt, fill=0.0, base=0,
                                       pattern=[[1, P]], channel_multiplier=-1).then_inc(s_c, 1)
                    pool.wait_ge(s_z, 16)
                    pool.wait_ge(s_sl, 1)
                    for k in range(2):
                        for t in range(TT):
                            pool.indirect_dma_start(slots_dram, bass.IndirectOffsetOnAxis(ap=slot_i[:, k, t:t + 1], axis=0),
                                                    tok_i[:, t:t + 1], None).then_inc(s_sc, 16)

                @block.sync
                def _(sp):
                    sp.wait_ge(s_c, 9)
                    sp.dma_start(slots_dram.rearrange("(p b) o -> p (b o)", b=MAXB), zer[:]).then_inc(s_z, 16)
                    sp.wait_ge(s_sc, 16 * 2 * TT)
                    sp.dma_start(slots[:, 0:MAXB], slots_dram.rearrange("(p b) o -> p (b o)", b=MAXB)).then_inc(s_ld, 16)
                    sp.wait_ge(s_ld, 16)

                @block.scalar
                def _(act):
                    act.wait_ge(s_go, 1)
                    act.activation(gex[:], gex[:], ACT.Exp).then_inc(s_ex, 1)
                    act.wait_ge(s_go, 2)
                    act.activation(ed[:], ed[:], ACT.Exp).then_inc(s_ex, 1)

                @block.tensor
                def _(pe):
                    pe.wait_ge(s_c, 10)
                    pe.wait_ge(s_m, 1)
                    for t in range(TT):
                        for j in range(t + 1):
                            pe.matmul(bank[0][:, t * NE:(t + 1) * NE], before[:] if j == t else onesb[:], mem[:, j, :],
                                      start=(j == 0), stop=(j == t))
                    for t in range(TT):
                        ins = pe.matmul(bank[1][:, 0:NE], onesb[:], mem[:, t, :], start=(t == 0), stop=(t == TT - 1))
                    ins.then_inc(s_rk, 1)

                @block.vector
                def _(dve):
                    ch = [0]

                    def link(ins):
                        ins.then_inc(s_ch, 1)
                        ch[0] += 1
                        dve.wait_ge(s_ch, ch[0])

                    def over(x, n):
                        return x.unsqueeze(len(x.shape)).to_broadcast([*x.shape, n])

                    dve.wait_ge(s_c, 10)
                    link(dve.memset(gl8[:], NEG))
                    link(dve.tensor_copy(gl8[:, :, 0:EG], logits[:, :, 0:EG]))
                    for t in range(TT):
                        ins = dve.max(gm8[:, t, :], gl8[:, t, :])
                    link(ins)
                    for t in range(TT):
                        ins = dve.max_index(gi8[:, t, :], gm8[:, t, :], gl8[:, t, :])
                    link(ins)
                    dve.tensor_tensor(gex[:], gl8[:, :, 0:EG], over(gm8[:, :, 0], EG), ALU.subtract).then_inc(s_go, 1)
                    link(dve.tensor_copy(gif[:], gi8[:, :, 0]))
                    link(dve.tensor_tensor(oh4[:], io[:, 0:EG].unsqueeze(1).to_broadcast([P, TT, EG]), over(gif[:], EG), ALU.is_equal))
                    link(dve.tensor_tensor(prod[:], logits[:, :, EG:NG].rearrange("p t (g e) -> p t g e", g=EG), over(oh4[:], EPG), ALU.mult))
                    link(dve.tensor_tensor(es[:], prod[:, :, 0, :], prod[:, :, 1, :], ALU.add))
                    link(dve.tensor_tensor(es[:], es[:], prod[:, :, 2, :], ALU.add))
                    link(dve.tensor_tensor(es[:], es[:], prod[:, :, 3, :], ALU.add))
                    for t in range(TT):
                        ins = dve.max(em8[:, t, :], es[:, t, :])
                    link(ins)
                    for t in range(TT):
                        ins = dve.max_index(ei8[:, t, :], em8[:, t, :], es[:, t, :])
                    link(ins)
                    dve.tensor_tensor(ed[:], em8[:, :, 1], em8[:, :, 0], ALU.subtract).then_inc(s_go, 1)
                    link(dve.tensor_copy(eif[:], ei8[:, :, 0:2]))
                    link(dve.scalar_tensor_tensor(eif[:], over(gif[:], 2), float(EPG), eif[:], ALU.mult, ALU.add))
                    for k in range(2):
                        ins = dve.tensor_tensor(oh[:, k], io[:].unsqueeze(1).to_broadcast([P, TT, NE]), over(eif[:, :, k], NE), ALU.is_equal)
                        link(ins)
                    dve.tensor_tensor(mem[:], oh[:, 0], oh[:, 1], ALU.add).then_inc(s_m, 1)
                    dve.wait_ge(s_ex, 2)
                    link(dve.tensor_reduce(gs[:], gex[:], X, ALU.add))
                    link(dve.tensor_scalar(er[:], ed[:], 1.0, None, ALU.add))
                    link(dve.tensor_tensor(er[:], er[:], gs[:], ALU.mult))
                    link(dve.reciprocal(gate2[:, :, 0], er[:]))
                    link(dve.tensor_tensor(gate2[:, :, 1], gate2[:, :, 0], ed[:], ALU.mult))
                    dve.wait_ge(s_rk, 1)
                    link(dve.tensor_copy(rank[:], bank[0][:, 0:TT * NE].rearrange("p (t e) -> p t e", e=NE)))
                    link(dve.tensor_copy(cnt[:], bank[1][:, 0:NE]))
                    link(dve.tensor_scalar(nb[:], cnt[:], 0.0, None, ALU.is_gt))
                    for j in range(1, TT):
                        link(dve.scalar_tensor_tensor(nb[:], cnt[:], float(P * j), nb[:], ALU.is_gt, ALU.add))
                    link(dve.tensor_tensor_scan(ends[:], onerow[:], nb[:], 0.0, ALU.mult, ALU.add))
                    link(dve.tensor_tensor(starts[:], ends[:], nb[:], ALU.subtract))
                    for k in range(2):
                        link(dve.tensor_tensor(t3[:], oh[:, k], rank[:], ALU.mult))
                        link(dve.tensor_reduce(rk[:, k], t3[:], X, ALU.add))
                        link(dve.tensor_tensor(t3[:], oh[:, k], starts[:].unsqueeze(1).to_broadcast([P, TT, NE]), ALU.mult))
                        link(dve.tensor_reduce(sb_[:, k], t3[:], X, ALU.add))
                    link(dve.tensor_scalar(jj[:], rk[:], float(P), None, ALU.is_ge))
                    for j in range(2, TT):
                        link(dve.scalar_tensor_tensor(jj[:], rk[:], float(P * j), jj[:], ALU.is_ge, ALU.add))
                    link(dve.tensor_tensor(sb_[:], sb_[:], jj[:], ALU.add))
                    link(dve.scalar_tensor_tensor(rk[:], jj[:], -float(P), rk[:], ALU.mult, ALU.add))
                    link(dve.scalar_tensor_tensor(fslot[:], rk[:], float(MAXB), sb_[:], ALU.mult, ALU.add))
                    dve.tensor_copy(slot_i[:], fslot[:]).then_inc(s_sl, 1)
                    dve.wait_ge(s_sl, 1)
                    link(dve.scalar_tensor_tensor(fslot[:], sb_[:], float(P), rk[:], ALU.mult, ALU.add))
                    link(dve.tensor_copy(rows_i[:].rearrange("p t k -> p k t"), fslot[:]))
                    link(dve.tensor_tensor(cmp_[:], ends[0:1, :].unsqueeze(1).to_broadcast([1, MAXB, NE]), over(iob[:], NE), ALU.is_le))
                    link(dve.tensor_reduce(bf[:], cmp_[:], X, ALU.add))
                    link(dve.tensor_scalar(bf[:], bf[:], float(NE - 1), None, ALU.min))
                    link(dve.tensor_copy(bexp[:], bf[:]))
                    link(dve.tensor_scalar(pf[:], iop[:], ends[0:1, NE - 1:NE], None, ALU.is_lt))
                    link(dve.tensor_reduce(pn[:], pf[:], X, ALU.add))
                    link(dve.tensor_scalar(pn[:], pn[:], -1.0, None, ALU.add))
                    link(dve.tensor_copy(npair[:], pn[:]))

        with ExitStack() as c2:
            WE = KT * DE
            raw = {m: sbuf(c2, "w_" + m, [P, WE]) for m in ("gate", "up", "down")}
            wh = sbuf(c2, "w_high", [P, 2, WE], F32R)
            wl = sbuf(c2, "w_low", [P, 2, WE], F32R)
            xg = sbuf(c2, "gathered", [P, 2, D])
            hf32 = sbuf(c2, "block_h", [P, KT, P])
            hTh = sbuf(c2, "block_hT_high", [P, KT, P], F32R)
            hTl = sbuf(c2, "block_hT_low", [P, KT, P], F32R)
            sg = sbuf(c2, "silu", [P, DE])
            gg = sbuf(c2, "gated", [P, DE])
            gTh = sbuf(c2, "gatedT_high", [P, JT, P], F32R)
            gTl = sbuf(c2, "gatedT_low", [P, JT, P], F32R)
            ob = sbuf(c2, "block_out", [P, 2, D])
            idx = sbuf(c2, "block_index", [P, 2], I32)
            ld = {m: sem("b_load_" + m) for m in raw}
            s_ix, s_tr, s_ht, s_hh, s_hl = [sem("b_" + n) for n in ("index", "turned", "h", "h_high", "h_low")]
            s_wh, s_wl, s_us = [sem("b_" + n) for n in ("w_high", "w_low", "w_used")]
            s_sg, s_gg, s_gt, s_gh, s_gl, s_ob = [sem("b_" + n) for n in ("silu", "gated", "gatedT", "g_high", "g_low", "out_copied")]
            s_own, s_own2 = sem("b_carrier"), sem("b_carrier2")
            s_x = [sem("b_gather0"), sem("b_gather1")]
            s_out = [sem("b_store0"), sem("b_store1")]
            dram = {"gate": a["w_expert_gate"][0].rearrange("e (p k) n -> e p (k n)", k=KT),
                    "up": a["w_expert_up"][0].rearrange("e (p k) n -> e p (k n)", k=KT),
                    "down": a["w_expert_down"][0].rearrange("e (p j) n -> e p (j n)", j=JT)}
            HW_ = WE // 2

            def gate_at(n):
                return n * 3 - 1

            def up_at(n):
                return n * 3

            def down_at(n, left):
                return n * 3 + (4 if left else 2)

            def over_blocks(eng, body):
                before_last = eng.value_load(npair[0:1, 0:1], min_val=MINB // 2 - 1, max_val=MAXB // 2 - 1)
                with eng.Fori(0, before_last) as i:
                    for u in range(2):
                        body(i * 2 + u, u, 2 if u else 3)
                for u in range(2):
                    body(before_last * 2 + u, u, 1 - u)
                return before_last + 1

            def split_high(act, kind, n, s, par, halves=(0, 1)):
                act.wait_ge(ld[kind], n * 16 + 16)
                for c in halves:
                    if not isinstance(s, int) or s >= 2:
                        act.wait_ge(s_us, s * 2 + (c - 3))
                    half = slice(c * HW_, (c + 1) * HW_)
                    act.activation(wh[:, par, half], raw[kind][:, half], ACT.Copy).then_inc(s_wh, 1)

            def split_low(dve, kind, s, par, halves=(0, 1)):
                for c in halves:
                    dve.wait_ge(s_wh, s * 2 + (c + 1))
                    half = slice(c * HW_, (c + 1) * HW_)
                    dve.tensor_tensor(wl[:, par, half], raw[kind][:, half], wh[:, par, half].bitcast(F32), ALU.subtract).then_inc(s_wl, 1)

            with nc.Block() as block:
                @block.sync
                def _(sp):
                    def load(kind, e):
                        sp.dma_start(raw[kind][:], dram[kind][bass.ds(e, 1)].rearrange("o p n -> (o p) n")).then_inc(ld[kind], 16)

                    e0 = sp.value_load(bexp[0:1, 0:1], min_val=0, max_val=NE - 1)
                    for kind in ("gate", "up", "down"):
                        load(kind, e0)
                    e1 = sp.value_load(bexp[0:1, 1:2], min_val=0, max_val=NE - 1)
                    for s, kind in enumerate(("gate", "up")):
                        sp.wait_ge(s_wl, 2 * s + 2)
                        load(kind, e1)

                    def expert(m):
                        return sp.value_load(bexp[0:1, bass.ds(m, 1)], min_val=0, max_val=NE - 1)

                    def follow(kinds, at, e_before, e_now):
                        with sp.If(e_now != e_before):
                            for kind in kinds:
                                sp.wait_ge(s_wl, at[kind] * 2 + 2)
                                sp.sem_inc(s_own2, 1)
                                load(kind, e_now)
                        with sp.Else():
                            for kind in kinds:
                                sp.wait_ge(s_wl, at[kind] * 2 + 2)
                                sp.sem_inc(ld[kind], 16)

                    def loads(n, u, left):
                        if left >= 1:
                            e1 = expert(n + 1)
                            if left >= 2:
                                e2 = expert(n + 2)
                                follow(("gate", "up"), {"gate": gate_at(n + 1), "up": up_at(n + 1)}, e1, e2)
                            follow(("down",), {"down": down_at(n, left)}, expert(n), e1)

                    over_blocks(sp, loads)

                @block.gpsimd
                def _(pool):
                    for m in range(3):
                        if m == 2:
                            pool.wait_ge(s_tr, 1)
                        pool.tensor_copy(idx[:, m % 2:m % 2 + 1], slots[:, m:m + 1]).then_inc(s_ix, 1)
                        pool.wait_ge(s_ix, m + 1)
                        pool.indirect_dma_start(xg[:, m % 2, :], None, normed_dram,
                                                bass.IndirectOffsetOnAxis(ap=idx[:, m % 2:m % 2 + 1], axis=0)).then_inc(s_x[m % 2], 16)

                    def gather(n, u, left):
                        if left >= 2:
                            v = 1 - u
                            pool.wait_ge(s_tr, n + 2)
                            pool.tensor_copy(idx[:, v:v + 1], slots[:, bass.ds(n + 3, 1)]).then_inc(s_ix, 1)
                            pool.wait_ge(s_ix, n + 4)
                            pool.sem_inc(s_own, 1)
                            pool.indirect_dma_start(xg[:, v, :], None, normed_dram,
                                                    bass.IndirectOffsetOnAxis(ap=idx[:, v:v + 1], axis=0)).then_inc(s_x[v], 16)

                    n_pairs = over_blocks(pool, gather)
                    pool.wait_ge(s_x[0], n_pairs * 16 + 16)
                    pool.sem_inc(s_own, 1)

                @block.tensor
                def _(pe):
                    pe.sem_inc(s_ob, 1)

                    def turn(u):
                        for k in range(KT):
                            ins = pe.transpose(bank[k // 4][:, (k % 4) * P:(k % 4 + 1) * P], xg[:, u, k:D:KT], ident[:])
                        ins.then_inc(s_tr, 1)

                    def project(b, s, par):
                        w = (wh[:, par].rearrange("p (k n) -> p k n", k=KT), wl[:, par].rearrange("p (k n) -> p k n", k=KT))
                        for k in range(KT):
                            if k % 4 == 0:
                                pe.wait_ge(s_wl, s * 2 + (k // 4 + 1))
                            ins = split_mm(pe, b, (hTh[:, k, :], hTl[:, k, :]), (w[0][:, k, :], w[1][:, k, :]), k == 0, k == KT - 1)
                            if k % 4 == 3:
                                ins.then_inc(s_us, 1)

                    def turn_gated():
                        for j in range(JT):
                            ins = pe.transpose(bank[4][:, j * P:(j + 1) * P], gg[:, j:DE:JT], ident[:])
                        ins.then_inc(s_gt, 1)

                    pe.wait_ge(s_x[0], 16)
                    turn(0)
                    pe.wait_ge(s_hl, 1)
                    project(bank[2], 0, 0)
                    project(bank[3], 1, 1)
                    pe.wait_ge(s_x[1], 16)
                    turn(1)
                    pe.wait_ge(s_gg, 1)
                    turn_gated()

                    def products(n, u, left):
                        if left >= 1:
                            pe.wait_ge(s_hl, n + 2)
                            pe.wait_ge(s_gg, n + 1)
                            project(bank[2], gate_at(n + 1), u)
                            project(bank[3], up_at(n + 1), 1 - u)
                        if left >= 2:
                            pe.wait_ge(s_x[u], n * 8 + (32 - 8 * u))
                            turn(u)
                        pe.wait_ge(s_gl, n + 1)
                        pe.wait_ge(s_ob, n + 1)
                        w = (wh[:, u].rearrange("p (j n) -> p j n", j=JT), wl[:, u].rearrange("p (j n) -> p j n", j=JT))
                        for j in range(JT):
                            if j % 2 == 0:
                                pe.wait_ge(s_wl, down_at(n, left) * 2 + (j // 2 + 1))
                            for hf in range(2):
                                at = slice(hf * HALF, (hf + 1) * HALF)
                                ins = split_mm(pe, bank[5 + hf], (gTh[:, j, :], gTl[:, j, :]), (w[0][:, j, at], w[1][:, j, at]), j == 0, j == JT - 1)
                            if j % 2 == 1:
                                ins.then_inc(s_us, 1)
                        if left >= 1:
                            pe.wait_ge(s_gg, n + 2)
                            turn_gated()

                    over_blocks(pe, products)

                @block.scalar
                def _(act):
                    act.sem_inc(s_out[0], 16)
                    act.sem_inc(s_out[1], 16)

                    def high_h(m):
                        act.wait_ge(s_tr, m + 1)
                        if not isinstance(m, int) or m >= 1:
                            act.wait_ge(s_hl, m)
                        for k in range(KT):
                            ins = act.activation(hf32[:, k, :], bank[k // 4][:, (k % 4) * P:(k % 4 + 1) * P], ACT.Identity,
                                                 scale=colmod[:, 0, 3, k:k + 1], bias=colmod[:, 0, 2, k:k + 1])
                        ins.then_inc(s_ht, 1)
                        act.wait_ge(s_ht, m + 1)
                        act.activation(hTh[:], hf32[:], ACT.Copy).then_inc(s_hh, 1)

                    high_h(0)
                    split_high(act, "gate", 0, 0, 0)
                    split_high(act, "up", 0, 1, 1)
                    act.wait_ge(s_us, 2)
                    act.activation(sg[:], bank[2], ACT.Silu).then_inc(s_sg, 1)
                    high_h(1)
                    split_high(act, "gate", 1, 2, 0)

                    def step(n, u, left):
                        if left >= 1:
                            split_high(act, "up", n + 1, up_at(n + 1), 1 - u)
                        act.wait_ge(s_gt, n + 1)
                        act.activation(gTh[:], bank[4].rearrange("p (j t) -> p j t", t=P), ACT.Copy).then_inc(s_gh, 1)
                        split_high(act, "down", n, down_at(n, left), u)
                        if left >= 1:
                            act.wait_ge(s_us, gate_at(n + 1) * 2 + 2)
                            act.wait_ge(s_gg, n + 1)
                            act.activation(sg[:], bank[2], ACT.Silu).then_inc(s_sg, 1)
                        if left >= 2:
                            split_high(act, "gate", n + 2, gate_at(n + 2), 1 - u, (0,))
                            high_h(n + 2)
                            split_high(act, "gate", n + 2, gate_at(n + 2), 1 - u, (1,))
                        act.wait_ge(s_us, down_at(n, left) * 2 + 2)
                        act.wait_ge(s_out[u], n * 8 + (16 - 8 * u))
                        act.activation(ob[:, u, 0:HALF], bank[5], ACT.Copy)
                        act.activation(ob[:, u, HALF:D], bank[6], ACT.Copy).then_inc(s_ob, 1)
                        act.wait_ge(s_ob, n + 2)
                        act.dma_start(moe_dram[bass.ds(n * P, P), :], ob[:, u, :]).then_inc(s_out[u], 16)

                    n_pairs = over_blocks(act, step)
                    for u in range(2):
                        act.wait_ge(s_out[u], n_pairs * 16 + 16)
                        act.sem_inc(s_own2, 1)

                @block.vector
                def _(dve):
                    def low_h(m):
                        dve.wait_ge(s_hh, m + 1)
                        dve.tensor_tensor(hTl[:], hf32[:], hTh[:].bitcast(F32), ALU.subtract).then_inc(s_hl, 1)

                    def gated(m, s):
                        dve.wait_ge(s_sg, m + 1)
                        dve.wait_ge(s_us, s * 2 + 2)
                        dve.tensor_tensor(gg[:], bank[3], sg[:], ALU.mult).then_inc(s_gg, 1)

                    low_h(0)
                    split_low(dve, "gate", 0, 0)
                    split_low(dve, "up", 1, 1)
                    gated(0, 1)
                    low_h(1)
                    split_low(dve, "gate", 2, 0)

                    def step(n, u, left):
                        if left >= 1:
                            split_low(dve, "up", up_at(n + 1), 1 - u)
                        dve.wait_ge(s_gh, n + 1)
                        dve.tensor_tensor(gTl[:], bank[4].rearrange("p (j t) -> p j t", t=P), gTh[:].bitcast(F32), ALU.subtract).then_inc(s_gl, 1)
                        split_low(dve, "down", down_at(n, left), u)
                        if left >= 1:
                            gated(n + 1, up_at(n + 1))
                        if left >= 2:
                            split_low(dve, "gate", gate_at(n + 2), 1 - u, (0,))
                            low_h(n + 2)
                            split_low(dve, "gate", gate_at(n + 2), 1 - u, (1,))

                    over_blocks(dve, step)

        with ExitStack() as c2:
            r0 = sbuf(c2, "result0", [P, 2, D])
            r1 = sbuf(c2, "result1", [P, 2, D])
            yy = sbuf(c2, "combined", [P, 2, D])
            sq = sbuf(c2, "comb_sq", [P, D])
            xo = sbuf(c2, "x2_tile", [P, 2, D])
            fg = sbuf(c2, "final_gain", [P, D])
            s_fg, s_a, s_b, s_y, s_sq, s_e, s_rs, s_o, s_r = [sem("e_" + n) for n in ("gain", "first", "second", "sum", "square", "eps", "rstd", "out", "root")]
            s_g = [[sem(f"e_gather{k}{u}") for u in range(2)] for k in range(2)]
            s_st = [sem("e_store0"), sem("e_store1")]
            with nc.Block() as block:
                @block.sync
                def _(sp):
                    sp.dma_start(fg[:], a["final_g"].rearrange("(o n) -> o n", o=1).to_broadcast([P, D])).then_inc(s_fg, 16)
                    for t in range(TT):
                        sp.wait_ge(s_o, t + 1)
                        sp.dma_start(x2_out[t * P:(t + 1) * P, :], xo[:, t % 2, :]).then_inc(s_st[t % 2], 16)
                    for u in range(2):
                        sp.wait_ge(s_st[u], 16 * (TT // 2))

                @block.gpsimd
                def _(pool):
                    def root(t):
                        pool.wait_ge(s_sq, t + 1)
                        pool.tensor_scalar(stat[:, t, 0:1], stat[:, t, 0:1], D * EPS, None, ALU.add).then_inc(s_e, 1)
                        pool.wait_ge(s_e, 2 * t + 1)
                        pool.tensor_tensor(stat[:, t, 1:2], stat[:, t, 0:1], mhalf[:], ALU.pow).then_inc(s_e, 1)
                        pool.wait_ge(s_e, 2 * t + 2)
                        pool.tensor_scalar(stat[:, t, 1:2], stat[:, t, 1:2], ROOT_D, None, ALU.mult).then_inc(s_rs, 1)

                    for t in range(TT):
                        if t >= 2:
                            pool.wait_ge(s_b, t - 1)
                        for k, r in enumerate((r0, r1)):
                            pool.indirect_dma_start(r[:, t % 2, :], None, moe_dram,
                                                    bass.IndirectOffsetOnAxis(ap=rows_i[:, t, k:k + 1], axis=0)).then_inc(s_g[k][t % 2], 16)
                        if t >= 1:
                            root(t - 1)
                    root(TT - 1)

                @block.scalar
                def _(act):
                    for t in range(TT):
                        act.wait_ge(s_y, t + 1)
                        if t >= 1:
                            act.wait_ge(s_sq, t)
                        act.activation(sq[:], x1[:, t, :], ACT.Square, accum_out=stat[:, t, 0:1]).then_inc(s_sq, 1)

                @block.vector
                def _(dve):
                    def close(t):
                        dve.wait_ge(s_rs, t + 1)
                        if t == 0:
                            dve.wait_ge(s_fg, 16)
                        if t >= 2:
                            dve.wait_ge(s_st[t % 2], 16 * (t // 2))
                        dve.scalar_tensor_tensor(xo[:, t % 2, :], x1[:, t, :], stat[:, t, 1:2], fg[:], ALU.mult, ALU.mult).then_inc(s_o, 1)

                    for t in range(TT):
                        u = t % 2
                        dve.wait_ge(s_g[0][u], 16 * (t // 2 + 1))
                        dve.tensor_scalar(yy[:, u, :], r0[:, u, :], gate2[:, t, 0:1], None, ALU.mult).then_inc(s_a, 1)
                        dve.wait_ge(s_a, 2 * t + 1)
                        dve.wait_ge(s_g[1][u], 16 * (t // 2 + 1))
                        dve.scalar_tensor_tensor(yy[:, u, :], r1[:, u, :], gate2[:, t, 1:2], yy[:, u, :], ALU.mult, ALU.add).then_inc(s_b, 1)
                        dve.wait_ge(s_b, t + 1)
                        dve.tensor_tensor(yy[:, u, :], yy[:, u, :], gates[:, 1, :], ALU.mult).then_inc(s_a, 1)
                        dve.wait_ge(s_a, 2 * t + 2)
                        dve.tensor_tensor(x1[:, t, :], x1[:, t, :], yy[:, u, :], ALU.add).then_inc(s_y, 1)
                        if t >= 1:
                            close(t - 1)
                    close(TT - 1)


def split_mm(pe, out, stationary, moving, start, stop):
    (sh, sl), (mh, ml) = stationary, moving
    pe.matmul(out, sh, mh, start=start, stop=False)
    pe.matmul(out, sh, ml, start=False, stop=False)
    return pe.matmul(out, sl, mh, start=False, stop=stop)


def norm_turn(nc, ctx, tag, sbuf, sem, bank, ident, mhalf, gain, shift, hTh, hTl, src, src_dram, ahead=None):
    stat = sbuf(ctx, tag + "_stat", [P, TT, 2])
    sq = sbuf(ctx, tag + "_sq", [P, D])
    xn = sbuf(ctx, tag + "_xn", [P, 2, D])
    hf32 = sbuf(ctx, tag + "_h", [P, 2, KT, P])
    s_ld = [sem(tag + "_load0"), sem(tag + "_load1")]
    s_sq, s_e, s_rs, s_xn, s_tr, s_ht, s_hi, s_lo = [sem(tag + "_" + n) for n in ("square", "eps", "rstd", "normed", "turned", "h", "high", "low")]
    ring = src.shape[1]
    with nc.Block() as block:
        @block.sync
        def _(sp):
            if ahead:
                ahead(sp)
            if src_dram is not None:
                for t in range(TT):
                    if t >= ring:
                        sp.wait_ge(s_xn, t - ring + 1)
                        sp.wait_ge(s_sq, t - ring + 1)
                    sp.dma_start(src[:, t % ring, :], src_dram[t * P:(t + 1) * P, :]).then_inc(s_ld[t % 2], 16)

        @block.scalar
        def _(act):
            def high(t):
                act.wait_ge(s_ht, 2 * t + 2)
                act.activation(hTh[:, :, t * P:(t + 1) * P], hf32[:, t % 2], ACT.Copy).then_inc(s_hi, 1)

            for t in range(TT):
                if src_dram is not None:
                    act.wait_ge(s_ld[t % 2], 16 * (t // 2 + 1))
                if t >= 1:
                    act.wait_ge(s_sq, t)
                act.activation(sq[:], src[:, t % ring, :], ACT.Square, accum_out=stat[:, t, 0:1]).then_inc(s_sq, 1)
                if t >= 2:
                    high(t - 2)
            high(TT - 2)
            high(TT - 1)

        @block.gpsimd
        def _(pool):
            for t in range(TT):
                pool.wait_ge(s_sq, t + 1)
                pool.tensor_scalar(stat[:, t, 0:1], stat[:, t, 0:1], D * EPS, None, ALU.add).then_inc(s_e, 1)
                pool.wait_ge(s_e, t + 1)
                pool.tensor_tensor(stat[:, t, 1:2], stat[:, t, 0:1], mhalf[:], ALU.pow).then_inc(s_rs, 1)

        @block.vector
        def _(dve):
            def normed(t):
                dve.wait_ge(s_rs, t + 1)
                if t >= 2:
                    dve.wait_ge(s_tr, 2 * (t - 1))
                dve.tensor_scalar(xn[:, t % 2, :], src[:, t % ring, :], stat[:, t, 1:2], ROOT_D, ALU.mult, ALU.mult).then_inc(s_xn, 1)

            def low(t):
                dve.wait_ge(s_hi, t + 1)
                dve.tensor_tensor(hTl[:, :, t * P:(t + 1) * P], hf32[:, t % 2], hTh[:, :, t * P:(t + 1) * P].bitcast(F32), ALU.subtract).then_inc(s_lo, 1)

            normed(0)
            for t in range(TT):
                if t + 1 < TT:
                    normed(t + 1)
                if t >= 2:
                    low(t - 2)
                    dve.wait_ge(s_lo, t - 1)
                for g in range(2):
                    dve.wait_ge(s_tr, 2 * t + g + 1)
                    for k in range(4 * g, 4 * g + 4):
                        ins = dve.tensor_scalar(hf32[:, t % 2, k, :], bank[g + 2 * (t % 2)][:, (k % 4) * P:(k % 4 + 1) * P],
                                                gain[:, k:k + 1], shift[:, k:k + 1], ALU.mult, ALU.add)
                    ins.then_inc(s_ht, 1)
            low(TT - 2)
            low(TT - 1)

        @block.tensor
        def _(pe):
            for t in range(TT):
                pe.wait_ge(s_xn, t + 1)
                if t >= 2:
                    pe.wait_ge(s_ht, 2 * (t - 1))
                for g in range(2):
                    for k in range(4 * g, 4 * g + 4):
                        ins = pe.transpose(bank[g + 2 * (t % 2)][:, (k % 4) * P:(k % 4 + 1) * P], xn[:, t % 2, k:D:KT], ident[:])
                    ins.then_inc(s_tr, 1)


def attention(nc, a, sbuf, sem, bank, ident, ones, mhalf, gates, colmod, psum, x2_dram, negf_dram, o_dram):
    w_pk = a["fox_w_in_2"][0].rearrange("(p k) n -> p k n", k=KT)
    with ExitStack() as outer:
        hTh = sbuf(outer, "fox_hT_high", [P, KT, S], F32R)
        hTl = sbuf(outer, "fox_hT_low", [P, KT, S], F32R)
        with ExitStack() as c2:
            xl = sbuf(c2, "fox_x_rows", [P, 2, D])
            norm_turn(nc, c2, "f", sbuf, sem, bank, ident, mhalf, colmod[:, 1, 1, :], colmod[:, 1, 0, :], hTh, hTl, xl, x2_dram)

        with ExitStack() as c2:
            wf = sbuf(c2, "w_forget", [P, KT, P])
            wfh = sbuf(c2, "w_forget_high", [P, KT, P], F32R)
            wfl = sbuf(c2, "w_forget_low", [P, KT, P], F32R)
            fb = sbuf(c2, "forget_bias", [HF, 1])
            fr = sbuf(c2, "forget_rows", [HF, 3, S])
            s_z, s_wf, s_wh, s_wl, s_f, s_ch, s_st = [sem("v_" + n) for n in ("zeroed", "wforget", "high", "low", "frow", "chain", "stored")]
            with nc.Block() as block:
                @block.sync
                def _(sp):
                    sp.wait_ge(s_z, 1)
                    sp.dma_start(wf[:, :, 0:HF], w_pk[:, :, 3 * D:3 * D + HF]).then_inc(s_wf, 16)
                    sp.dma_start(fb[:], a["fox_b_f_2"][0].rearrange("(h o) -> h o", o=1)).then_inc(s_wf, 16)
                    sp.wait_ge(s_ch, 7)
                    sp.dma_start(negf_dram, fr[:, 1, :]).then_inc(s_st, 16)
                    sp.wait_ge(s_st, 16)

                @block.gpsimd
                def _(pool):
                    pool.memset(wf[:], 0.0).then_inc(s_z, 1)

                @block.tensor
                def _(pe):
                    pe.wait_ge(s_wl, 1)
                    for hf in range(2):
                        at = slice(hf * HALF, (hf + 1) * HALF)
                        for k in range(KT):
                            ins = split_mm(pe, bank[4 + hf], (wfh[:, k, :], wfl[:, k, :]), (hTh[:, k, at], hTl[:, k, at]), k == 0, k == KT - 1)
                        ins.then_inc(s_f, 1)

                @block.scalar
                def _(act):
                    act.wait_ge(s_wf, 32)
                    act.activation(wfh[:], wf[:], ACT.Copy).then_inc(s_wh, 1)
                    act.wait_ge(s_ch, 3)
                    act.activation(fr[:, 1, :], fr[:, 1, :], ACT.Exp, scale=-1.0).then_inc(s_ch, 1)
                    act.wait_ge(s_ch, 4)
                    act.activation(fr[:, 1, :], fr[:, 1, :], ACT.Ln, bias=1.0).then_inc(s_ch, 1)

                @block.vector
                def _(dve):
                    dve.wait_ge(s_wh, 1)
                    dve.tensor_tensor(wfl[:], wf[:], wfh[:].bitcast(F32), ALU.subtract).then_inc(s_wl, 1)
                    for hf in range(2):
                        dve.wait_ge(s_f, hf + 1)
                        dve.tensor_scalar(fr[:, 0, hf * HALF:(hf + 1) * HALF], bank[4 + hf][0:HF, :], fb[:], None, ALU.add).then_inc(s_ch, 1)
                    dve.wait_ge(s_ch, 2)
                    dve.scalar_tensor_tensor(fr[:, 1, :], fr[:, 0, :], -1.0, fr[:, 0, :], ALU.mult, ALU.max).then_inc(s_ch, 1)
                    dve.wait_ge(s_ch, 5)
                    dve.scalar_tensor_tensor(fr[:, 2, :], fr[:, 0, :], 0.0, fr[:, 1, :], ALU.min, ALU.subtract).then_inc(s_ch, 1)
                    dve.wait_ge(s_ch, 6)
                    dve.tensor_scalar(fr[:, 0, :], fr[:, 2, :], -1.0, None, ALU.mult).then_inc(s_f, 1)
                    dve.wait_ge(s_f, 3)
                    dve.tensor_tensor_scan(fr[:, 1, :], fr[:, 0, :], fr[:, 0, :], 0.0, ALU.add, ALU.bypass).then_inc(s_ch, 1)

        with ExitStack() as c2:
            w = sbuf(c2, "w_qkv", [P, 3, KT, P])
            wh = sbuf(c2, "w_qkv_high", [P, 3, KT, P], F32R)
            wl = sbuf(c2, "w_qkv_low", [P, 3, KT, P], F32R)
            qh = sbuf(c2, "q_high", [P, 2, S], F32R)
            ql = sbuf(c2, "q_low", [P, 2, S], F32R)
            kh = sbuf(c2, "k_high", [P, 2, S], F32R)
            kl = sbuf(c2, "k_low", [P, 2, S], F32R)
            va = sbuf(c2, "v_and_ones", [P, TT, 2, P])
            sq = sbuf(c2, "qk_square", [P, 4, HALF])
            xq = sbuf(c2, "qk_normed", [P, 2, HALF])
            nf = sbuf(c2, "minus_F_rows", [P, S])
            pT = sbuf(c2, "probsT", [P, 4, HALF])
            dg = sbuf(c2, "max_diagonal", [P, 2, HALF])
            o = sbuf(c2, "outT", [P, S])
            vT = sbuf(c2, "valuesT", [P, S])
            bd = sbuf(c2, "head_mean", [P, P])
            zt = sbuf(c2, "zeros", [P, P])
            idb = sbuf(c2, "ident_bf16", [P, P], BF16)
            cm = sbuf(c2, "causal_query_major", [P, P], BF16)
            cmT = sbuf(c2, "causal_key_major", [P, P], BF16)
            gq = sbuf(c2, "qk_gain", [P, 3])
            epc = sbuf(c2, "eps_col", [P, 1])
            mx = sbuf(c2, "row_max", [P, 2 * TT])
            NQ = 2 * TT
            rows = (slice(0, DH), slice(DH, P))
            f_row, m_row = (DH, 0), (96, 32)
            chunks = [(h, s, c) for h in range(2) for s in range(TT) for c in range(2) if s * P < (c + 1) * HALF]
            NCH = len(chunks)
            LAG = 2
            ready = {(h, c): max(n for n, x in enumerate(chunks) if x[0] == h and x[2] == c) for h in range(2) for c in range(2)}
            names = ("gain", "consts", "w_high", "w_low", "proj", "square", "mean", "root", "recip", "normed", "qk_high", "qk_low",
                     "F_high", "F_low", "values", "v_copied", "logits", "max", "diagonal", "max_rows", "m_high", "m_low", "m_zeroed",
                     "logitsT", "exp", "weighted", "recsum", "out", "stored", "loaded_F")
            (s_g, s_c, s_wh, s_wl, s_pj, s_sq, s_mn, s_rt, s_rc, s_x, s_h, s_l, s_fh, s_fl, s_v, s_ve, s_lg, s_mx, s_dd, s_mr,
             s_mh, s_ml, s_z, s_b, s_ex, s_o, s_rs, s_on, s_st, s_f) = [sem("a_" + n) for n in names]
            l_w = [sem("a_load_" + n) for n in ("wq", "wk", "wv")]
            s_own, s_own2 = sem("a_carrier"), sem("a_carrier2")
            s_zt, s_init, s_vc, s_vt = sem("a_zero_tile"), sem("a_rows_set"), sem("a_vT_copied"), sem("a_values_turned")

            def over_pairs(eng, body):
                with eng.Fori(0, PAIRS - 1) as i:
                    body(i, False)
                body(PAIRS - 1, True)

            def sum_bank(h, half):
                return bank[(6 if h == 0 else 4) + half]

            def columns(n):
                h, s, c = chunks[n]
                return max(s * P, c * HALF) - c * HALF

            with nc.Block() as block:
                @block.sync
                def _(sp):
                    for r in range(2):
                        for n, name in enumerate(("fox_q_norm_2", "fox_k_norm_2")):
                            sp.dma_start(gq[rows[r], n:n + 1], a[name][0].rearrange("(d o) -> d o", o=1)).then_inc(s_g, 16)
                    for g in range(3):
                        sp.dma_start(w[:, g], w_pk[:, :, g * D:g * D + P]).then_inc(l_w[g], 16)
                    for h in range(2):
                        sp.dma_start(nf[f_row[h]:f_row[h] + 1, :], negf_dram[h:h + 1, :]).then_inc(s_f, 16)

                    def pair(i, last):
                        if not last:
                            for g in range(3):
                                sp.wait_ge(s_wl, i * 3 + (g + 1))
                                sp.sem_inc(s_own, 1)
                                sp.dma_start(w[:, g], w_pk[:, :, bass.ds(i * P + (g * D + P), P)]).then_inc(l_w[g], 16)
                            sp.wait_ge(s_fl, i + 1)
                            sp.sem_inc(s_own, 1)
                            for h in range(2):
                                sp.dma_start(nf[f_row[h]:f_row[h] + 1, :], negf_dram[bass.ds(i * 2 + (h + 2), 1), :]).then_inc(s_f, 16)
                        sp.wait_ge(s_on, i * 4 + 5)
                        sp.sem_inc(s_own, 1)
                        sp.dma_start(o_dram[bass.ds(i * P, P), :], o[:]).then_inc(s_st, 16)

                    over_pairs(sp, pair)
                    sp.wait_ge(s_st, 16 * PAIRS + 16)

                @block.gpsimd
                def _(pool):
                    pool.memset(bd[:], 0.0).then_inc(s_c, 1)
                    pool.memset(dg[:, :, 0:P], 0.0).then_inc(s_c, 1)
                    pool.memset(zt[:], 0.0).then_inc(s_c, 1)
                    pool.memset(epc[:], EPS).then_inc(s_c, 1)
                    pool.memset(va[:], 1.0).then_inc(s_c, 1)
                    pool.tensor_copy(idb[:], ident[:]).then_inc(s_c, 1)
                    pool.wait_ge(s_c, 6)
                    pool.sem_inc(s_zt, 1)
                    for n, (x, sign) in enumerate(((cm, 1), (cmT, -1))):
                        mask = dg[:, n, 0:P]
                        pool.affine_select(out=mask, in_=mask, compare_op=ALU.is_ge, fill=NEG, base=0,
                                           pattern=[[-sign, P]], channel_multiplier=sign).then_inc(s_c, 1)
                        pool.wait_ge(s_c, 7 + 2 * n)
                        pool.tensor_copy(x[:], mask).then_inc(s_c, 1)
                    pool.wait_ge(s_c, 10)
                    for r in rows:
                        pool.memset(bd[r, r], 1.0 / DH).then_inc(s_c, 1)
                    pool.wait_ge(s_c, 12)
                    pool.sem_inc(s_z, 1)

                    def low_weights(n):
                        for g in range(3):
                            pool.wait_ge(s_wh, n * 3 + (g + 1))
                            pool.tensor_tensor(wl[:, g], w[:, g], wh[:, g].bitcast(F32), ALU.subtract).then_inc(s_wl, 1)

                    low_weights(0)

                    def pair(i, last):
                        pool.wait_ge(s_z, i + 1)
                        for j in range(NQ):
                            h, t = divmod(j, TT)
                            half = t // 4
                            if h == 1 and t % 4 == 0:
                                pool.wait_ge(s_mr, i * 4 + (half + 1))
                            pool.wait_ge(s_mx, i * NQ + (j + 1))
                            pool.sem_inc(s_own2, 1)
                            pool.tensor_scalar(dg[:, half, (t % 4) * P:(t % 4 + 1) * P], ident[:], mx[:, j:j + 1], -1.0, ALU.mult, ALU.mult).then_inc(s_dd, 1)
                        if not last:
                            low_weights(i + 1)
                            pool.wait_ge(s_wl, i * 3 + 6)
                            pool.wait_ge(s_b, i * NCH + NCH)
                            pool.sem_inc(s_own2, 1)
                            for x in (qh, ql):
                                for h in range(2):
                                    at = slice(m_row[h], m_row[h] + 1)
                                    ins = pool.tensor_copy(x[at, h, :].rearrange("p (a b) -> p a b", b=P), zt[at, :].unsqueeze(1).to_broadcast([1, TT, P]))
                            ins.then_inc(s_z, 1)

                    over_pairs(pool, pair)

                @block.tensor
                def _(pe):
                    pe.wait_ge(s_c, 12)

                    def pair(i, last):
                        def mean(g):
                            pe.wait_ge(s_sq, i * 4 + (g + 1))
                            if g >= 2:
                                pe.wait_ge(s_rt, i * 4 + (g - 1))
                            pe.matmul(bank[4 + g % 2], bd[:], sq[:, g, :], start=True, stop=True).then_inc(s_mn, 1)

                        pe.wait_ge(s_ex, i * NCH + 1)
                        for g in range(4):
                            pe.wait_ge(s_wl, i * 3 + (g // 2 + 1))
                            at = slice((g % 2) * HALF, (g % 2 + 1) * HALF)
                            for k in range(KT):
                                ins = split_mm(pe, bank[g], (wh[:, g // 2, k, :], wl[:, g // 2, k, :]), (hTh[:, k, at], hTl[:, k, at]), k == 0, k == KT - 1)
                            ins.then_inc(s_pj, 1)
                            if g == 1:
                                pe.wait_ge(s_on, i * 4 + 1)
                            if g >= 1:
                                mean(g - 1)
                        pe.wait_ge(s_wl, i * 3 + 3)
                        for b in range(2):
                            at = slice(b * HALF, (b + 1) * HALF)
                            for k in range(KT):
                                ins = split_mm(pe, bank[6 + b], (wh[:, 2, k, :], wl[:, 2, k, :]), (hTh[:, k, at], hTl[:, k, at]), k == 0, k == KT - 1)
                            ins.then_inc(s_v, 1)
                            if b == 0:
                                mean(3)

                        def turn_values(b):
                            pe.wait_ge(s_vc, i * 2 + (b + 1))
                            for t in range(4):
                                ins = pe.transpose(bank[6 + b][:, t * P:(t + 1) * P], vT[:, b * HALF + t * P:b * HALF + (t + 1) * P], ident[:])
                            ins.then_inc(s_vt, 1)

                        def logits(j):
                            h, t = divmod(j, TT)
                            b = 2 * (j % 3)
                            if j >= 3:
                                pe.wait_ge(s_mx, i * NQ + (j - 2))
                            width = (t + 1) * P
                            at = slice(t * P, width)
                            for c in range(0, width, HALF):
                                n = min(HALF, width - c)
                                diagonal = c + n == width
                                split_mm(pe, bank[b + c // HALF][:, 0:n], (qh[:, h, at], ql[:, h, at]), (kh[:, h, c:c + n], kl[:, h, c:c + n]), True, not diagonal)
                            pe.matmul(bank[b + c // HALF][:, n - P:n], idb[:], cm[:], start=False, stop=True).then_inc(s_lg, 1)

                        def max_rows(h):
                            for half in range(2):
                                pe.wait_ge(s_dd, i * NQ + (h * TT + 4 * half + 4))
                                if h == 0:
                                    pe.wait_ge(s_ve, i * 2 + 2)
                                pe.matmul(sum_bank(h, half), ones[:], dg[:, half, :], start=True, stop=True).then_inc(s_mr, 1)

                        turn_values(0)
                        pe.wait_ge(s_l, i * 4 + 4)
                        pe.wait_ge(s_fl, i + 1)
                        pe.wait_ge(s_z, i + 1)
                        pe.wait_ge(s_rt, i * 4 + 4)
                        for j in range(NQ):
                            logits(j)
                            if j == 2:
                                turn_values(1)
                            if j == 12:
                                max_rows(0)

                        def logitsT(n):
                            h, s, c = chunks[n]
                            if s == 0:
                                pe.wait_ge(s_ml, i * 4 + (2 * h + c + 1))
                            if n in (0, 2):
                                pe.wait_ge(s_mx, i * NQ + (NQ - 2 + n))
                            if n >= 4:
                                pe.wait_ge(s_ex, i * NCH + (n - 2))
                            at, a0 = slice(s * P, (s + 1) * P), columns(n)
                            q = slice(c * HALF + a0, (c + 1) * HALF)
                            diagonal = s // 4 == c
                            ins = split_mm(pe, bank[(n + 2) % 4][:, a0:HALF], (kh[:, h, at], kl[:, h, at]), (qh[:, h, q], ql[:, h, q]), True, not diagonal)
                            if diagonal:
                                ins = pe.matmul(bank[(n + 2) % 4][:, a0:a0 + P], idb[:], cmT[:], start=False, stop=True)
                            ins.then_inc(s_b, 1)

                        def weigh(n):
                            h, s, c = chunks[n]
                            if n == 0:
                                pe.wait_ge(s_ve, i * 2 + 2)
                            pe.wait_ge(s_ex, i * NCH + (n + 2))
                            a0 = columns(n)
                            pe.matmul(sum_bank(h, c)[:, a0:HALF], va[:, s, h, :], pT[:, n % 4, 0:HALF - a0],
                                      start=(s == 0), stop=(n == ready[h, c])).then_inc(s_o, 1)

                        for n in range(NCH + LAG):
                            if n < NCH:
                                logitsT(n)
                            if n >= LAG:
                                weigh(n - LAG)
                            if n == 4:
                                max_rows(1)

                    over_pairs(pe, pair)

                @block.scalar
                def _(act):
                    act.sem_inc(s_ex, 1)
                    act.wait_ge(s_zt, 1)
                    for x in (qh, ql, kh, kl):
                        act.activation(x[:].rearrange("p h (a b) -> p (h a) b", b=P), zt[:].unsqueeze(1).to_broadcast([P, NQ, P]), ACT.Copy).then_inc(s_init, 1)

                    def high_weights(n):
                        for g in range(3):
                            act.wait_ge(l_w[g], n * 16 + 16)
                            act.activation(wh[:, g], w[:, g], ACT.Copy).then_inc(s_wh, 1)

                    high_weights(0)
                    act.wait_ge(s_init, 4)
                    for x, row in ((qh, f_row), (kh, m_row)):
                        for h in range(2):
                            at = slice(row[h], row[h] + 1)
                            act.activation(x[at, h, :].rearrange("p (a b) -> p a b", b=P), ones[at, :].unsqueeze(1).to_broadcast([1, TT, P]),
                                           ACT.Copy).then_inc(s_init, 1)
                    act.wait_ge(s_init, 8)

                    def pair(i, last):
                        def square(g):
                            act.wait_ge(s_pj, i * 4 + (g + 1))
                            act.activation(sq[:, g, :], bank[g], ACT.Square).then_inc(s_sq, 1)

                        def root(g):
                            act.wait_ge(s_mn, i * 4 + (g + 1))
                            act.activation(sq[:, g, :], bank[4 + g % 2], ACT.Sqrt, bias=epc[:]).then_inc(s_rt, 1)

                        def high(g):
                            act.wait_ge(s_x, i * 4 + (g + 1))
                            at = slice((g % 2) * HALF, (g % 2 + 1) * HALF)
                            for h, r in enumerate(rows):
                                ins = act.activation((qh if g < 2 else kh)[r, h, at], xq[r, g % 2, :], ACT.Copy)
                            ins.then_inc(s_h, 1)

                        def copy_valuesT(b):
                            act.wait_ge(s_v, i * 2 + (b + 1))
                            act.activation(vT[:, b * HALF:(b + 1) * HALF], bank[6 + b], ACT.Copy).then_inc(s_vc, 1)

                        def copy_values(b):
                            act.wait_ge(s_vt, i * 2 + (b + 1))
                            src = bank[6 + b].rearrange("p (t n) -> p t n", n=P)
                            for h, r in enumerate(rows):
                                ins = act.activation(va[:, 4 * b:4 * b + 4, h, r], src[:, :, r], ACT.Copy)
                            ins.then_inc(s_ve, 1)

                        def max_high(h):
                            for half in range(2):
                                act.wait_ge(s_mr, i * 4 + (2 * h + half + 1))
                                at = slice(m_row[h], m_row[h] + 1)
                                act.activation(qh[at, h, half * HALF:(half + 1) * HALF], sum_bank(h, half)[at, :], ACT.Copy).then_inc(s_mh, 1)

                        square(0)
                        act.wait_ge(s_f, i * 32 + 32)
                        for h in range(2):
                            at = slice(f_row[h], f_row[h] + 1)
                            ins = act.activation(kh[at, h, :], nf[at, :], ACT.Copy)
                        ins.then_inc(s_fh, 1)
                        square(1)
                        root(0)
                        square(2)
                        root(1)
                        high(0)
                        square(3)
                        root(2)
                        high(1)
                        copy_valuesT(0)
                        root(3)
                        high(2)
                        copy_valuesT(1)
                        high(3)
                        copy_values(0)
                        copy_values(1)
                        max_high(0)
                        for n in range(NCH):
                            act.wait_ge(s_b, i * NCH + (n + 1))
                            a0 = columns(n)
                            act.activation(pT[:, n % 4, 0:HALF - a0], bank[(n + 2) % 4][:, a0:HALF], ACT.Exp).then_inc(s_ex, 1)
                            if n == 4:
                                max_high(1)
                            if n == 16 and not last:
                                high_weights(i + 1)

                    over_pairs(act, pair)

                @block.vector
                def _(dve):
                    dve.wait_ge(s_g, 64)
                    dve.tensor_scalar(gq[:, 2:3], gq[:, 0:1], DH ** -0.5, None, ALU.mult).then_inc(s_rs, 1)
                    dve.wait_ge(s_rs, 1)
                    dve.sem_inc(s_on, 1)
                    dve.sem_inc(s_st, 16)

                    def pair(i, last):
                        def normed(g):
                            dve.wait_ge(s_rt, i * 4 + (g + 1))
                            dve.reciprocal(sq[:, g, :], sq[:, g, :]).then_inc(s_rc, 1)
                            dve.wait_ge(s_rc, i * 4 + (g + 1))
                            if g < 2:
                                dve.wait_ge(s_on, i * 4 + 1)
                            else:
                                dve.wait_ge(s_l, i * 4 + (g - 1))
                            dve.scalar_tensor_tensor(xq[:, g % 2, :], bank[g], gq[:, 2:3] if g < 2 else gq[:, 1:2], sq[:, g, :],
                                                     ALU.mult, ALU.mult).then_inc(s_x, 1)

                        def low(g):
                            dve.wait_ge(s_h, i * 4 + (g + 1))
                            at = slice((g % 2) * HALF, (g % 2 + 1) * HALF)
                            hi, lo = (qh, ql) if g < 2 else (kh, kl)
                            for h, r in enumerate(rows):
                                ins = dve.tensor_tensor(lo[r, h, at], xq[r, g % 2, :], hi[r, h, at].bitcast(F32), ALU.subtract)
                            ins.then_inc(s_l, 1)

                        def forget_low():
                            dve.wait_ge(s_fh, i + 1)
                            for h in range(2):
                                at = slice(f_row[h], f_row[h] + 1)
                                ins = dve.tensor_tensor(kl[at, h, :], nf[at, :], kh[at, h, :].bitcast(F32), ALU.subtract)
                            ins.then_inc(s_fl, 1)

                        def max_low(h):
                            for half in range(2):
                                dve.wait_ge(s_mh, i * 4 + (2 * h + half + 1))
                                at, q = slice(m_row[h], m_row[h] + 1), slice(half * HALF, (half + 1) * HALF)
                                dve.tensor_tensor(ql[at, h, q], sum_bank(h, half)[at, :], qh[at, h, q].bitcast(F32), ALU.subtract).then_inc(s_ml, 1)

                        def leave(h, c):
                            dve.wait_ge(s_o, i * NCH + (ready[h, c] + 1))
                            src = sum_bank(h, c)
                            dve.reciprocal(xq[rows[h], c, :], src[rows[1 - h], :]).then_inc(s_rs, 1)
                            dve.wait_ge(s_rs, i * 4 + (2 * h + c + 2))
                            dve.tensor_tensor(o[rows[h], c * HALF:(c + 1) * HALF], src[rows[h], :], xq[rows[h], c, :], ALU.mult).then_inc(s_on, 1)

                        forget_low()
                        normed(0)
                        normed(1)
                        low(0)
                        normed(2)
                        low(1)
                        normed(3)
                        low(2)
                        low(3)
                        for j in range(NQ):
                            t = j % TT
                            b = 2 * (j % 3)
                            dve.wait_ge(s_lg, i * NQ + (j + 1))
                            dve.tensor_reduce(mx[:, j:j + 1], psum[:, b:b + 2, :].rearrange("p b n -> p (b n)")[:, 0:(t + 1) * P], X, ALU.max).then_inc(s_mx, 1)
                            if j == 13:
                                max_low(0)
                        max_low(1)
                        dve.wait_ge(s_st, i * 16 + 16)
                        for h in range(2):
                            for c in range(2):
                                leave(h, c)

                    over_pairs(dve, pair)


def fox_out(nc, a, sbuf, sem, bank, ident, ones, mhalf, gates, colmod, x2_dram, o_dram, x3):
    with ExitStack() as c2:
        ld = {m: sbuf(c2, "fox_out_" + m, [P, 2, S]) for m in ("o", "w")}
        hi = {m: sbuf(c2, "fox_out_" + m + "_high", [P, KT, S], F32R) for m in ("o", "w")}
        lo = {m: sbuf(c2, "fox_out_" + m + "_low", [P, KT, S], F32R) for m in ("o", "w")}
        mix = sbuf(c2, "fox_mix", [P, 2, HALF])
        src = {"o": o_dram.rearrange("(k p) n -> p k n", p=P), "w": a["fox_w_out_2"][0].rearrange("(k p) n -> p k n", p=P)}
        s_ld = {m: [sem("p_load_" + m + "0"), sem("p_load_" + m + "1")] for m in ld}
        s_x, s_hi, s_lo, s_m, s_g, s_r = [sem("p_" + n) for n in ("x2", "high", "low", "mm", "gated", "residual")]
        with nc.Block() as block:
            @block.sync
            def _(sp):
                for k in range(KT):
                    if k >= 2:
                        sp.wait_ge(s_lo, 2 * (k - 1))
                    for m in ("o", "w"):
                        sp.dma_start(ld[m][:, k % 2, :], src[m][:, k, :]).then_inc(s_ld[m][k % 2], 16)
                sp.dma_start(x3[:], x2_dram.rearrange("(t p) n -> p t n", p=P)).then_inc(s_x, 16)

            @block.scalar
            def _(act):
                for k in range(KT):
                    for m in ("o", "w"):
                        act.wait_ge(s_ld[m][k % 2], 16 * (k // 2 + 1))
                        act.activation(hi[m][:, k, :], ld[m][:, k % 2, :], ACT.Copy).then_inc(s_hi, 1)

            @block.tensor
            def _(pe):
                def product(j, b, k):
                    t, hf = divmod(j, 2)
                    rows, at = slice(t * P, (t + 1) * P), slice(hf * HALF, (hf + 1) * HALF)
                    return split_mm(pe, bank[b], (hi["o"][:, k, rows], lo["o"][:, k, rows]), (hi["w"][:, k, at], lo["w"][:, k, at]), k == 0, k == KT - 1)

                for k in range(KT):
                    pe.wait_ge(s_lo, 2 * k + 2)
                    for j in range(TT):
                        ins = product(j, j, k)
                        if k == KT - 1:
                            ins.then_inc(s_m, 1)
                for j in range(TT, 2 * TT):
                    pe.wait_ge(s_g, j - TT + 1)
                    for k in range(KT):
                        ins = product(j, j - TT, k)
                    ins.then_inc(s_m, 1)

            @block.vector
            def _(dve):
                for k in range(KT):
                    for n, m in enumerate(("o", "w")):
                        dve.wait_ge(s_hi, 2 * k + n + 1)
                        dve.tensor_tensor(lo[m][:, k, :], ld[m][:, k % 2, :], hi[m][:, k, :].bitcast(F32), ALU.subtract).then_inc(s_lo, 1)
                dve.wait_ge(s_x, 16)
                for j in range(2 * TT):
                    t, hf = divmod(j, 2)
                    at = slice(hf * HALF, (hf + 1) * HALF)
                    dve.wait_ge(s_m, j + 1)
                    if j >= 2:
                        dve.wait_ge(s_r, j - 1)
                    dve.tensor_tensor(mix[:, j % 2, :], bank[j % TT], gates[:, 2, at], ALU.mult).then_inc(s_g, 1)
                    dve.wait_ge(s_g, j + 1)
                    dve.tensor_tensor(x3[:, t, at], x3[:, t, at], mix[:, j % 2, :], ALU.add).then_inc(s_r, 1)


def mlp(nc, a, sbuf, sem, bank, ident, ones, mhalf, gates, colmod, x3, hTh, hTl, out):
    W = 2 * P
    NB = FF // W
    NO = 2 * TT
    with ExitStack() as c2:
        w1 = sbuf(c2, "w_mlp_in", [P, KT, W])
        w2 = sbuf(c2, "w_mlp_out", [P, 2, D])
        l1, l2 = sem("h_w1"), sem("h_w2")
        w1_d = a["w_mlp_in_2"][0].rearrange("(p k) n -> p k n", k=KT)
        w2_d = a["w_mlp_out_2"][0].rearrange("(f p) n -> p f n", p=P)

        def first_weights(sp):
            sp.dma_start(w1[:], w1_d[:, :, 0:W]).then_inc(l1, 16)
            sp.dma_start(w2[:], w2_d[:, 0:2, :]).then_inc(l2, 16)

        with ExitStack() as c3:
            norm_turn(nc, c3, "n", sbuf, sem, bank, ident, mhalf, colmod[:, 1, 3, :], colmod[:, 1, 2, :], hTh, hTl, x3, None, first_weights)
        w1h = sbuf(c2, "w_mlp_in_high", [P, 2, KT, W], F32R)
        w1l = sbuf(c2, "w_mlp_in_low", [P, 2, KT, W], F32R)
        w2h = sbuf(c2, "w_mlp_out_high", [P, 2, D], F32R)
        w2l = sbuf(c2, "w_mlp_out_low", [P, 2, D], F32R)
        gTh = sbuf(c2, "hiddenT_high", [P, 2, S], F32R)
        gTl = sbuf(c2, "hiddenT_low", [P, 2, S], F32R)
        rl = sbuf(c2, "relu", [P, 2, HALF])
        gf = sbuf(c2, "relu_squared", [P, 2, HALF])
        s_own, s_out = sem("h_carrier"), sem("h_stored")
        s_w1h, s_w1l, s_w2s, s_w2h, s_w2l = [sem("h_" + n) for n in ("w1_high", "w1_low", "w2_scaled", "w2_high", "w2_low")]
        s_h, s_rl, s_sq, s_gh, s_gl, s_o, s_r = [sem("h_" + n) for n in ("hidden", "relu", "squared", "g_high", "g_low", "out", "residual")]
        groups = [(0, 0), (1, 0), (0, 1), (1, 1)]

        def over_blocks(eng, body):
            with eng.Fori(0, NB // 2 - 1) as i:
                for u in range(2):
                    body(i * 2 + u, u, False)
            for u in range(2):
                body(NB - 2 + u, u, u == 1)

        with nc.Block() as block:
            @block.sync
            def _(sp):
                def load(n, u, last):
                    if last:
                        return
                    sp.wait_ge(s_w1l, n + 2)
                    sp.sem_inc(s_own, 1)
                    sp.dma_start(w1[:], w1_d[:, :, bass.ds(n * W + W, W)]).then_inc(l1, 16)
                    sp.wait_ge(s_w2l, n + 2)
                    sp.sem_inc(s_own, 1)
                    sp.dma_start(w2[:], w2_d[:, bass.ds(n * 2 + 2, 2), :]).then_inc(l2, 16)

                over_blocks(sp, load)
                for t in range(TT):
                    sp.wait_ge(s_r, (NB - 1) * NO + 2 * t + 2 + 4)
                    sp.dma_start(out[0, t * P:(t + 1) * P, :], x3[:, t, :]).then_inc(s_out, 16)
                sp.wait_ge(s_out, 16 * TT)

            @block.tensor
            def _(pe):
                pe.sem_inc(s_h, 1)
                pe.sem_inc(s_o, 1)

                def products(n, u, last):
                    pe.wait_ge(s_w1l, n + 2)
                    for g, (m, hf) in enumerate(groups):
                        pe.wait_ge(s_rl, n * 4 + g + 1)
                        at = slice(hf * HALF, (hf + 1) * HALF)
                        for k in range(KT):
                            ins = split_mm(pe, bank[g], (w1h[:, u, k, m * P:(m + 1) * P], w1l[:, u, k, m * P:(m + 1) * P]),
                                           (hTh[:, k, at], hTl[:, k, at]), k == 0, k == KT - 1)
                        ins.then_inc(s_h, 1)
                    pe.wait_ge(s_w2l, n + 2)
                    for j in range(NO):
                        t, hf = divmod(j, 2)
                        if j == 0:
                            pe.wait_ge(s_gl, n * 4 + 2 + 4)
                        if t == 4 and hf == 0:
                            pe.wait_ge(s_gl, n * 4 + 4 + 4)
                        pe.wait_ge(s_r, n * NO + j + 1)
                        for m in range(2):
                            ins = split_mm(pe, bank[4 + j % 4], (gTh[:, m, t * P:(t + 1) * P], gTl[:, m, t * P:(t + 1) * P]),
                                           (w2h[:, m, hf * HALF:(hf + 1) * HALF], w2l[:, m, hf * HALF:(hf + 1) * HALF]), m == 0, m == 1)
                        ins.then_inc(s_o, 1)

                over_blocks(pe, products)

            @block.scalar
            def _(act):
                act.sem_inc(s_rl, 4)

                def high1(n, u):
                    act.wait_ge(l1, n * 16 + 16)
                    act.activation(w1h[:, u], w1[:], ACT.Copy).then_inc(s_w1h, 1)

                def step(n, u, last):
                    act.wait_ge(s_w2s, n + 1)
                    act.wait_ge(s_o, n * NO + 1)
                    act.activation(w2h[:], w2[:], ACT.Copy).then_inc(s_w2h, 1)
                    for g in range(5):
                        if g < 4:
                            act.wait_ge(s_h, n * 4 + g + 2)
                            act.wait_ge(s_sq, n * 4 + g + 1)
                            act.activation(rl[:, g % 2, :], bank[g], ACT.Relu).then_inc(s_rl, 1)
                        if g >= 1:
                            m, hf = groups[g - 1]
                            act.wait_ge(s_sq, n * 4 + g + 2)
                            act.activation(gTh[:, m, hf * HALF:(hf + 1) * HALF], gf[:, (g - 1) % 2, :], ACT.Copy).then_inc(s_gh, 1)
                    if not last:
                        high1(n + 1, 1 - u)

                high1(0, 0)
                over_blocks(act, step)

            @block.vector
            def _(dve):
                dve.sem_inc(s_w1l, 1)
                dve.sem_inc(s_w2l, 1)
                dve.sem_inc(s_sq, 2)
                dve.sem_inc(s_gl, 4)
                dve.sem_inc(s_r, 4)

                def low1(n, u):
                    dve.wait_ge(s_w1h, n + 1)
                    dve.tensor_tensor(w1l[:, u], w1[:], w1h[:, u].bitcast(F32), ALU.subtract).then_inc(s_w1l, 1)

                def step(n, u, last):
                    dve.wait_ge(l2, n * 16 + 16)
                    dve.tensor_tensor(w2[:], w2[:], gates[:, 3, :].unsqueeze(1).to_broadcast([P, 2, D]), ALU.mult).then_inc(s_w2s, 1)
                    dve.wait_ge(s_w2h, n + 1)
                    dve.tensor_tensor(w2l[:], w2[:], w2h[:].bitcast(F32), ALU.subtract).then_inc(s_w2l, 1)
                    for g in range(5):
                        if g < 4:
                            dve.wait_ge(s_rl, n * 4 + g + 5)
                            dve.wait_ge(s_gl, n * 4 + g + 3)
                            dve.tensor_tensor(gf[:, g % 2, :], rl[:, g % 2, :], rl[:, g % 2, :], ALU.mult).then_inc(s_sq, 1)
                        if g >= 1:
                            m, hf = groups[g - 1]
                            dve.wait_ge(s_gh, n * 4 + g)
                            dve.tensor_tensor(gTl[:, m, hf * HALF:(hf + 1) * HALF], gf[:, (g - 1) % 2, :],
                                              gTh[:, m, hf * HALF:(hf + 1) * HALF].bitcast(F32), ALU.subtract).then_inc(s_gl, 1)
                    for j in range(NO):
                        t, hf = divmod(j, 2)
                        at = slice(hf * HALF, (hf + 1) * HALF)
                        if j == NO // 2 and not last:
                            low1(n + 1, 1 - u)
                        dve.wait_ge(s_o, n * NO + j + 2)
                        dve.tensor_tensor(x3[:, t, at], x3[:, t, at], bank[4 + j % 4], ALU.add).then_inc(s_r, 1)

                low1(0, 0)
                over_blocks(dve, step)


def kernel(**inputs):
    import concourse.bacc as bacc
    import numpy as np
    from concourse.bass_utils import run_bass_kernel_spmd

    nc = bacc.Bacc("TRN2", target_bir_lowering=False, num_devices=1)
    arrays, aps = {}, {}
    for name, value in inputs.items():
        value = np.ascontiguousarray(value)
        if not value.size:
            continue
        arrays["in_" + name] = value
        aps[name] = nc.dram_tensor("in_" + name, value.shape, mybir.dt.from_np(value.dtype), kind="ExternalInput").ap()
    out = nc.dram_tensor("out", [1, S, D], F32, kind="ExternalOutput").ap()
    build(nc, aps, out)
    return run_bass_kernel_spmd(nc, [arrays], core_ids=[0]).results[0]["out"]
```
